# Optimizing a Trainium2 kernel written in Bass

```python
import math
import jax, jax.numpy as jnp
from jax import lax
import numpy as np

D_MODEL = 1024
BATCH = 1
SEQ = 1024
DEPTH = 1
DEC_BATCH = 8
DEC_SEQ = 8
PAST_LEN = 8192
PAGE_SIZE = 128

HEAD_DIM = 64
N_RET_HEADS = 8
N_ATT_HEADS = 8
RET_WIDTH = N_RET_HEADS * HEAD_DIM
ATT_WIDTH = N_ATT_HEADS * HEAD_DIM
MIX_WIDTH = RET_WIDTH + ATT_WIDTH
W_IN_COLS = 4 * RET_WIDTH + 3 * ATT_WIDTH
RET_CHUNK = 128
DIL_PATTERNS = ((128, 1), (512, 4), (2048, 16))
MAX_WINDOW = 2048
ATT_BLOCK = 128
N_BUCKETS = 32
MAX_DISTANCE = 2048
ROPE_BASE = 10000.0
D_FF = -(-8 * D_MODEL // (3 * 256)) * 256
NORM_EPS = 1e-6
GN_EPS = 1e-5

kernel_name = 'hymba_retention_dilated_swa_decoder_step'

def rmsnorm(x, g):
    xf = x.astype(jnp.float32)
    y = xf * lax.rsqrt(jnp.mean(xf * xf, axis=-1, keepdims=True) + NORM_EPS) * g.astype(jnp.float32)
    return y.astype(x.dtype)

def rope(x, pos):
    half = HEAD_DIM // 2
    inv = ROPE_BASE ** (-jnp.arange(0, HEAD_DIM, 2, dtype=jnp.float32) / HEAD_DIM)
    ang = pos.astype(jnp.float32)[:, None] * inv[None, :]
    cos = jnp.cos(ang)[None, :, None, :]
    sin = jnp.sin(ang)[None, :, None, :]
    xf = x.astype(jnp.float32)
    x1, x2 = xf[..., :half], xf[..., half:]
    return jnp.concatenate([x1 * cos - x2 * sin, x2 * cos + x1 * sin], axis=-1).astype(x.dtype)

def t5_bucket(dist):
    max_exact = N_BUCKETS // 2
    d_f = jnp.maximum(dist, 1).astype(jnp.float32)
    large = max_exact + (jnp.log(d_f / max_exact) / math.log(MAX_DISTANCE / max_exact)
                         * (N_BUCKETS - max_exact)).astype(jnp.int32)
    large = jnp.minimum(large, N_BUCKETS - 1)
    return jnp.where(dist < max_exact, dist, large)

def pattern_bias(rel_bias, dil, nk):
    dist = jnp.arange(nk + 1, dtype=jnp.int32) * dil
    return rel_bias[t5_bucket(dist)].astype(jnp.float32)

def retention_log_decay():
    return jnp.log1p(-jnp.exp2(-5.0 - jnp.arange(N_RET_HEADS, dtype=jnp.float32)))

def retention_chunk(S, q, k, v, log_g):
    C = q.shape[1]
    q, k, v = q.astype(jnp.float32), k.astype(jnp.float32), v.astype(jnp.float32)
    i = jnp.arange(C, dtype=jnp.float32)
    rel = i[:, None] - i[None, :]
    decay = jnp.where(rel[None] >= 0, jnp.exp(jnp.maximum(rel, 0.0)[None] * log_g[:, None, None]), 0.0)
    inner = jnp.einsum('bihd,bjhd->bhij', q, k) * decay[None]
    cross_decay = jnp.exp((i + 1.0)[:, None] * log_g[None, :])
    o = (jnp.einsum('bhij,bjhe->bihe', inner, v)
         + jnp.einsum('bihd,bhde->bihe', q, S) * cross_decay[None, :, :, None])
    k_decay = jnp.exp((C - 1.0 - i)[:, None] * log_g[None, :])
    S_new = (S * jnp.exp(C * log_g)[None, :, None, None]
             + jnp.einsum('bjhd,bjhe,jh->bhde', k, v, k_decay))
    return S_new, o

def retention_prompt(q, k, v, log_g):
    B, T, H, D = q.shape
    C = min(RET_CHUNK, T)
    nc = T // C
    to_chunks = lambda t: jnp.moveaxis(t.reshape(B, nc, C, H, D), 1, 0)
    S0 = jnp.zeros((B, H, D, D), jnp.float32)

    def step(S, inp):
        qc, kc, vc = inp
        return retention_chunk(S, qc, kc, vc, log_g)

    S_fin, outs = lax.scan(step, S0, (to_chunks(q), to_chunks(k), to_chunks(v)))
    return S_fin, jnp.moveaxis(outs, 0, 1).reshape(B, T, H, D)

def dilated_prompt_stats(q, k, v, bias_k, dil, nk):
    B, S, H, D = q.shape
    Ls = S // dil
    nb = -(-Ls // ATT_BLOCK)
    Lp = nb * ATT_BLOCK

    def sub(t):
        t = t.reshape(B, Ls, dil, H, D).transpose(0, 2, 1, 3, 4).reshape(B * dil, Ls, H, D)
        t = jnp.pad(t, ((0, 0), (0, Lp - Ls), (0, 0), (0, 0)))
        return t.reshape(B * dil, nb, ATT_BLOCK, H, D)

    def band(t):
        prev = jnp.pad(t, ((0, 0), (1, 0), (0, 0), (0, 0), (0, 0)))[:, :-1]
        return jnp.concatenate([prev, t], axis=2)

    qs = sub(q).astype(jnp.float32)
    kb = band(sub(k)).astype(jnp.float32)
    vb = band(sub(v)).astype(jnp.float32)
    qi = jnp.arange(ATT_BLOCK)[:, None]
    kj = jnp.arange(2 * ATT_BLOCK)[None, :]
    dist = ATT_BLOCK + qi - kj
    valid = (dist >= 0) & (dist <= nk)
    valid = valid[None] & ((jnp.arange(nb)[:, None, None] > 0) | (kj[None] >= ATT_BLOCK))
    bias = bias_k[jnp.minimum(jnp.maximum(dist, 0), nk)].transpose(2, 0, 1)
    s = jnp.einsum('bnqhd,bnkhd->bnhqk', qs, kb) + bias
    s = jnp.where(valid[None, :, None], s, -jnp.inf)
    m = jnp.max(s, axis=-1)
    p = jnp.exp(s - m[..., None])
    l = jnp.sum(p, axis=-1)
    acc = jnp.einsum('bnhqk,bnkhd->bnqhd', p, vb)

    def unsub(t):
        rest = t.shape[3:]
        t = t.reshape((B, dil, Lp) + rest)[:, :, :Ls]
        return jnp.swapaxes(t, 1, 2).reshape((B, S) + rest)

    return unsub(jnp.swapaxes(m, 2, 3)), unsub(jnp.swapaxes(l, 2, 3)), unsub(acc)

def dilated_sample_stats(q, k_all, v_all, bias_k, dil, nk, L):
    T = q.shape[1]
    idx = L + jnp.arange(T)[:, None] - jnp.arange(nk + 1)[None, :] * dil
    valid = idx >= 0
    idx_c = jnp.maximum(idx, 0)
    kg = jnp.take(k_all, idx_c, axis=1).astype(jnp.float32)
    vg = jnp.take(v_all, idx_c, axis=1).astype(jnp.float32)
    s = jnp.einsum('bthd,btkhd->bthk', q.astype(jnp.float32), kg) + bias_k.T[None, None]
    s = jnp.where(valid[None, :, None, :], s, -jnp.inf)
    m = jnp.max(s, axis=-1)
    p = jnp.exp(s - m[..., None])
    l = jnp.sum(p, axis=-1)
    acc = jnp.einsum('bthk,btkhd->bthd', p, vg)
    return m, l, acc

def combine_by_denominator(stats):
    m_all = jnp.max(jnp.stack([st[0] for st in stats]), axis=0)
    num = 0.0
    den = 0.0
    for m, l, acc in stats:
        w = jnp.exp(m - m_all)
        num = num + w[..., None] * acc
        den = den + w * l
    return num / den[..., None]

def decoder_layer(x, pos, ret_state, k_buf, v_buf, rel_bias, w_in, g_ret, w_out,
                  g_pre_mix, g_post_mix, g_pre_ffn, g_post_ffn, w_gu, w_down):
    B, T, _ = x.shape
    h = rmsnorm(x, g_pre_mix)
    z = h @ w_in
    R, A = RET_WIDTH, ATT_WIDTH
    rq = z[..., 0:R]
    rk = z[..., R:2 * R]
    rv = z[..., 2 * R:3 * R]
    rg = z[..., 3 * R:4 * R]
    aq = z[..., 4 * R:4 * R + A]
    ak = z[..., 4 * R + A:4 * R + 2 * A]
    av = z[..., 4 * R + 2 * A:4 * R + 3 * A]
    heads = lambda t, n: t.reshape(B, T, n, HEAD_DIM)

    log_g = retention_log_decay()
    rq = rope(heads(rq, N_RET_HEADS), pos)
    rk = rope(heads(rk, N_RET_HEADS), pos) * (HEAD_DIM ** -0.5)
    rv = heads(rv, N_RET_HEADS)
    if ret_state is None:
        S_new, ro = retention_prompt(rq, rk, rv, log_g)
    else:
        S_new, ro = retention_chunk(ret_state.astype(jnp.float32), rq, rk, rv, log_g)
    mu = jnp.mean(ro, axis=-1, keepdims=True)
    var = jnp.mean(jnp.square(ro - mu), axis=-1, keepdims=True)
    ro = (ro - mu) * lax.rsqrt(var + GN_EPS) * g_ret.astype(jnp.float32)[None, None]
    ro = ro.reshape(B, T, RET_WIDTH) * jax.nn.silu(rg.astype(jnp.float32))

    aq = heads(aq, N_ATT_HEADS) * (HEAD_DIM ** -0.5)
    ak = heads(ak, N_ATT_HEADS)
    av = heads(av, N_ATT_HEADS)
    stats = []
    if k_buf is None:
        for win, dil in DIL_PATTERNS:
            nk = win // dil
            stats.append(dilated_prompt_stats(aq, ak, av, pattern_bias(rel_bias, dil, nk), dil, nk))
        L = min(MAX_WINDOW, T)
        k_new, v_new = ak[:, T - L:], av[:, T - L:]
    else:
        L = k_buf.shape[1]
        k_all = jnp.concatenate([k_buf.astype(ak.dtype), ak], axis=1)
        v_all = jnp.concatenate([v_buf.astype(av.dtype), av], axis=1)
        for win, dil in DIL_PATTERNS:
            nk = win // dil
            stats.append(dilated_sample_stats(aq, k_all, v_all, pattern_bias(rel_bias, dil, nk), dil, nk, L))
        k_new, v_new = k_all[:, T:], v_all[:, T:]
    ao = combine_by_denominator(stats).reshape(B, T, ATT_WIDTH)

    mix = jnp.concatenate([ro.astype(x.dtype), ao.astype(x.dtype)], axis=-1) @ w_out
    x = x + rmsnorm(mix, g_post_mix)

    h = rmsnorm(x, g_pre_ffn)
    gu = h @ w_gu
    gate, up = gu[..., :D_FF], gu[..., D_FF:]
    f = (jax.nn.silu(gate) * up) @ w_down
    x = x + rmsnorm(f, g_post_ffn)
    return x, S_new.astype(x.dtype), k_new, v_new

def setup_inputs(seed: int = 0) -> dict:
    key = jax.random.key(seed)
    ks = jax.random.split(key, 20)
    f32 = jnp.float32
    L = min(MAX_WINDOW, PAST_LEN)
    nrm = lambda k, shape, s: jax.random.normal(k, shape, f32) * s
    gain = lambda k, shape: 1.0 + 0.05 * jax.random.normal(k, shape, f32)
    return {
        'x_prompt': nrm(ks[0], (BATCH, SEQ, D_MODEL), 1.0),
        'x_sample': nrm(ks[1], (DEC_BATCH, DEC_SEQ, D_MODEL), 1.0),
        'state_ret': nrm(ks[2], (DEPTH, DEC_BATCH, N_RET_HEADS, HEAD_DIM, HEAD_DIM), 1.0),
        'cache_k_win': nrm(ks[3], (DEPTH, DEC_BATCH, L, N_ATT_HEADS, HEAD_DIM), 1.0),
        'cache_v_win': nrm(ks[4], (DEPTH, DEC_BATCH, L, N_ATT_HEADS, HEAD_DIM), 1.0),
        'rel_bias': nrm(ks[5], (N_BUCKETS, N_ATT_HEADS), 0.5),
        'w_in': nrm(ks[6], (DEPTH, D_MODEL, W_IN_COLS), D_MODEL ** -0.5),
        'g_ret': gain(ks[7], (DEPTH, N_RET_HEADS, HEAD_DIM)),
        'w_out': nrm(ks[8], (DEPTH, MIX_WIDTH, D_MODEL), MIX_WIDTH ** -0.5),
        'g_pre_mix': gain(ks[9], (DEPTH, D_MODEL)),
        'g_post_mix': gain(ks[10], (DEPTH, D_MODEL)),
        'g_pre_ffn': gain(ks[11], (DEPTH, D_MODEL)),
        'g_post_ffn': gain(ks[12], (DEPTH, D_MODEL)),
        'w_gu': nrm(ks[13], (DEPTH, D_MODEL, 2 * D_FF), D_MODEL ** -0.5),
        'w_down': nrm(ks[14], (DEPTH, D_FF, D_MODEL), D_FF ** -0.5),
    }

def reference(x_prompt, x_sample, state_ret, cache_k_win, cache_v_win, rel_bias, w_in, g_ret,
              w_out, g_pre_mix, g_post_mix, g_pre_ffn, g_post_ffn, w_gu, w_down):
    pos_p = jnp.arange(x_prompt.shape[1], dtype=jnp.int32)
    pos_s = PAST_LEN + jnp.arange(x_sample.shape[1], dtype=jnp.int32)
    yp, ys = x_prompt, x_sample
    sp_l, kp_l, vp_l, ss_l, ks_l, vs_l = [], [], [], [], [], []
    for l in range(DEPTH):
        yp, sp, kp, vp = decoder_layer(yp, pos_p, None, None, None, rel_bias, w_in[l], g_ret[l],
                                       w_out[l], g_pre_mix[l], g_post_mix[l], g_pre_ffn[l],
                                       g_post_ffn[l], w_gu[l], w_down[l])
        ys, ss, ksn, vsn = decoder_layer(ys, pos_s, state_ret[l], cache_k_win[l], cache_v_win[l],
                                         rel_bias, w_in[l], g_ret[l], w_out[l], g_pre_mix[l],
                                         g_post_mix[l], g_pre_ffn[l], g_post_ffn[l], w_gu[l], w_down[l])
        sp_l.append(sp); kp_l.append(kp); vp_l.append(vp)
        ss_l.append(ss); ks_l.append(ksn); vs_l.append(vsn)
    return (yp, ys, jnp.stack(sp_l), jnp.stack(kp_l), jnp.stack(vp_l),
            jnp.stack(ss_l), jnp.stack(ks_l), jnp.stack(vs_l))


_drawn_inputs = setup_inputs


def setup_inputs(seed=0):
    import zlib

    import numpy as np

    out = dict(_drawn_inputs(seed))
    spreads = {}
    factors = {}
    for name, (base, spread) in spreads.items():
        noise = np.random.default_rng([zlib.crc32(name.encode()), seed]).standard_normal(out[name].shape)
        drawn = base * np.exp(spread * noise) if base else spread * noise
        out[name] = __import__('jax').numpy.asarray(drawn.astype(out[name].dtype))
    for name, factor in factors.items():
        out[name] = (out[name] * factor).astype(out[name].dtype)
    return out
```

```python
import numpy as np
from contextlib import ExitStack

import concourse.bass as bass
from concourse import mybir

F32 = mybir.dt.float32
F32R = mybir.dt.float32r
ALU = mybir.AluOpType
ACT = mybir.ActivationFunctionType
AXX = mybir.AxisListType.X

D_MODEL, SEQ, DEC_B, DEC_T, PAST = 1024, 1024, 8, 8, 8192
HD, NH, NPAIR = 64, 8, 4
WID = NH * HD
ZC = 7 * WID
L = 2048
D_FF = 2816
NS = DEC_B * DEC_T
NTOK = SEQ + NS
KT = D_MODEL // 128
PT = SEQ // 128
TT = PT + 1
EPS, GN_EPS = 1e-6, 1e-5
NEG = -1e30
N_BUCKETS, MAX_DISTANCE = 32, 2048
WIDE, REST, STILES = 8, 1536, 11
TABW = 1152
TABC = 896 + 127


def t5_bucket(dist):
    me = N_BUCKETS // 2
    d = np.maximum(dist, 1).astype(np.float32)
    big = me + (np.log(d / np.float32(me)) / np.float32(np.log(MAX_DISTANCE / me))
                * np.float32(N_BUCKETS - me)).astype(np.int32)
    return np.where(dist < me, dist, np.minimum(big, N_BUCKETS - 1))


def pattern_rows(dist):
    d = np.asarray(dist)
    ok = d >= 0
    c = ((d <= 128).astype(int) + ((d <= 512) & (d % 4 == 0)) + ((d <= 2048) & (d % 16 == 0))) * ok
    rows = np.zeros((N_BUCKETS + 1,) + d.shape, np.float32)
    b = t5_bucket(np.maximum(d, 0))
    for n in range(N_BUCKETS):
        rows[n] = (b == n) & (c > 0)
    rows[N_BUCKETS] = np.where(c > 0, np.log(np.maximum(c, 1)), NEG)
    return rows


def shape_constants():
    c = {}
    f64 = np.float64
    inv = (10000.0 ** (-np.arange(0, HD, 2) / HD)).astype(np.float32)
    pos = np.zeros((TT, 128), np.float32)
    pos[:PT] = np.arange(SEQ).reshape(PT, 128)
    pos[PT, :NS] = PAST + np.arange(NS) % DEC_T
    ang = (pos[:, :, None] * inv[None, None, :]).astype(np.float32).astype(f64)
    rope = np.zeros((128, TT, 2, HD), np.float32)
    rope[:, :, 0] = np.concatenate([np.cos(ang), np.cos(ang)], -1).transpose(1, 0, 2)
    rope[:, :, 1] = np.concatenate([-np.sin(ang), np.sin(ang)], -1).transpose(1, 0, 2)
    c["c_rope"] = rope
    lg = np.log1p(-np.exp2(-5.0 - np.arange(NH))).astype(f64)
    i = np.arange(128)
    rel = i[None, :] - i[:, None]
    dec = np.where(rel[None] >= 0, np.exp(np.maximum(rel, 0)[None] * lg[:, None, None]), 0) / 8
    c["c_decay"] = dec.transpose(1, 0, 2).astype(np.float32)
    cross = np.exp((i + 1)[None, :] * lg[:, None])
    pairs = np.repeat(lg.reshape(NPAIR, 2).T, HD, 0)
    c["c_cross"] = np.exp(pairs[:, :, None] * (i + 1)).astype(np.float32)
    c["c_kdec"] = (np.exp((127 - i)[:, None] * lg[None]) / 8).astype(np.float32)
    c["c_chunk"] = np.exp(128 * pairs).astype(np.float32)
    n = np.arange(NS)
    same = (n[:, None] // DEC_T == n[None, :] // DEC_T)
    rs = n[None, :] - n[:, None]
    c["c_decay_s"] = (np.where(same & (rs >= 0), np.exp(np.maximum(rs, 0)[None] * lg[:, None, None]), 0)
                      / 8).transpose(1, 0, 2).astype(np.float32)
    c["c_cross_s"] = np.exp(pairs[:, :, None] * (n % DEC_T + 1)).astype(np.float32)
    c["c_kdec_s"] = (np.exp((DEC_T - 1 - n % DEC_T)[:, None] * lg[None]) / 8).astype(np.float32)
    c["c_chunk_s"] = np.exp(DEC_T * pairs).astype(np.float32)
    c["c_bmask"] = (n[:, None] // DEC_T == np.arange(DEC_B)[None]).astype(np.float32)
    c["c_ident"] = np.eye(128, dtype=np.float32)
    c["c_dist_p"] = pattern_rows(TABC - np.arange(TABW))
    p = np.arange(128)
    rows = [16 * p + j for j in range(WIDE)]
    rows += [REST + 16 * (p // 4) + 8 + 2 * (p % 4) + j for j in range(2)]
    rows += [np.where(p < DEC_T, L + p, 10 * L)]
    rows = np.stack(rows)
    dist = L + np.arange(DEC_T)[None, :, None] - rows[:, None, :]
    c["c_dist_s"] = pattern_rows(dist).reshape(N_BUCKETS + 1, -1)
    return {k: np.ascontiguousarray(v) for k, v in c.items()}


def tile_rows(t):
    return 128 if t < PT else NS


def spread(ap, shape):
    return ap.unsqueeze(2).broadcast_to(shape)


def known(t, value):
    return isinstance(t, int) and t == value


def in_projection(nc, A, z, h_hi, h_lo, ident):
    GROUPS = ZC // WID
    HK = KT // 2
    w_v = A["w_in"][0].rearrange("(q k p) n -> q p k n", q=2, p=128)
    x_v = [A["x_prompt"][0, t * 128:(t + 1) * 128, :] for t in range(PT)]
    x_v.append(A["x_sample"].rearrange("b t d -> (b t) d"))
    with ExitStack() as ctx:
        sb = lambda n, s, d=F32: ctx.enter_context(nc.sbuf_tensor(n, s, d))
        ps = lambda n, s: ctx.enter_context(nc.psum_tensor(n, s, F32))
        sem = lambda n: nc.alloc_semaphore("p1_" + n)
        w_raw = sb("w_raw", [128, 2, HK, WID])
        w_hi, w_lo = sb("w_hi", [128, 2, KT, WID], F32R), sb("w_lo", [128, 2, KT, WID], F32R)
        xt = sb("xt", [128, 2, D_MODEL])
        xn = sb("xn", [128, 2, D_MODEL])
        hg = sb("hg", [128, 2, HK, 128])
        g_rows, gT = sb("g_rows", [KT, 128]), sb("gT", [128, KT])
        stat, mhalf = sb("stat", [128, 3, TT]), sb("mhalf", [128, 1])
        z_out = sb("z_out", [128, 3, WID])
        t_ps = [ps(f"t_ps{i}", [128, HK, 128]) for i in range(2)]
        z_ps = [ps(f"z_ps{i}", [128, WID]) for i in range(3)]
        x_landed = [sem(f"x_landed{i}") for i in range(2)]
        w_landed = [sem(f"w_landed{i}") for i in range(2)]
        g_landed, i_landed, g_turned, g_ready = map(sem, ("g_landed", "i_landed", "g_turned", "g_ready"))
        half_set, squared, mean_ready, rstd_ready, xn_ready = map(
            sem, ("half_set", "squared", "mean_ready", "rstd_ready", "xn_ready"))
        turned, hg_ready, hi_ready, lo_ready = map(sem, ("turned", "hg_ready", "hi_ready", "lo_ready"))
        w_hi_ready, w_lo_ready = sem("w_hi_ready"), sem("w_lo_ready")
        z_done, z_evac = sem("z_done"), sem("z_evac")
        z_stored = [sem(f"z_stored{i}") for i in range(3)]

        with nc.Block() as block:

            @block.sync
            def _(sp):
                def load_weights(c):
                    for q in range(2):
                        if not isinstance(c, int) or c > 0:
                            sp.wait_ge(w_lo_ready, 2 * c + q - 1)
                        sp.dma_start(w_raw[:, q], w_v[q][:, :, bass.ds(c * WID, WID)]).then_inc(w_landed[q], 16)

                def store_z(c, t):
                    n = tile_rows(t)
                    sp.wait_ge(z_evac, TT * c + t + 1)
                    sp.dma_start(z[t * 128:t * 128 + n, bass.ds(c * WID, WID)],
                                 z_out[128 - n:128, t % 3, :]).then_inc(z_stored[t % 3], 16)

                sp.dma_start(xt[:, 0, :], x_v[0]).then_inc(x_landed[0], 16)
                sp.dma_start(ident[:, :], A["c_ident"]).then_inc(i_landed, 16)
                sp.dma_start(g_rows[:, :], A["g_pre_mix"][0].rearrange("(k p) -> k p", p=128)).then_inc(g_landed, 16)
                sp.dma_start(xt[:, 1, :], x_v[1]).then_inc(x_landed[1], 16)
                load_weights(0)
                for t in range(2, TT):
                    sp.wait_ge(xn_ready, t - 1)
                    sp.dma_start(xt[0:tile_rows(t), t % 2, :], x_v[t]).then_inc(x_landed[t % 2], 16)
                load_weights(1)
                for t in range(TT):
                    store_z(0, t)
                with sp.Fori(1, GROUPS - 1) as c:
                    load_weights(c + 1)
                    for t in range(TT):
                        store_z(c, t)
                for t in range(TT):
                    store_z(GROUPS - 1, t)
                for m in range(3):
                    sp.wait_ge(z_stored[m], 16 * 3 * GROUPS)

            @block.gpsimd
            def _(pool):
                pool.memset(mhalf[:, :], -0.5).then_inc(half_set, 1)
                pool.wait_ge(half_set, 1)

                def rstd(t):
                    n = tile_rows(t)
                    pool.wait_ge(mean_ready, t + 1)
                    pool.tensor_tensor(stat[0:n, 2, t:t + 1], stat[0:n, 1, t:t + 1], mhalf[0:n, :],
                                       ALU.pow).then_inc(rstd_ready, 1)

                rstd(0)
                for t in range(TT):
                    if t + 1 < TT:
                        rstd(t + 1)
                    n = tile_rows(t)
                    for q in range(2):
                        pool.wait_ge(hi_ready, 2 * t + q + 1)
                        cut = (slice(None), slice(HK * q, HK * q + HK), slice(t * 128, t * 128 + n))
                        pool.tensor_tensor(h_lo[cut], hg[:, q, :, 0:n], h_hi[cut].bitcast(F32),
                                           ALU.subtract).then_inc(lo_ready, 1)

            @block.scalar
            def _(act):
                def square(t):
                    n = tile_rows(t)
                    act.wait_ge(x_landed[t % 2], 16 * (t // 2 + 1))
                    if t >= 2:
                        act.wait_ge(turned, 2 * (t - 1))
                    act.activation(xn[0:n, t % 2, :], xt[0:n, t % 2, :], ACT.Square,
                                   accum_out=stat[0:n, 0, t:t + 1]).then_inc(squared, 1)

                def split_weights(c, par, q):
                    act.wait_ge(w_landed[q], 16 * c + 16)
                    if not isinstance(c, int) or c >= 2:
                        act.wait_ge(z_done, TT * c - TT)
                    act.copy(w_hi[:, par, HK * q:HK * q + HK, :], w_raw[:, q]).then_inc(w_hi_ready, 1)

                def evacuate(c, t):
                    n = tile_rows(t)
                    act.wait_ge(z_done, TT * c + t + 1)
                    if not isinstance(c, int) or c > 0 or t >= 3:
                        act.wait_ge(z_stored[t % 3], 48 * c + 16 * (t // 3))
                    act.copy(z_out[128 - n:128, t % 3, :], z_ps[t % 3][128 - n:128, :]).then_inc(z_evac, 1)

                def group(c, par, last=False):
                    for t in range(TT):
                        evacuate(c, t)
                        if not last and t in (1, 4):
                            split_weights(c + 1, 1 - par, t // 4)

                square(0)
                square(1)
                split_weights(0, 0, 0)
                split_weights(0, 0, 1)
                for t in range(TT):
                    n = tile_rows(t)
                    for q in range(2):
                        act.wait_ge(hg_ready, 2 * t + q + 1)
                        act.copy(h_hi[:, HK * q:HK * q + HK, t * 128:t * 128 + n],
                                 hg[:, q, :, 0:n]).then_inc(hi_ready, 1)
                    if t + 2 < TT:
                        square(t + 2)
                    if t >= 1:
                        evacuate(0, t - 1)
                    if t in (4, 6):
                        split_weights(1, 1, t // 5)
                evacuate(0, TT - 1)
                with act.Fori(0, (GROUPS - 3) // 2) as i:
                    group(2 * i + 1, 1)
                    group(2 * i + 2, 0)
                group(GROUPS - 2, 1)
                group(GROUPS - 1, 0, last=True)

            @block.vector
            def _(dve):
                def normalise(t):
                    n = tile_rows(t)
                    dve.wait_ge(squared, t + 1)
                    dve.tensor_scalar(stat[0:n, 1, t:t + 1], stat[0:n, 0, t:t + 1], 1.0 / D_MODEL, EPS,
                                      ALU.mult, ALU.add).then_inc(mean_ready, 1)
                    dve.wait_ge(rstd_ready, t + 1)
                    dve.tensor_scalar(xn[0:n, t % 2, :], xt[0:n, t % 2, :], stat[0:n, 2, t:t + 1], None,
                                      ALU.mult).then_inc(xn_ready, 1)

                def split_weights(c, par, q):
                    dve.wait_ge(w_hi_ready, 2 * c + q + 1)
                    cut = (slice(None), par, slice(HK * q, HK * q + HK))
                    dve.tensor_tensor(w_lo[cut], w_raw[:, q], w_hi[cut].bitcast(F32),
                                      ALU.subtract).then_inc(w_lo_ready, 1)

                normalise(0)
                dve.wait_ge(g_turned, 1)
                dve.tensor_copy(gT[:, :], t_ps[1][:, 0, 0:KT]).then_inc(g_ready, 1)
                dve.wait_ge(g_ready, 1)
                for t in range(TT):
                    n = tile_rows(t)
                    if t + 1 < TT:
                        normalise(t + 1)
                    for q in range(2):
                        dve.wait_ge(turned, 2 * t + q + 1)
                        if t >= 1:
                            dve.wait_ge(lo_ready, 2 * t + q - 1)
                        dve.tensor_tensor(hg[:, q, :, 0:n], t_ps[q][:, :, 0:n],
                                          spread(gT[:, HK * q:HK * q + HK], [128, HK, n]),
                                          ALU.mult).then_inc(hg_ready, 1)
                    if t == 0:
                        split_weights(0, 0, 0)
                        split_weights(0, 0, 1)
                split_weights(1, 1, 0)
                split_weights(1, 1, 1)
                with dve.Fori(0, (GROUPS - 3) // 2) as i:
                    for par in (0, 1):
                        for q in range(2):
                            split_weights(2 * i + 2 + par, par, q)
                for q in range(2):
                    split_weights(GROUPS - 1, 0, q)

            @block.tensor
            def _(pe):
                def turn(t):
                    n = tile_rows(t)
                    pe.wait_ge(xn_ready, t + 1)
                    for q in range(2):
                        if t >= 1:
                            pe.wait_ge(hg_ready, 2 * t + q - 1)
                        for k in range(HK):
                            col = (HK * q + k) * 128
                            mm = pe.transpose(t_ps[q][:, k, 0:n], xn[0:n, t % 2, col:col + 128], ident[0:n, 0:n])
                        mm.then_inc(turned, 1)

                def project(c, par, t):
                    if not isinstance(c, int) or c > 0 or t >= 3:
                        pe.wait_ge(z_evac, TT * c + t - 2)
                    end = t * 128 + tile_rows(t)
                    first, last = (0, 0), (KT - 1, 2)
                    for k in range(KT):
                        for n, (x, w) in enumerate(((h_hi, w_hi), (h_hi, w_lo), (h_lo, w_hi))):
                            mm = pe.matmul(z_ps[t % 3][:, :], x[:, k, end - 128:end], w[:, par, k, :],
                                           start=(k, n) == first, stop=(k, n) == last)
                    mm.then_inc(z_done, 1)

                pe.wait_ge(i_landed, 16)
                pe.wait_ge(g_landed, 16)
                pe.transpose(t_ps[1][:, 0, 0:KT], g_rows[:, :], ident[0:KT, 0:KT]).then_inc(g_turned, 1)
                pe.wait_ge(g_ready, 1)
                turn(0)
                for t in range(TT):
                    if t + 1 < TT:
                        turn(t + 1)
                    pe.wait_ge(lo_ready, 2 * t + 2)
                    if t == 0:
                        pe.wait_ge(w_lo_ready, 2)
                    project(0, 0, t)
                with pe.Fori(0, (GROUPS - 1) // 2) as i:
                    for par in (1, 0):
                        c = 2 * i + 2 - par
                        pe.wait_ge(w_lo_ready, 2 * c + 2)
                        for t in range(TT):
                            project(c, par, t)


def by(t):
    return t + 2


def diagonal(t4, par):
    return t4[HD * par:HD * par + HD, :, HD * par:HD * par + HD]


def retention(nc, A, z, mix, ident, state_p, state_s):
    with ExitStack() as ctx:
        sb = lambda n, s, d=F32: ctx.enter_context(nc.sbuf_tensor(n, s, d))
        ps = lambda n, s: ctx.enter_context(nc.psum_tensor(n, s, F32))
        sem = lambda n: nc.alloc_semaphore("p2_" + n)
        zr = sb("zr", [128, 2, 4, NH, HD])
        rope = sb("rope", [128, TT, 2, HD])
        decay, cross = sb("decay", [128, NH, 128]), sb("cross", [128, NPAIR, 128])
        kdec, chunk = sb("kdec", [128, NH]), sb("chunk", [128, NPAIR])
        decay_s, cross_s = sb("decay_s", [NS, NH, NS]), sb("cross_s", [128, NPAIR, NS])
        kdec_s, chunk_s = sb("kdec_s", [NS, NH]), sb("chunk_s", [128, NPAIR])
        bmask = sb("bmask", [NS, DEC_B])
        g_row = sb("g_row", [128, WID])
        t1, t2 = sb("t1", [128, 2 * NH, HD]), sb("t2", [128, 2 * NH, HD])
        qk = sb("qk", [128, 2 * NH, HD])
        qT = sb("qT2", [128, NPAIR, 128])
        kT = sb("kT2", [128, 2, NPAIR, 128])
        qd = sb("qd", [128, NPAIR, 128])
        kd = sb("kd", [128, NH, HD])
        inT = sb("inT", [128, 2, NPAIR, 128])
        S = sb("S", [128, 2, NPAIR, 128])
        Sg = sb("Sg", [128, NPAIR, 128])
        swish, gate = sb("swish", [128, WID]), sb("gate", [128, WID])
        oc, sq, on = (sb(n, [128, NH, HD]) for n in ("oc", "sq", "on"))
        stat, mhalf = sb("stat2", [128, 5, NH]), sb("mhalf2", [128, NH])
        mixr = sb("mixr", [128, 2, WID])
        S_in = sb("S_in", [128, DEC_B, NPAIR, 128])
        S_out = sb("S_out", [128, DEC_B, NPAIR, HD])
        qdm = sb("qdm", [128, NPAIR, DEC_B * NS])
        vm = sb("vm", [NS, DEC_B, WID])
        qk_ps = [ps(f"qk_ps{i}", [128, NPAIR, 128]) for i in range(2)]
        in_ps = [ps(f"in_ps{i}", [128, NPAIR, 128]) for i in range(2)]
        o_ps, su_ps = ps("o_ps", [128, NH, HD]), ps("su_ps", [128, NPAIR, 128])

        z_landed = [sem(f"z_landed{i}") for i in range(2)]
        rope_landed, tab_landed, state_landed = map(sem, ("rope_landed", "tab_landed", "state_landed"))
        names = ("t1_ready", "qk_ready", "qk_turned", "qkT_ready", "qd_ready", "kd_ready", "inner_done",
                 "inT_ready", "update_done", "S_ready", "Sg_ready", "o_done", "swish_ready", "gate_ready",
                 "oc_ready", "sq_ready", "var_ready", "rstd_ready", "on_ready", "mix_ready")
        (t1_ready, qk_ready, qk_turned, qkT_ready, qd_ready, kd_ready, inner_done, inT_ready, update_done,
         S_ready, Sg_ready, o_done, swish_ready, gate_ready, oc_ready, sq_ready, var_ready, rstd_ready,
         on_ready, mix_ready) = map(sem, names)
        cleared, dve_step, vm_ready, sout_ready = map(sem, ("cleared", "dve_step", "vm_ready", "sout_ready"))
        mix_stored = [sem(f"mix_stored{i}") for i in range(2)]
        state_stored = sem("state_stored")
        TABS, SAMPLE = 10, PT

        with nc.Block() as block:

            @block.sync
            def _(sp):
                def load(t, par, rows=128):
                    sp.dma_start(zr[0:rows, par].rearrange("p a h d -> p (a h d)"),
                                 z[bass.ds(t * 128, rows), 0:4 * WID]).then_inc(z_landed[par], 16)

                def store(t, par, rows=128):
                    sp.wait_ge(mix_ready, by(t))
                    sp.dma_start(mix[bass.ds(t * 128, rows), 0:WID], mixr[0:rows, par, :]).then_inc(mix_stored[par], 16)

                load(0, 0)
                sp.dma_start(rope[:, :, :, :], A["c_rope"]).then_inc(rope_landed, 16)
                for dst, name in ((kdec, "c_kdec"), (cross, "c_cross"), (decay, "c_decay"), (chunk, "c_chunk"),
                                  (decay_s, "c_decay_s"), (cross_s, "c_cross_s"), (kdec_s, "c_kdec_s"),
                                  (chunk_s, "c_chunk_s"), (bmask, "c_bmask")):
                    sp.dma_start(dst[:], A[name]).then_inc(tab_landed, 16)
                sp.dma_start(g_row[:, :], A["g_ret"][0].rearrange("h d -> (h d)").partition_broadcast(128)).then_inc(tab_landed, 16)
                load(1, 1)
                sp.wait_ge(cleared, 5)
                for par in range(2):
                    sp.dma_start(S_in[HD * par:HD * par + HD, :, :, HD * par:HD * par + HD],
                                 A["state_ret"][0].rearrange("b (p r) d e -> r d b p e", r=2)[par]).then_inc(state_landed, 16)
                with sp.Fori(0, PT // 2 - 1) as i:
                    for par in range(2):
                        store(2 * i + par, par)
                        load(2 * i + par + 2, par)
                store(PT - 2, 0)
                load(SAMPLE, 0, NS)
                store(PT - 1, 1)
                for par in range(2):
                    sp.dma_start(state_p.rearrange("(p r) d e -> r d p e", r=2)[par],
                                 diagonal(S[:, PT % 2], par)).then_inc(state_stored, 16)
                store(SAMPLE, 0, NS)
                sp.wait_ge(sout_ready, 8)
                for par in range(2):
                    sp.dma_start(state_s.rearrange("b (p r) d e -> r d b p e", r=2)[par],
                                 S_out[HD * par:HD * par + HD]).then_inc(state_stored, 16)
                sp.wait_ge(state_stored, 64)
                sp.wait_ge(mix_stored[0], 80)
                sp.wait_ge(mix_stored[1], 64)

            @block.gpsimd
            def _(pool):
                for s in (t1_ready, kd_ready, gate_ready, Sg_ready, rstd_ready, on_ready):
                    pool.sem_inc(s, 1)
                pool.memset(mhalf[:, :], -0.5).then_inc(cleared, 1)
                pool.memset(S[:, :, :, :], 0.0).then_inc(cleared, 1)
                pool.memset(kT[:, :, :, :], 0.0).then_inc(cleared, 1)
                pool.memset(qdm[:, :, :], 0.0).then_inc(cleared, 1)
                pool.memset(S_in[:, :, :, :], 0.0).then_inc(cleared, 1)
                pool.wait_ge(rope_landed, 16)

                def cosine(t, par, lap):
                    pool.wait_ge(z_landed[par], lap)
                    pool.wait_ge(qk_ready, by(t - 1))
                    pool.tensor_tensor(t1[:, :, :], zr[:, par, 0:2].rearrange("p a h d -> p (a h) d"),
                                       rope[:, t, 0, :].unsqueeze(1).broadcast_to([128, 2 * NH, HD]),
                                       ALU.mult).then_inc(t1_ready, 1)

                def early(t, par, rows, kdec, S_now):
                    pool.wait_ge(qk_ready, by(t))
                    pool.wait_ge(update_done, by(t - 1))
                    pool.tensor_tensor(kd[0:rows], qk[0:rows, NH:2 * NH, :], spread(kdec[:, :], [rows, NH, HD]),
                                       ALU.mult).then_inc(kd_ready, 1)
                    if S_now is not None:
                        pool.wait_ge(S_ready, by(t - 1))
                        pool.tensor_tensor(Sg[:, :, :], S_now, spread(chunk[:, :], [128, NPAIR, 128]),
                                           ALU.mult).then_inc(Sg_ready, 1)
                    pool.wait_ge(swish_ready, by(t))
                    pool.wait_ge(mix_ready, by(t - 1))
                    pool.tensor_tensor(gate[:, :], swish[:, :], g_row[:, :], ALU.mult).then_inc(gate_ready, 1)

                def late(t):
                    pool.wait_ge(var_ready, by(t))
                    pool.tensor_tensor(stat[:, 4, :], stat[:, 3, :], mhalf[:, :], ALU.pow).then_inc(rstd_ready, 1)
                    pool.wait_ge(rstd_ready, by(t))
                    pool.tensor_tensor(on[:, :, :], oc[:, :, :], spread(stat[:, 4, :], [128, NH, HD]),
                                       ALU.mult).then_inc(on_ready, 1)

                cosine(0, 0, 16)
                pool.wait_ge(tab_landed, 16 * TABS)
                with pool.Fori(0, PT // 2) as i:
                    for par in range(2):
                        t = 2 * i + par
                        early(t, par, 128, kdec, S[:, par])
                        cosine(t + 1, 1 - par, 16 * i + 16 + 16 * par)
                        late(t)
                early(SAMPLE, 0, NS, kdec_s, None)
                pool.tensor_tensor(vm[:, :, :], zr[0:NS, 0, 2].rearrange("p h d -> p (h d)").unsqueeze(1)
                                   .broadcast_to([NS, DEC_B, WID]), spread(bmask[:, :], [NS, DEC_B, WID]),
                                   ALU.mult).then_inc(vm_ready, 1)
                late(SAMPLE)

            @block.scalar
            def _(act):
                for s in (swish_ready, qkT_ready, sq_ready):
                    act.sem_inc(s, 1)
                act.wait_ge(cleared, 3)

                def swish_gate(t, par, lap):
                    act.wait_ge(z_landed[par], lap)
                    act.wait_ge(gate_ready, by(t - 1))
                    act.activation(swish[:, :], zr[:, par, 3].rearrange("p h d -> p (h d)"), ACT.Silu).then_inc(swish_ready, 1)

                def step(t, par, rows):
                    act.wait_ge(qk_turned, by(t))
                    act.wait_ge(inner_done, by(t - 1))
                    act.wait_ge(qd_ready, by(t - 1))
                    act.copy(qT[:, :, 0:rows], qk_ps[0][:, :, 0:rows])
                    for r in range(2):
                        d = slice(HD * r, HD * r + HD)
                        x = act.copy(kT[d, r, :, 0:rows], qk_ps[1][d, :, 0:rows])
                    x.then_inc(qkT_ready, 1)

                def square(t):
                    act.wait_ge(oc_ready, by(t))
                    act.activation(sq[:, :, :], oc[:, :, :], ACT.Square).then_inc(sq_ready, 1)

                with act.Fori(0, PT // 2) as i:
                    for par in range(2):
                        swish_gate(2 * i + par, par, 16 * i + 16)
                        step(2 * i + par, par, 128)
                        square(2 * i + par)
                swish_gate(SAMPLE, 0, 16 * PT // 2 + 16)
                step(SAMPLE, 0, NS)
                square(SAMPLE)

            @block.vector
            def _(dve):
                for s in (qk_ready, qd_ready, inT_ready, S_ready, oc_ready, var_ready, mix_ready):
                    dve.sem_inc(s, 1)
                dve.sem_inc(dve_step, 1)
                dve.wait_ge(rope_landed, 16)

                def rotate(t, par, lap):
                    dve.wait_ge(z_landed[par], lap)
                    x = zr[:, par, 0:2].rearrange("p a h d -> p (a h) d")
                    for a, b in ((0, 32), (32, 0)):
                        dve.tensor_tensor(t2[:, :, a:a + 32], x[:, :, b:b + 32],
                                          rope[:, t, 1, a:a + 32].unsqueeze(1).broadcast_to([128, 2 * NH, 32]),
                                          ALU.mult).then_inc(dve_step, 1)
                    dve.wait_ge(dve_step, 5 * t + 3)
                    dve.wait_ge(t1_ready, by(t))
                    dve.wait_ge(qk_turned, by(t - 1))
                    dve.wait_ge(kd_ready, by(t - 1))
                    dve.tensor_tensor(qk[:, :, :], t1[:, :, :], t2[:, :, :], ALU.add).then_inc(qk_ready, 1)

                def scores(t, rows, cross, decay):
                    dve.wait_ge(qkT_ready, by(t))
                    dve.wait_ge(o_done, by(t - 1))
                    q = qT[:, :, 0:rows]
                    if rows == 128:
                        dve.tensor_tensor(qd[:, :, :], q, cross[:, :, :], ALU.mult).then_inc(qd_ready, 1)
                    else:
                        dve.wait_ge(cleared, 4)
                        own = bass.AP(tensor=qdm[:].tensor, offset=qdm[:].offset,
                                      ap=[list(qdm[:].ap[0]), [DEC_B * NS, NPAIR], [NS + DEC_T, DEC_B], [1, DEC_T]])
                        split = lambda x: x.rearrange("p a (b t) -> p a b t", b=DEC_B)
                        dve.tensor_tensor(own, split(q), split(cross[:, :, :]), ALU.mult).then_inc(qd_ready, 1)
                    dve.wait_ge(inner_done, by(t))
                    for r in range(2):
                        x = dve.tensor_tensor(inT[0:rows, r, :, 0:rows], in_ps[r][0:rows, :, 0:rows],
                                              decay[:, r:NH:2, :], ALU.mult)
                    x.then_inc(inT_ready, 1)

                def new_state(t, S_next):
                    dve.wait_ge(update_done, by(t))
                    dve.wait_ge(Sg_ready, by(t))
                    for r in range(2):
                        x = dve.tensor_tensor(diagonal(S_next, r), diagonal(Sg, r), diagonal(su_ps, r), ALU.add)
                    x.then_inc(S_ready, 1)

                def centre(t, rows):
                    dve.wait_ge(o_done, by(t))
                    dve.tensor_reduce(stat[0:rows, 0, :], o_ps[0:rows], AXX, ALU.add).then_inc(dve_step, 1)
                    dve.wait_ge(dve_step, 5 * t + 4)
                    dve.tensor_scalar(stat[0:rows, 1, :], stat[0:rows, 0, :], -1.0 / HD, None, ALU.mult).then_inc(dve_step, 1)
                    dve.wait_ge(dve_step, 5 * t + 5)
                    dve.wait_ge(on_ready, by(t - 1))
                    dve.tensor_tensor(oc[0:rows], o_ps[0:rows], spread(stat[0:rows, 1, :], [rows, NH, HD]),
                                      ALU.add).then_inc(oc_ready, 1)

                def variance(t):
                    dve.wait_ge(sq_ready, by(t))
                    dve.tensor_reduce(stat[:, 2, :], sq[:, :, :], AXX, ALU.add).then_inc(dve_step, 1)
                    dve.wait_ge(dve_step, 5 * t + 6)
                    dve.tensor_scalar(stat[:, 3, :], stat[:, 2, :], 1.0 / HD, GN_EPS, ALU.mult, ALU.add).then_inc(var_ready, 1)

                def finish(t, par, stored):
                    dve.wait_ge(on_ready, by(t))
                    dve.wait_ge(gate_ready, by(t))
                    if stored is not None:
                        dve.wait_ge(mix_stored[par], stored)
                    dve.tensor_tensor(mixr[:, par, :], on[:, :, :].rearrange("p h d -> p (h d)"), gate[:, :],
                                      ALU.mult).then_inc(mix_ready, 1)

                rotate(0, 0, 16)
                dve.wait_ge(tab_landed, 16 * TABS)

                def tile(t, par, i, first=False):
                    scores(t, 128, cross, decay)
                    new_state(t, S[:, 1 - par])
                    centre(t, 128)
                    variance(t)
                    rotate(t + 1, 1 - par, 16 * i + 16 + 16 * par)
                    finish(t, par, None if first else 16 * i)

                dve.wait_ge(cleared, 2)
                tile(0, 0, 0, True)
                tile(1, 1, 0, True)
                with dve.Fori(1, PT // 2) as i:
                    for par in range(2):
                        tile(2 * i + par, par, i)
                scores(SAMPLE, NS, cross_s, decay_s)
                dve.wait_ge(state_landed, 32)
                for p in range(NPAIR):
                    dve.wait_ge(update_done, by(SAMPLE) + p)
                    for r in range(2):
                        rows = slice(HD * r, HD * r + HD)
                        dve.scalar_tensor_tensor(S_out[rows, :, p], S_in[rows, :, p, HD * r:HD * r + HD],
                                                 chunk_s[rows, p:p + 1],
                                                 su_ps[rows].rearrange("d a (c e) -> d (a c) e", e=HD),
                                                 ALU.mult, ALU.add).then_inc(sout_ready, 1)
                centre(SAMPLE, NS)
                variance(SAMPLE)
                finish(SAMPLE, 0, 16 * PT // 2)

            @block.tensor
            def _(pe):
                for s in (qk_turned, inner_done, update_done, o_done):
                    pe.sem_inc(s, 1)

                def turn(t):
                    pe.wait_ge(qk_ready, by(t))
                    pe.wait_ge(qkT_ready, by(t - 1))
                    for g in range(2):
                        for p in range(NPAIR):
                            h = g * NH + 2 * p
                            mm = pe.transpose(qk_ps[g][:, p, :], qk[:, h:h + 2, :].rearrange("t h d -> t (h d)"), ident[:, :])
                    mm.then_inc(qk_turned, 1)

                def inner(t, rows):
                    pe.wait_ge(qkT_ready, by(t))
                    pe.wait_ge(inT_ready, by(t - 1))
                    for p in range(NPAIR):
                        for r in range(2):
                            mm = pe.matmul(in_ps[r][0:rows, p, 0:rows], kT[:, r, p, 0:rows], qT[:, p, 0:rows],
                                           start=True, stop=True)
                    mm.then_inc(inner_done, 1)

                def tile(t, par):
                    turn(t)
                    inner(t, 128)
                    pe.wait_ge(kd_ready, by(t))
                    pe.wait_ge(S_ready, by(t - 1))
                    for p in range(NPAIR):
                        mm = pe.matmul(su_ps[:, p, :], kd[:, 2 * p:2 * p + 2, :].rearrange("t h d -> t (h d)"),
                                       zr[:, par, 2, 2 * p:2 * p + 2, :].rearrange("t h d -> t (h d)"), start=True, stop=True)
                    mm.then_inc(update_done, 1)
                    pe.wait_ge(qd_ready, by(t))
                    pe.wait_ge(inT_ready, by(t))
                    pe.wait_ge(oc_ready, by(t - 1))
                    for p in range(NPAIR):
                        pe.matmul(o_ps[:, 2 * p:2 * p + 2, :].rearrange("t h d -> t (h d)"), qd[:, p, :], S[:, par, p, :],
                                  start=True, stop=False)
                        for r in range(2):
                            mm = pe.matmul(o_ps[:, 2 * p + r, :], inT[:, r, p, :], zr[:, par, 2, 2 * p + r, :],
                                           start=False, stop=(r == 1))
                    mm.then_inc(o_done, 1)

                pe.wait_ge(cleared, 2)
                with pe.Fori(0, PT // 2) as i:
                    for par in range(2):
                        tile(2 * i + par, par)
                turn(SAMPLE)
                inner(SAMPLE, NS)
                pe.wait_ge(kd_ready, by(SAMPLE))
                pe.wait_ge(vm_ready, 1)
                pe.wait_ge(S_ready, by(PT - 1))
                for p in range(NPAIR):
                    if p:
                        pe.wait_ge(sout_ready, 2 * p)
                    for r in range(2):
                        mm = pe.matmul(su_ps[HD * r:HD * r + HD].rearrange("d a (c e) -> d (a c) e", e=HD),
                                       kd[0:NS, 2 * p + r, :], vm[:, :, HD * (2 * p + r):HD * (2 * p + r + 1)],
                                       start=True, stop=True)
                    mm.then_inc(update_done, 1)
                pe.wait_ge(state_landed, 32)
                pe.wait_ge(qd_ready, by(SAMPLE))
                pe.wait_ge(inT_ready, by(SAMPLE))
                pe.wait_ge(oc_ready, by(SAMPLE - 1))
                for p in range(NPAIR):
                    for b in range(DEC_B):
                        pe.matmul(o_ps[0:NS, 2 * p:2 * p + 2, :].rearrange("t h d -> t (h d)"),
                                  qdm[:, p, b * NS:b * NS + NS], S_in[:, b, p, :], start=(b == 0), stop=False)
                    for r in range(2):
                        mm = pe.matmul(o_ps[0:NS, 2 * p + r, :], inT[0:NS, r, p, 0:NS], zr[0:NS, 0, 2, 2 * p + r, :],
                                       start=False, stop=(r == 1))
                mm.then_inc(o_done, 1)


def distance_tables(nc, A, tab, bias_s):
    K = N_BUCKETS + 1
    with ExitStack() as ctx:
        sb = lambda n, s, d=F32: ctx.enter_context(nc.sbuf_tensor(n, s, d))
        ps = lambda n, s: ctx.enter_context(nc.psum_tensor(n, s, F32))
        sem = lambda n: nc.alloc_semaphore("p0_" + n)
        rel = sb("rel", [K, NH])
        dist_p, dist_s = sb("dist_p", [K, TABW]), sb("dist_s", [K, STILES * DEC_T * 128])
        row = sb("row", [NH, TABW])
        r_ps = [ps(f"r_ps{i}", [NH, TABW // 3]) for i in range(3)]
        b_ps = [ps(f"b_ps{i}", [128, n, DEC_T, NH]) for i, n in enumerate((6, STILES - 6))]
        landed, samples_landed, ones_set = sem("landed"), sem("samples_landed"), sem("ones_set")
        rows_done, row_ready, bias_done, bias_ready, stored = map(
            sem, ("rows_done", "row_ready", "bias_done", "bias_ready", "stored"))

        with nc.Block() as block:

            @block.sync
            def _(sp):
                sp.dma_start(rel[0:N_BUCKETS, :], A["rel_bias"]).then_inc(landed, 16)
                sp.dma_start(dist_p[:, :], A["c_dist_p"]).then_inc(landed, 16)
                sp.dma_start(dist_s[:, :], A["c_dist_s"]).then_inc(samples_landed, 16)
                sp.wait_ge(row_ready, 3)
                sp.dma_start(tab, row[:, :].unsqueeze(1).broadcast_to([NH, 128, TABW])).then_inc(stored, 16)
                sp.wait_ge(stored, 16)

            @block.vector
            def _(dve):
                dve.memset(rel[N_BUCKETS:K, :], 1.0).then_inc(ones_set, 1)
                dve.wait_ge(rows_done, 1)
                for n in range(3):
                    w = TABW // 3
                    dve.tensor_copy(row[:, n * w:n * w + w], r_ps[n][:, :]).then_inc(row_ready, 1)
                dve.wait_ge(bias_done, 1)
                for n, cut in enumerate((slice(0, 6), slice(6, STILES))):
                    dve.tensor_copy(bias_s[:, cut], b_ps[n][:].rearrange("k j t h -> k j h t")).then_inc(bias_ready, 1)

            @block.tensor
            def _(pe):
                pe.wait_ge(ones_set, 1)
                pe.wait_ge(landed, 32)
                for n in range(3):
                    w = TABW // 3
                    mm = pe.matmul(r_ps[n][:, :], rel[:, :], dist_p[:, n * w:n * w + w], start=True, stop=True)
                mm.then_inc(rows_done, 1)
                pe.wait_ge(samples_landed, 16)
                for j in range(STILES):
                    for t in range(DEC_T):
                        c = (j * DEC_T + t) * 128
                        mm = pe.matmul(b_ps[j // 6][:, j % 6, t, :], dist_s[:, c:c + 128], rel[:, :], start=True, stop=True)
                mm.then_inc(bias_done, 1)


def prompt_attention(nc, A, z, mix, tab, ident):
    UNITS = 2 * PT
    at = lambda p, u: UNITS * p + u + 3
    with ExitStack() as ctx:
        sb = lambda n, s, d=F32: ctx.enter_context(nc.sbuf_tensor(n, s, d))
        ps = lambda n, s: ctx.enter_context(nc.psum_tensor(n, s, F32))
        sem = lambda n: nc.alloc_semaphore("p3_" + n)
        q_n, k_n = sb("q_n", [128, PT, 128]), sb("k_n", [128, PT, 128])
        v_all = sb("v_all", [128, PT, WID])
        bias = sb("bias", [128, NH, SEQ])
        qT, kT = sb("qT", [128, SEQ]), sb("kT", [128, 2, SEQ])
        S, P_T = sb("S3", [128, 2, SEQ]), sb("P_T", [128, 2, PT, 128])
        O = sb("O", [128, PT, 128])
        least, total, share = (sb(n, [128, UNITS]) for n in ("least", "total", "share"))
        S_ps = [ps(f"S_ps{i}", [128, SEQ]) for i in range(2)]
        T_ps = [ps(f"T_ps{i}", [128, 4, 128]) for i in range(2)]
        O_ps, prep_ps = ps("O_ps", [128, 128]), ps("prep_ps", [128, 4, 128])
        pair_landed, prep_done, prep_ready = sem("pair_landed"), sem("prep_done"), sem("prep_ready")
        zeros_set, N_ready = sem("zeros_set"), sem("N_ready")
        S_done, E_ready, P_ready, T_done, PT_low, PT_high, share_ready, V_done, O_ready = map(
            sem, ("S_done", "E_ready", "P_ready", "T_done", "PT_low", "PT_high", "share_ready", "V_done", "O_ready"))
        O_stored, bias_landed = sem("O_stored"), sem("bias_landed")
        high = lambda p, u: PT * p + (u - PT) + 3

        with nc.Block() as block:

            @block.sync
            def _(sp):
                rows = z[0:SEQ, :].rearrange("(t p) c -> p t c", p=128)

                def load(p):
                    for n, dst in enumerate((q_n[:, :, :], k_n[:, :, :], v_all[:, :, bass.ds(p * 128, 128)])):
                        sp.dma_start(dst, rows[:, :, bass.ds((4 + n) * WID + p * 128, 128)]).then_inc(pair_landed, 16)

                def store(p):
                    sp.wait_ge(O_ready, at(p, UNITS - 1))
                    sp.dma_start(mix[0:SEQ, bass.ds(WID + p * 128, 128)].rearrange("(t p) c -> p t c", p=128),
                                 O[:, :, :]).then_inc(O_stored, 16)

                load(0)
                for h in range(NH):
                    sp.dma_start(bias[:, h, :], bass.AP(tensor=tab.tensor, offset=h * 128 * TABW + 127, ap=[[TABW - 1, 128], [1, SEQ]])
                                 ).then_inc(bias_landed, 16)
                with sp.Fori(0, NPAIR - 1) as p:
                    sp.wait_ge(pair_landed, 48 * p + 48)
                    sp.wait_ge(prep_done, 4 * p + 4)
                    load(p + 1)
                    store(p)
                store(NPAIR - 1)
                sp.wait_ge(O_stored, 16 * NPAIR)

            @block.scalar
            def _(act):
                for s in (P_ready, PT_high, O_ready):
                    act.sem_inc(s, 2)
                act.sem_inc(prep_ready, 1)

                def exp(p, u):
                    n = (u // 2 + 1) * 128
                    act.wait_ge(E_ready, at(p, u))
                    act.activation(S[:, u % 2, 0:n], S[:, u % 2, 0:n], ACT.Exp, bias=least[:, u:u + 1], scale=-1.0,
                                   accum_out=total[:, u:u + 1]).then_inc(P_ready, 1)

                def evacuate(p, u):
                    nt = u // 2 + 1
                    if nt > 4:
                        act.wait_ge(T_done, at(p, u))
                        act.wait_ge(V_done, at(p, u - 2))
                        act.copy(P_T[:, u % 2, 4:nt, :], T_ps[1][:, 0:nt - 4, :]).then_inc(PT_high, 1)

                def scale(p, u):
                    act.wait_ge(V_done, at(p, u))
                    act.wait_ge(share_ready, at(p, u))
                    if u == 0:
                        act.wait_ge(O_stored, 16 * p)
                    own = slice(HD * (u % 2), HD * (u % 2) + HD)
                    act.activation(O[:, u // 2, own], O_ps[:, own], ACT.Copy, scale=share[:, u:u + 1]).then_inc(O_ready, 1)

                def pair(p):
                    for g in range(4):
                        act.wait_ge(prep_done, 4 * p + g + 1)
                        if g == 0:
                            act.wait_ge(S_done, at(p - 1, UNITS - 1))
                        src, cols = prep_ps[:].rearrange("c t p -> c (t p)"), slice(512 * (g % 2), 512 * (g % 2) + 512)
                        if g < 2:
                            act.mul(qT[:, cols], src, HD ** -0.5).then_inc(prep_ready, 1)
                        else:
                            act.copy(kT[0:HD, 0, cols], src[0:HD, :])
                            act.copy(kT[HD:128, 1, cols], src[HD:128, :]).then_inc(prep_ready, 1)
                    for u in range(UNITS + 2):
                        if u < UNITS:
                            exp(p, u)
                        if 1 <= u <= UNITS:
                            evacuate(p, u - 1)
                        if u >= 2:
                            scale(p, u - 2)

                act.wait_ge(zeros_set, 1)
                with act.Fori(0, NPAIR) as p:
                    pair(p)

            @block.vector
            def _(dve):
                dve.memset(kT[:, :, :], 0.0).then_inc(zeros_set, 1)
                for s in (N_ready, E_ready, PT_low, share_ready):
                    dve.sem_inc(s, 2)

                def scores(p, u):
                    n = (u // 2 + 1) * 128
                    dve.wait_ge(S_done, at(p, u))
                    dve.wait_ge(T_done, at(p, u - 2))
                    dve.scalar_tensor_tensor(
                        S[:, u % 2, 0:n], S_ps[u % 2][:, 0:n], -1.0,
                        bias[:, bass.ds(2 * p + u % 2, 1), SEQ - n:SEQ].rearrange("q h k -> q (h k)"),
                        ALU.mult, ALU.subtract).then_inc(N_ready, 1)
                    dve.wait_ge(N_ready, at(p, u))
                    dve.tensor_reduce(least[:, u:u + 1], S[:, u % 2, 0:n], AXX, ALU.min).then_inc(E_ready, 1)

                def evacuate(p, u):
                    nt = min(u // 2 + 1, 4)
                    dve.wait_ge(T_done, at(p, u))
                    dve.wait_ge(V_done, at(p, u - 2))
                    dve.tensor_copy(P_T[:, u % 2, 0:nt, :], T_ps[0][:, 0:nt, :]).then_inc(PT_low, 1)

                def reciprocal(p, u):
                    dve.wait_ge(P_ready, at(p, u))
                    dve.wait_ge(O_ready, at(p, u - 2))
                    dve.reciprocal(share[:, u:u + 1], total[:, u:u + 1]).then_inc(share_ready, 1)

                dve.wait_ge(bias_landed, 16 * NH)
                with dve.Fori(0, NPAIR) as p:
                    for u in range(UNITS + 1):
                        if u < UNITS:
                            scores(p, u)
                        if u >= 1:
                            evacuate(p, u - 1)
                            reciprocal(p, u - 1)

            @block.tensor
            def _(pe):
                for s in (S_done, T_done, V_done):
                    pe.sem_inc(s, 2)

                def scores(p, u):
                    n = (u // 2 + 1) * 128
                    q0 = (u // 2) * 128
                    pe.wait_ge(E_ready, at(p, u - 2))
                    for k in range(0, n, 512):
                        m = min(n, k + 512)
                        mm = pe.matmul(S_ps[u % 2][:, k:m], qT[:, q0:q0 + 128], kT[:, u % 2, k:m], start=True, stop=True)
                    mm.then_inc(S_done, 1)

                def turn(p, u):
                    pe.wait_ge(P_ready, at(p, u))
                    pe.wait_ge(PT_low, at(p, u - 1))
                    if u > PT:
                        pe.wait_ge(PT_high, high(p, u - 1))
                    for k in range(u // 2 + 1):
                        mm = pe.transpose(T_ps[k // 4][:, k % 4, :], S[:, u % 2, k * 128:k * 128 + 128], ident[:, :])
                    mm.then_inc(T_done, 1)

                def values(p, u):
                    nt = u // 2 + 1
                    pe.wait_ge(PT_low, at(p, u))
                    if u >= PT:
                        pe.wait_ge(PT_high, high(p, u))
                    pe.wait_ge(O_ready, at(p, u - 1))
                    for k in range(nt):
                        mm = pe.matmul(O_ps[:, :], P_T[:, u % 2, k, :], v_all[:, k, bass.ds(p * 128, 128)],
                                       start=(k == 0), stop=(k == nt - 1))
                    mm.then_inc(V_done, 1)

                with pe.Fori(0, NPAIR) as p:
                    pe.wait_ge(pair_landed, 48 * p + 48)
                    for g in range(4):
                        pe.wait_ge(prep_ready, 4 * p + g + 1)
                        for t in range(4):
                            mm = pe.transpose(prep_ps[:, t, :], (q_n, k_n)[g // 2][:, 4 * (g % 2) + t, :], ident[:, :])
                        mm.then_inc(prep_done, 1)
                    pe.wait_ge(prep_ready, 4 * p + 5)
                    scores(p, 0)
                    scores(p, 1)
                    for u in range(UNITS + 1):
                        if u + 2 < UNITS:
                            scores(p, u + 2)
                        if u < UNITS:
                            turn(p, u)
                        if u >= 1:
                            values(p, u - 1)


def sample_attention(nc, A, z, mix, bias_s, ident):
    RING = 4
    C = NH * DEC_T
    EVEN, ODD = (STILES + 1) // 2, STILES // 2
    with ExitStack() as ctx:
        sb = lambda n, s, d=F32: ctx.enter_context(nc.sbuf_tensor(n, s, d))
        ps = lambda n, s: ctx.enter_context(nc.psum_tensor(n, s, F32))
        sem = lambda n: nc.alloc_semaphore("p4_" + n)
        K, V = sb("K", [128, 2, STILES, WID]), sb("V", [128, 2, STILES, WID])
        KT = sb("KT", [128, STILES, NPAIR, 128])
        q_n = sb("q_n4", [NS, WID])
        Q = sb("Q", [128, NPAIR, DEC_B, 2 * DEC_T])
        Q_b = sb("Q_b", [128, NPAIR, 2 * DEC_T])
        E, P = sb("E4", [128, STILES, C]), sb("P4", [128, STILES, C])
        most, part = sb("most", [128, 128]), sb("part", [128, C])
        peak, diag = sb("peak", [C, 1]), sb("diag", [C, C])
        ones, share = sb("ones", [128, 128]), sb("share4", [128, C])
        OT = sb("OT", [128, NPAIR, NS])
        mixs = sb("mixs", [NS, WID])
        K_ps = [ps(f"K_ps{i}", [128, NPAIR, 128]) for i in range(RING)]
        E_ps = [ps("E_psa", [128, WIDE, C]), ps("E_psb", [128, STILES - WIDE, C])]
        m_ps, O_ps = ps("m_ps", [128, 128]), ps("O_ps4", [128, NPAIR, 2 * DEC_T])
        K_landed, V_landed = ([sem(f"{n}_landed{i}") for i in range(2)] for n in "KV")
        q_landed, set_up, q_turned, Q_ready, Qb_ready = map(sem, ("q_landed", "set_up", "q_turned", "Q_ready", "Qb_ready"))
        (turned, K_even, K_odd, S_done, added, E_ready, most_turned, peak_ready, diag_ready, peak_spread, less_ready,
         P_ready, part_ready, total_done, V_done, share_ready, O_ready, out_turned, out_ready, stored) = map(
            sem, ("turned", "K_even", "K_odd", "S_done", "added", "E_ready", "most_turned", "peak_ready", "diag_ready",
                  "peak_spread", "less_ready", "P_ready", "part_ready", "total_done", "V_done", "share_ready", "O_ready",
                  "out_turned", "out_ready", "stored"))

        def evacuated(b, j):
            return (K_odd, ODD * (b + 1) + j // 2 + 1) if j % 2 else (K_even, EVEN * (b + 1) + j // 2 + 1)

        with nc.Block() as block:

            @block.sync
            def _(sp):
                def load(b, par):
                    for X, name, landed, zc in ((K, "cache_k_win", K_landed, 5), (V, "cache_v_win", V_landed, 6)):
                        rows = A[name][0].rearrange("b l h d -> (b l) (h d)")
                        if not isinstance(b, int) or b >= 2:
                            sp.wait_ge(*((turned, STILES * (b - 1)) if X is K else (V_done, by(b - 2))))
                        wide = rows[bass.ds(b * L, L), :].rearrange("(p x) c -> p (x c)", x=16)[:, 0:WIDE * WID]
                        sp.dma_start(X[:, par, 0:WIDE, :].rearrange("p j c -> p (j c)"), wide).then_inc(landed[par], 16)
                        rest = rows[bass.ds(b * L + REST, L - REST), :].rearrange("(g x) c -> g (x c)", x=16)[:, WIDE * WID:]
                        sp.dma_start(X[:, par, WIDE:WIDE + 2, :].rearrange("p j c -> p (j c)"),
                                     rest.rearrange("g (x c) -> g x c", x=4)).then_inc(landed[par], 16)
                        sp.dma_start(X[0:DEC_T, par, STILES - 1, :],
                                     z[bass.ds(SEQ + b * DEC_T, DEC_T), zc * WID:zc * WID + WID]).then_inc(landed[par], 16)

                sp.dma_start(q_n[:, :], z[SEQ:NTOK, 4 * WID:5 * WID]).then_inc(q_landed, 16)
                sp.wait_ge(set_up, 5)
                load(0, 0)
                load(1, 1)
                with sp.Fori(1, DEC_B // 2) as i:
                    for par in range(2):
                        load(2 * i + par, par)
                sp.wait_ge(out_ready, 1)
                sp.dma_start(mix[SEQ:NTOK, WID:2 * WID], mixs[:, :]).then_inc(stored, 16)
                sp.wait_ge(stored, 16)

            @block.gpsimd
            def _(pool):
                pool.memset(K[:, 0, STILES - 1, :], 0.0).then_inc(set_up, 1)
                pool.memset(K[:, 1, STILES - 1, :], 0.0).then_inc(set_up, 1)
                pool.memset(V[:, 0, STILES - 1, :], 0.0).then_inc(set_up, 1)
                pool.memset(V[:, 1, STILES - 1, :], 0.0).then_inc(set_up, 1)
                pool.memset(Q[:, :, :, :], 0.0).then_inc(set_up, 1)
                pool.memset(ones[:, :], 1.0).then_inc(set_up, 1)
                pool.memset(most[:, :], 0.0).then_inc(set_up, 1)
                pool.wait_ge(Q_ready, 1)
                pool.sem_inc(Qb_ready, 1)
                with pool.Fori(0, DEC_B) as b:
                    pool.wait_ge(S_done, by(b - 1))
                    pool.tensor_copy(Q_b[:, :, :], Q[:, :, bass.ds(b, 1), :].rearrange("d p b t -> d p (b t)")).then_inc(Qb_ready, 1)

            @block.scalar
            def _(act):
                act.sem_inc(K_even, EVEN)
                act.sem_inc(P_ready, 1)

                def evacuate(b, j):
                    act.wait_ge(turned, STILES * b + j + 1)
                    act.wait_ge(S_done, by(b - 1))
                    act.copy(KT[:, j], K_ps[j % RING][:, :, :]).then_inc(K_even, 1)

                def exp(b):
                    act.wait_ge(less_ready, by(b))
                    act.wait_ge(V_done, by(b - 1))
                    act.activation(P[:, :, :], E[:, :, :], ACT.Exp).then_inc(P_ready, 1)

                def step(b, first=False, last=False):
                    for j in range(0, STILES, 2):
                        if j == 8 and not first:
                            exp(b - 1)
                        if not last:
                            evacuate(b, j)

                act.wait_ge(q_turned, 1)
                act.wait_ge(set_up, 5)
                for r in range(2):
                    d = slice(HD * r, HD * r + HD)
                    x = act.mul(Q[d, :, :, DEC_T * r:DEC_T * r + DEC_T],
                                K_ps[RING - 1][d, :, 0:NS].rearrange("d p (b t) -> d p b t", b=DEC_B), HD ** -0.5)
                x.then_inc(Q_ready, 1)
                step(0, first=True)
                with act.Fori(1, DEC_B) as b:
                    step(b)
                step(DEC_B, last=True)
                act.wait_ge(out_turned, 1)
                act.copy(mixs[:, :], K_ps[0][0:NS].rearrange("t p c -> t (p c)")).then_inc(out_ready, 1)

            @block.vector
            def _(dve):
                dve.sem_inc(K_odd, ODD)
                dve.wait_ge(set_up, 7)
                for s in (added, E_ready, peak_ready, diag_ready, less_ready, part_ready, share_ready, O_ready):
                    dve.sem_inc(s, 1)

                def evacuate(b, j):
                    dve.wait_ge(turned, STILES * b + j + 1)
                    dve.wait_ge(S_done, by(b - 1))
                    dve.tensor_copy(KT[:, j], K_ps[j % RING][:, :, :]).then_inc(K_odd, 1)

                def add_bias(b):
                    dve.wait_ge(S_done, by(b))
                    dve.wait_ge(P_ready, by(b - 1))
                    dve.tensor_tensor(E[:, 0:WIDE], E_ps[0][:, :, :], bias_s[:, 0:WIDE].rearrange("k j h t -> k j (h t)"), ALU.add)
                    dve.tensor_tensor(E[:, WIDE:], E_ps[1][:, :, :], bias_s[:, WIDE:].rearrange("k j h t -> k j (h t)"),
                                      ALU.add).then_inc(added, 1)
                    dve.wait_ge(added, by(b))
                    dve.wait_ge(most_turned, by(b - 1))
                    dve.tensor_reduce(most[:, 0:C], E[:, :, :].rearrange("k j c -> k c j"), AXX, ALU.max).then_inc(E_ready, 1)

                def find_peak(b):
                    dve.wait_ge(most_turned, by(b))
                    dve.tensor_reduce(peak[:, :], m_ps[0:C, :], AXX, ALU.max).then_inc(peak_ready, 1)
                    dve.wait_ge(peak_ready, by(b))
                    dve.wait_ge(peak_spread, by(b - 1))
                    dve.tensor_scalar(diag[:, :], ident[0:C, 0:C], peak[:, 0:1], None, ALU.mult).then_inc(diag_ready, 1)

                def subtract(b):
                    dve.wait_ge(peak_spread, by(b))
                    dve.tensor_tensor(E[:, :, :], E[:, :, :], m_ps[:, 0:C].unsqueeze(1).broadcast_to([128, STILES, C]),
                                      ALU.subtract).then_inc(less_ready, 1)

                def partial_sums(b):
                    dve.wait_ge(P_ready, by(b))
                    dve.wait_ge(total_done, by(b - 1))
                    dve.tensor_reduce(part[:, :], P[:, :, :].rearrange("k j c -> k c j"), AXX, ALU.add).then_inc(part_ready, 1)

                def normalise(b):
                    dve.wait_ge(total_done, by(b))
                    dve.wait_ge(O_ready, by(b - 1))
                    dve.reciprocal(share[:, :], m_ps[:, 0:C]).then_inc(share_ready, 1)
                    dve.wait_ge(share_ready, by(b))
                    dve.wait_ge(V_done, by(b))
                    for r in range(2):
                        d = slice(HD * r, HD * r + HD)
                        x = dve.tensor_tensor(OT[d, :, bass.ds(b * DEC_T, DEC_T)], O_ps[d, :, DEC_T * r:DEC_T * r + DEC_T],
                                              share[d, :].rearrange("d (p r t) -> d p r t", r=2, t=DEC_T)[:, :, r], ALU.mult)
                    x.then_inc(O_ready, 1)

                def step(b, first=False, last=False):
                    for j in range(1, STILES, 2):
                        if j == 5 and not first:
                            find_peak(b - 1)
                        if j == 7 and not first:
                            subtract(b - 1)
                        if not last:
                            evacuate(b, j)
                    if not first:
                        partial_sums(b - 1)
                    if not last:
                        add_bias(b)
                    if not first:
                        normalise(b - 1)

                step(0, first=True)
                with dve.Fori(1, DEC_B) as b:
                    step(b)
                step(DEC_B, last=True)

            @block.tensor
            def _(pe):
                for s in (S_done, most_turned, peak_spread, total_done, V_done):
                    pe.sem_inc(s, 1)

                def turn(b, par, j):
                    before = j - RING if j >= RING else max(x for x in range(STILES) if x % RING == j)
                    pe.wait_ge(*evacuated(b if j >= RING else b - 1, before))
                    for p in range(NPAIR):
                        mm = pe.transpose(K_ps[j % RING][:, p, :], K[:, par, j, 128 * p:128 * p + 128], ident[:, :])
                    mm.then_inc(turned, 1)

                def scores(b):
                    pe.wait_ge(*evacuated(b, STILES - 1))
                    pe.wait_ge(*evacuated(b, STILES - 2))
                    pe.wait_ge(added, by(b - 1))
                    pe.wait_ge(Qb_ready, by(b))
                    for j in range(STILES):
                        for p in range(NPAIR):
                            mm = pe.matmul(E_ps[j // WIDE][:, j % WIDE, 16 * p:16 * p + 16], KT[:, j, p, :],
                                           Q_b[:, p, :], start=True, stop=True)
                    mm.then_inc(S_done, 1)

                def turn_most(b):
                    pe.wait_ge(E_ready, by(b))
                    pe.wait_ge(share_ready, by(b - 1))
                    pe.transpose(m_ps[:, :], most[:, :], ident[:, :]).then_inc(most_turned, 1)

                def spread_peak(b):
                    pe.wait_ge(diag_ready, by(b))
                    pe.matmul(m_ps[:, 0:C], ones[0:C, :], diag[:, :], start=True, stop=True).then_inc(peak_spread, 1)

                def values(b, par):
                    pe.wait_ge(P_ready, by(b))
                    pe.wait_ge(O_ready, by(b - 1))
                    pe.wait_ge(part_ready, by(b))
                    pe.matmul(m_ps[:, 0:C], ones[:, :], part[:, :], start=True, stop=True).then_inc(total_done, 1)
                    for p in range(NPAIR):
                        for j in range(STILES):
                            mm = pe.matmul(O_ps[:, p, :], V[:, par, j, 128 * p:128 * p + 128], P[:, j, 16 * p:16 * p + 16],
                                           start=(j == 0), stop=(j == STILES - 1))
                    mm.then_inc(V_done, 1)

                def step(b, par, lap, first=False, last=False):
                    if not last:
                        pe.wait_ge(K_landed[par], 48 * lap)
                    for j in range(STILES):
                        if j == 4 and not first:
                            turn_most(b - 1)
                        if j == 7 and not first:
                            spread_peak(b - 1)
                        if not last:
                            turn(b, par, j)
                    if not last:
                        scores(b)
                    if not first:
                        values(b - 1, 1 - par)

                pe.wait_ge(q_landed, 16)
                for p in range(NPAIR):
                    mm = pe.transpose(K_ps[RING - 1][:, p, 0:NS], q_n[:, 128 * p:128 * p + 128], ident[0:NS, 0:NS])
                mm.then_inc(q_turned, 1)
                pe.wait_ge(Q_ready, 1)
                pe.wait_ge(set_up, 7)
                step(0, 0, 1, first=True)
                pe.wait_ge(V_landed[0], 48)
                with pe.Fori(0, DEC_B // 2 - 1) as i:
                    step(2 * i + 1, 1, i + 1)
                    pe.wait_ge(V_landed[1], 48 * i + 48)
                    step(2 * i + 2, 0, i + 2)
                    pe.wait_ge(V_landed[0], 48 * i + 96)
                step(DEC_B - 1, 1, DEC_B // 2)
                pe.wait_ge(V_landed[1], 24 * DEC_B)
                step(DEC_B, 0, 0, last=True)
                pe.wait_ge(O_ready, by(DEC_B - 1))
                for p in range(NPAIR):
                    mm = pe.transpose(K_ps[0][0:NS, p, :], OT[:, p, :], ident[:, :])
                mm.then_inc(out_turned, 1)


def out_projection(nc, A, mix, x_mid, h_hi, h_lo, ident):
    HK = KT // 2
    w_v = A["w_out"][0].rearrange("(q k p) n -> q p k n", q=4, p=128)
    with ExitStack() as ctx:
        sb = lambda n, s, d=F32: ctx.enter_context(nc.sbuf_tensor(n, s, d))
        ps = lambda n, s: ctx.enter_context(nc.psum_tensor(n, s, F32))
        sem = lambda n: nc.alloc_semaphore("p5_" + n)
        w_raw = sb("wo_raw", [128, 2, D_MODEL])
        w_hi, w_lo = sb("wo_hi", [128, KT, D_MODEL], F32R), sb("wo_lo", [128, KT, D_MODEL], F32R)
        m_n, x_n = sb("m_n", [128, 2, D_MODEL]), sb("x_n", [128, 2, D_MODEL])
        m_hi, m_lo = sb("m_hi", [128, 1, KT, 128], F32R), sb("m_lo", [128, 1, KT, 128], F32R)
        y, xm, xn = sb("y5", [128, D_MODEL]), sb("xm", [128, 2, D_MODEL]), sb("xn5", [128, D_MODEL])
        hg = sb("hg5", [128, 2, HK, 128])
        g_post, g_rows, gT = sb("g_post", [128, D_MODEL]), sb("g_rows5", [KT, 128]), sb("gT5", [128, KT])
        stat, mhalf = sb("stat5", [128, 6]), sb("mhalf5", [128, 1])
        m_ps = [ps(f"m5_ps{i}", [128, HK, 128]) for i in range(2)]
        x_ps = [ps(f"x5_ps{i}", [128, HK, 128]) for i in range(2)]
        y_ps = [ps(f"y5_ps{i}", [128, D_MODEL]) for i in range(2)]
        m_landed, x_landed, xm_stored, w_landed = (
            [sem(f"{n}{i}") for i in range(2)] for n in ("m_landed", "x_landed", "xm_stored", "w_landed"))
        g_landed, w_hi_ready, w_lo_ready, set_up, g_turned, g_ready = map(
            sem, ("g_landed", "w_hi_ready", "w_lo_ready", "set_up", "g_turned", "g_ready"))
        (m_turned, m_hi_ready, m_lo_ready, y_done, y_squared, y_mean, y_rstd, y_ready, xm_ready, xm_squared, xm_mean,
         xm_rstd, xn_ready, x_turned, hg_ready, hi_ready, lo_ready) = map(
            sem, ("m_turned", "m_hi_ready", "m_lo_ready", "y_done", "y_squared", "y_mean", "y_rstd", "y_ready", "xm_ready",
                  "xm_squared", "xm_mean", "xm_rstd", "xn_ready", "x_turned", "hg_ready", "hi_ready", "lo_ready"))
        half = lambda t, q: 2 * t + q + 3
        S = PT

        def over_tiles(eng, step):
            step(0, 0)
            step(1, 1)
            with eng.Fori(1, PT // 2) as i:
                for par in range(2):
                    step(2 * i + par, par, i)
            step(S, 0)

        with nc.Block() as block:

            @block.sync
            def _(sp):
                def load(t, par, x_rows, rows=128):
                    if not isinstance(t, int) or t >= 2:
                        sp.wait_ge(m_turned, by(t - 2))
                        sp.wait_ge(xm_ready, by(t - 2))
                    sp.dma_start(m_n[0:rows, par, :], mix[bass.ds(t * 128, rows), :]).then_inc(m_landed[par], 16)
                    sp.dma_start(x_n[0:rows, par, :], x_rows).then_inc(x_landed[par], 16)

                def store(t, par, rows=128):
                    sp.wait_ge(xm_ready, by(t))
                    sp.dma_start(x_mid[bass.ds(t * 128, rows), :], xm[0:rows, par, :]).then_inc(xm_stored[par], 16)

                x_p = A["x_prompt"][0]
                load(0, 0, x_p[0:128, :])
                sp.dma_start(g_rows[:, :], A["g_pre_ffn"][0].rearrange("(k p) -> k p", p=128)).then_inc(g_landed, 16)
                sp.dma_start(g_post[:, :], A["g_post_mix"][0].partition_broadcast(128)).then_inc(g_landed, 16)
                for k in range(KT):
                    if k >= 2:
                        sp.wait_ge(w_lo_ready, k - 1)
                    sp.dma_start(w_raw[:, k % 2, :], A["w_out"][0, k * 128:k * 128 + 128, :]).then_inc(w_landed[k % 2], 16)
                load(1, 1, x_p[128:256, :])
                with sp.Fori(0, PT // 2 - 1) as i:
                    for par in range(2):
                        load(2 * i + 2 + par, par, x_p[bass.ds(i * 256 + 256 + 128 * par, 128), :])
                        store(2 * i + par, par)
                load(S, 0, A["x_sample"].rearrange("b t d -> (b t) d"), NS)
                store(PT - 2, 0)
                store(PT - 1, 1)
                store(S, 0, NS)
                sp.wait_ge(xm_stored[0], 80)
                sp.wait_ge(xm_stored[1], 64)

            @block.gpsimd
            def _(pool):
                pool.memset(mhalf[:, :], -0.5).then_inc(set_up, 1)
                for s in (y_rstd, xm_ready, xm_rstd):
                    pool.sem_inc(s, 1)
                pool.sem_inc(lo_ready, 2)
                pool.wait_ge(set_up, 1)

                def residual(t, par, i=0):
                    pool.wait_ge(y_mean, by(t))
                    pool.tensor_tensor(stat[:, 2:3], stat[:, 1:2], mhalf[:, :], ALU.pow).then_inc(y_rstd, 1)
                    pool.wait_ge(y_ready, by(t))
                    pool.wait_ge(x_landed[par], 16 * PT // 2 + 16 if known(t, S) else 16 * i + 16)
                    if known(t, S) or not known(i, 0):
                        pool.wait_ge(xm_stored[par], 16 * PT // 2 if known(t, S) else 16 * i)
                    pool.wait_ge(xn_ready, by(t - 1))
                    pool.tensor_tensor(xm[:, par, :], y[:, :], x_n[:, par, :], ALU.add).then_inc(xm_ready, 1)
                    pool.wait_ge(xm_mean, by(t))
                    pool.tensor_tensor(stat[:, 5:6], stat[:, 4:5], mhalf[:, :], ALU.pow).then_inc(xm_rstd, 1)

                def low(t, n=128):
                    for q in range(2):
                        pool.wait_ge(hi_ready, half(t, q))
                        cut = (slice(None), slice(HK * q, HK * q + HK), bass.ds(t * 128, n))
                        pool.tensor_tensor(h_lo[cut], hg[:, q, :, 0:n], h_hi[cut].bitcast(F32), ALU.subtract).then_inc(lo_ready, 1)

                residual(0, 0)
                residual(1, 1)
                low(0)
                with pool.Fori(1, PT // 2) as i:
                    for par in range(2):
                        residual(2 * i + par, par, i)
                        low(2 * i + par - 1)
                residual(S, 0)
                low(S - 1)
                low(S, NS)

            @block.scalar
            def _(act):
                for s in (m_hi_ready, y_squared, xm_squared):
                    act.sem_inc(s, 1)
                act.sem_inc(hi_ready, 2)

                def mix_high(t):
                    act.wait_ge(m_turned, by(t))
                    act.wait_ge(y_done, by(t - 1))
                    for q in range(2):
                        x = act.copy(m_hi[:, 0, HK * q:HK * q + HK, :], m_ps[q][:, :, :])
                    x.then_inc(m_hi_ready, 1)

                def square_y(t, par):
                    act.wait_ge(y_done, by(t))
                    act.wait_ge(xm_ready, by(t - 1))
                    act.activation(y[:, :], y_ps[par][:, :], ACT.Square, accum_out=stat[:, 0:1]).then_inc(y_squared, 1)

                def square_x(t, par):
                    act.wait_ge(xm_ready, by(t))
                    act.wait_ge(x_turned, half(t - 1, 1))
                    act.activation(xn[:, :], xm[:, par, :], ACT.Square, accum_out=stat[:, 3:4]).then_inc(xm_squared, 1)

                def high(t, n=128):
                    for q in range(2):
                        act.wait_ge(hg_ready, half(t, q))
                        act.copy(h_hi[:, HK * q:HK * q + HK, bass.ds(t * 128, n)], hg[:, q, :, 0:n]).then_inc(hi_ready, 1)

                def step(t, par, i=0):
                    if not known(t, S):
                        mix_high(t + 1)
                    square_y(t, par)
                    if not known(t, 0):
                        high(t - 1)
                    square_x(t, par)

                mix_high(0)
                for k in range(KT):
                    act.wait_ge(w_landed[k % 2], 16 * (k // 2) + 16)
                    act.copy(w_hi[:, k, :], w_raw[:, k % 2, :]).then_inc(w_hi_ready, 1)
                over_tiles(act, step)
                high(S, NS)

            @block.vector
            def _(dve):
                for s in (m_lo_ready, y_mean, y_ready, xm_mean, xn_ready):
                    dve.sem_inc(s, 1)
                dve.sem_inc(hg_ready, 2)
                dve.wait_ge(g_turned, 1)
                dve.tensor_copy(gT[:, :], x_ps[0][:, 0, 0:KT]).then_inc(g_ready, 1)
                dve.wait_ge(g_ready, 1)
                dve.wait_ge(g_landed, 32)

                def mix_low(t):
                    dve.wait_ge(m_hi_ready, by(t))
                    for q in range(2):
                        cut = (slice(None), 0, slice(HK * q, HK * q + HK))
                        x = dve.tensor_tensor(m_lo[cut], m_ps[q][:, :, :], m_hi[cut].bitcast(F32), ALU.subtract)
                    x.then_inc(m_lo_ready, 1)

                def scale_y(t, par):
                    dve.wait_ge(y_squared, by(t))
                    dve.tensor_scalar(stat[:, 1:2], stat[:, 0:1], 1.0 / D_MODEL, EPS, ALU.mult, ALU.add).then_inc(y_mean, 1)
                    dve.wait_ge(y_rstd, by(t))
                    dve.scalar_tensor_tensor(y[:, :], y_ps[par][:, :], stat[:, 2:3], g_post[:, :], ALU.mult, ALU.mult).then_inc(y_ready, 1)

                def scale_x(t, par):
                    dve.wait_ge(xm_squared, by(t))
                    dve.tensor_scalar(stat[:, 4:5], stat[:, 3:4], 1.0 / D_MODEL, EPS, ALU.mult, ALU.add).then_inc(xm_mean, 1)
                    dve.wait_ge(xm_rstd, by(t))
                    dve.tensor_scalar(xn[:, :], xm[:, par, :], stat[:, 5:6], None, ALU.mult).then_inc(xn_ready, 1)

                def gain(t):
                    for q in range(2):
                        dve.wait_ge(x_turned, half(t, q))
                        dve.wait_ge(lo_ready, half(t - 1, q))
                        dve.tensor_tensor(hg[:, q], x_ps[q][:, :, :], spread(gT[:, HK * q:HK * q + HK], [128, HK, 128]),
                                          ALU.mult).then_inc(hg_ready, 1)

                def step(t, par, i=0):
                    if not known(t, S):
                        mix_low(t + 1)
                    scale_y(t, par)
                    if not known(t, 0):
                        gain(t - 1)
                    scale_x(t, par)

                mix_low(0)
                for k in range(KT):
                    dve.wait_ge(w_hi_ready, k + 1)
                    dve.tensor_tensor(w_lo[:, k, :], w_raw[:, k % 2, :], w_hi[:, k, :].bitcast(F32), ALU.subtract).then_inc(w_lo_ready, 1)
                over_tiles(dve, step)
                gain(S)

            @block.tensor
            def _(pe):
                for s in (m_turned, y_done):
                    pe.sem_inc(s, 1)
                pe.sem_inc(x_turned, 2)

                def turn_mix(t, par, lap):
                    pe.wait_ge(m_landed[par], lap)
                    pe.wait_ge(m_lo_ready, by(t - 1))
                    for k in range(KT):
                        mm = pe.transpose(m_ps[k // HK][:, k % HK, :], m_n[:, par, 128 * k:128 * k + 128], ident[:, :])
                    mm.then_inc(m_turned, 1)

                def project(t, par):
                    pe.wait_ge(m_lo_ready, by(t))
                    pe.wait_ge(y_ready, by(t - 2)) if (not isinstance(t, int) or t >= 2) else None
                    for c in range(0, D_MODEL, 512):
                        for k in range(KT):
                            if known(t, 0) and c == 0:
                                pe.wait_ge(w_lo_ready, k + 1)
                            for n, (x, w) in enumerate(((m_hi, w_hi), (m_hi, w_lo), (m_lo, w_hi))):
                                mm = pe.matmul(y_ps[par][:, c:c + 512], x[:, 0, k, :], w[:, k, c:c + 512],
                                               start=(k, n) == (0, 0), stop=(k, n) == (KT - 1, 2))
                    mm.then_inc(y_done, 1)

                def turn_x(t):
                    pe.wait_ge(xn_ready, by(t))
                    for q in range(2):
                        pe.wait_ge(hg_ready, half(t - 1, q))
                        for k in range(HK):
                            c = (HK * q + k) * 128
                            mm = pe.transpose(x_ps[q][:, k, :], xn[:, c:c + 128], ident[:, :])
                        mm.then_inc(x_turned, 1)

                def step(t, par, i=0):
                    if not known(t, S):
                        lap = 16 if known(t, 0) else 32 if known(t, 1) else 16 * i + 16 + 16 * par
                        turn_mix(t + 1, 1 - par, lap)
                    project(t, par)
                    if not known(t, 0):
                        turn_x(t - 1)

                pe.wait_ge(g_landed, 32)
                pe.transpose(x_ps[0][:, 0, 0:KT], g_rows[:, :], ident[0:KT, 0:KT]).then_inc(g_turned, 1)
                pe.wait_ge(g_ready, 1)
                turn_mix(0, 0, 16)
                over_tiles(pe, step)
                turn_x(S)


def ffn(nc, A, z, h_hi, h_lo, acc):
    HK, SUB, GROUP_D = KT // 2, 2, 2 * TT
    GROUPS = D_FF // (128 * SUB)
    CHUNKS = ((0, 364), (364, 362), (726, 362))
    UNITS = SUB * len(CHUNKS)
    DOWN_AFTER = (0, 3, 4, 4, 4, 3)
    SHARE = (L - DEC_T) // ((GROUPS - 1) * UNITS)
    gu_v = A["w_gu"][0].rearrange("(q k p) n -> q p k n", q=2, p=128)
    keep = lambda a: a[0].rearrange("b l h d -> b (l h d)")
    with ExitStack() as ctx:
        sb = lambda n, s, d=F32: ctx.enter_context(nc.sbuf_tensor(n, s, d))
        ps = lambda n, s: ctx.enter_context(nc.psum_tensor(n, s, F32))
        sem = lambda n: nc.alloc_semaphore("p6_" + n)
        raw = sb("raw6", [128, 2, D_MODEL])
        gu_hi, gu_lo = (sb(n, [128, SUB, KT, 2, 128], F32R) for n in ("gu_hi", "gu_lo"))
        wd_hi, wd_lo = (sb(n, [128, SUB, D_MODEL], F32R) for n in ("wd_hi", "wd_lo"))
        s_t, f_t = sb("s_t", [128, 364]), sb("f_t", [128, 364])
        f_hi, f_lo = (sb(n, [128, 2, SUB, NTOK], F32R) for n in ("f_hi", "f_lo"))
        gate_ps = [ps(f"gate_ps{i}", [128, 512]) for i in range(2)]
        up_ps = [ps(f"up_ps{i}", [128, 512]) for i in range(2)]
        d_ps = [ps(f"d_ps{i}", [128, 512]) for i in range(4)]
        landed = [sem(f"landed{i}") for i in range(2)]
        (hi_ready, lo_ready, unit_done, silu_ready, f_ready, f_hi_ready, f_lo_ready, down_done, added, zeroed,
         kept) = map(sem, ("hi_ready", "lo_ready", "unit_done", "silu_ready", "f_ready", "f_hi_ready", "f_lo_ready",
                           "down_done", "added", "zeroed", "kept"))
        piece = lambda g, e, p: 6 * g + 2 * e + p
        raw_gu = lambda p: raw[:, p, :].rearrange("q (k h n) -> q k h n", k=HK, h=2)

        def over_steps(eng, step):
            step(0, 0)
            with eng.Fori(0, (GROUPS - 3) // 2) as i:
                step(2 * i + 1, 1)
                step(2 * i + 2, 0)
            step(GROUPS - 2, 1)
            step(GROUPS - 1, 0)
            step(GROUPS, 1)

        with nc.Block() as block:

            @block.sync
            def _(sp):
                def load_gu(g, e, tile):
                    for p in range(2):
                        if not known(g, 0) or e > 0:
                            sp.wait_ge(lo_ready, piece(g, e, p) - 1)
                        for h in range(2):
                            sp.dma_start(raw_gu(p)[:, :, h, :],
                                         gu_v[p][:, :, bass.ds(tile * 128 + h * D_FF, 128)]).then_inc(landed[p], 16)

                def load_down(g, e, group):
                    for p in range(2):
                        sp.wait_ge(lo_ready, piece(g, e, p) - 1)
                        sp.dma_start(raw[:, p, :], A["w_down"][0, bass.ds((group * 2 + p) * 128, 128), :]).then_inc(landed[p], 16)

                def step(g, par):
                    if known(g, GROUPS):
                        load_down(GROUPS - 1, 2, GROUPS - 1)
                        return
                    if not known(g, 0):
                        load_down(g, 0, g - 1)
                    load_gu(g, 1, 2 * g + 1)
                    if not known(g, GROUPS - 1):
                        load_gu(g, 2, 2 * g + 2)

                load_gu(0, 0, 0)
                over_steps(sp, step)

            @block.gpsimd
            def _(pool):
                def copy_out(out, a):
                    pool.dma_start(out, a).then_inc(kept, 16)

                def step(g, par):
                    if known(g, GROUPS):
                        return
                    for u in range(UNITS):
                        if not known(g, 0):
                            rows = bass.ds(((g - 1) * UNITS + u) * (SHARE * WID), SHARE * WID)
                            past = bass.ds(((g - 1) * UNITS + u) * (SHARE * WID) + DEC_T * WID, SHARE * WID)
                            copy_out(keep(A["ks_sample"])[:, rows], keep(A["cache_k_win"])[:, past])
                            copy_out(keep(A["vs_sample"])[:, rows], keep(A["cache_v_win"])[:, past])
                        c, n = CHUNKS[u % 3]
                        cut = (slice(None), par, u // 3, slice(c, c + n))
                        pool.wait_ge(f_hi_ready, UNITS * g + u + 1)
                        pool.tensor_tensor(f_lo[cut], f_t[:, 0:n], f_hi[cut].bitcast(F32), ALU.subtract).then_inc(f_lo_ready, 1)

                pool.memset(acc[:, :, :], 0.0).then_inc(zeroed, 1)
                for n, (p_out, s_out) in enumerate((("k_prompt", "ks_sample"), ("v_prompt", "vs_sample"))):
                    cols = slice((5 + n) * WID, (6 + n) * WID)
                    copy_out(A[p_out][0, 0].rearrange("s h d -> s (h d)"), z[0:SEQ, cols])
                    copy_out(A[s_out][0, :, L - DEC_T:L].rearrange("b t h d -> b t (h d)"),
                             z[SEQ:NTOK, cols].rearrange("(b t) c -> b t c", b=DEC_B))
                over_steps(pool, step)
                pool.wait_ge(kept, 16 * (4 + 2 * (GROUPS - 1) * UNITS))

            @block.scalar
            def _(act):
                def split(dst, src, out, lap):
                    for p in dst:
                        act.wait_ge(landed[p], lap)
                        act.copy(out(p), src(p)).then_inc(hi_ready, 1)

                gu = lambda s: lambda p: gu_hi[:, s, HK * p:HK * p + HK]
                raw_wd = lambda p: raw[:, p, :]
                wd = lambda p: wd_hi[:, p, :]

                def unit(g, par, u):
                    c, n = CHUNKS[u % 3]
                    act.wait_ge(unit_done, UNITS * g + u + 1)
                    if not (known(g, 0) and u == 0):
                        act.wait_ge(f_ready, UNITS * g + u)
                    act.activation(s_t[:, 0:n], gate_ps[u % 2][:, 0:n], ACT.Silu).then_inc(silu_ready, 1)
                    act.wait_ge(f_ready, UNITS * g + u + 1)
                    act.copy(f_hi[:, par, u // 3, c:c + n], f_t[:, 0:n]).then_inc(f_hi_ready, 1)

                def step(g, par):
                    if known(g, GROUPS):
                        act.wait_ge(down_done, GROUP_D * g)
                        split((0, 1), raw_wd, wd, 80 * g)
                        return
                    if not known(g, 0):
                        act.wait_ge(down_done, GROUP_D * g)
                        split((0, 1), raw_wd, wd, 80 * g + 32)
                    unit(g, par, 0)
                    if not known(g, 0):
                        act.wait_ge(unit_done, UNITS * g)
                    split((0, 1), raw_gu, gu(1), 80 * g + 64)
                    unit(g, par, 1)
                    unit(g, par, 2)
                    for u in (3, 4):
                        if not known(g, GROUPS - 1):
                            act.wait_ge(unit_done, UNITS * g + 3)
                            split((u - 3,), raw_gu, gu(0), 80 * g + 96)
                        unit(g, par, u)
                    unit(g, par, 5)

                split((0, 1), raw_gu, gu(0), 32)
                over_steps(act, step)

            @block.vector
            def _(dve):
                dve.sem_inc(added, 4)

                def split(n, dst, src, hi, lo):
                    for p in dst:
                        dve.wait_ge(hi_ready, n + p + 1)
                        dve.tensor_tensor(lo(p), src(p), hi(p).bitcast(F32), ALU.subtract).then_inc(lo_ready, 1)

                raw_wd = lambda p: raw[:, p, :]
                wd = lambda t: lambda p: t[:, p, :]
                gu = lambda t, s: lambda p: t[:, s, HK * p:HK * p + HK]

                def unit(g, u):
                    c, n = CHUNKS[u % 3]
                    dve.wait_ge(silu_ready, UNITS * g + u + 1)
                    if not (known(g, 0) and u == 0):
                        dve.wait_ge(f_lo_ready, UNITS * g + u)
                    dve.tensor_tensor(f_t[:, 0:n], s_t[:, 0:n], up_ps[u % 2][:, 0:n], ALU.mult).then_inc(f_ready, 1)

                def add(g, par, first, count):
                    for j in range(first, first + count):
                        lo = 64 if j // 2 == PT else 0
                        cut = (slice(lo, 128), j // 2, slice(j % 2 * 512, j % 2 * 512 + 512))
                        dve.wait_ge(down_done, GROUP_D * g + j + 1)
                        dve.tensor_tensor(acc[cut], acc[cut], d_ps[(2 * (1 - par) + j) % 4][lo:128, :], ALU.add).then_inc(added, 1)

                def step(g, par):
                    if known(g, GROUPS):
                        split(piece(GROUPS - 1, 2, 0), (0, 1), raw_wd, wd(wd_hi), wd(wd_lo))
                        add(g, par, 0, GROUP_D)
                        return
                    if not known(g, 0):
                        split(piece(g, 0, 0), (0, 1), raw_wd, wd(wd_hi), wd(wd_lo))
                    unit(g, 0)
                    split(piece(g, 1, 0), (0, 1), raw_gu, gu(gu_hi, 1), gu(gu_lo, 1))
                    first = 0
                    for u in range(1, UNITS):
                        if u in (3, 4) and not known(g, GROUPS - 1):
                            split(piece(g, 2, 0), (u - 3,), raw_gu, gu(gu_hi, 0), gu(gu_lo, 0))
                        unit(g, u)
                        if not known(g, 0):
                            add(g, par, first, DOWN_AFTER[u])
                            first += DOWN_AFTER[u]

                split(0, (0, 1), raw_gu, gu(gu_hi, 0), gu(gu_lo, 0))
                dve.wait_ge(zeroed, 1)
                over_steps(dve, step)

            @block.tensor
            def _(pe):
                pe.sem_inc(down_done, GROUP_D)

                def unit(g, u):
                    s, (c, n) = u // 3, CHUNKS[u % 3]
                    if not known(g, 0) or u >= 2:
                        pe.wait_ge(f_ready, UNITS * g + u - 1)
                    for h, bank in enumerate((gate_ps, up_ps)):
                        for k in range(KT):
                            for m, (w, x) in enumerate(((gu_hi, h_hi), (gu_hi, h_lo), (gu_lo, h_hi))):
                                mm = pe.matmul(bank[u % 2][:, 0:n], w[:, s, k, h, :], x[:, k, c:c + n],
                                               start=(k, m) == (0, 0), stop=(k, m) == (KT - 1, 2))
                    mm.then_inc(unit_done, 1)

                def down(g, par, first, count):
                    for j in range(first, first + count):
                        end, col = min(j // 2 * 128 + 128, NTOK), j % 2 * 512
                        pe.wait_ge(added, GROUP_D * (g - 1) + j + 1)
                        for s in range(SUB):
                            for m, (x, w) in enumerate(((f_hi, wd_hi), (f_hi, wd_lo), (f_lo, wd_hi))):
                                mm = pe.matmul(d_ps[(2 * (1 - par) + j) % 4][:, :], x[:, 1 - par, s, end - 128:end],
                                               w[:, s, col:col + 512], start=(s, m) == (0, 0), stop=(s, m) == (SUB - 1, 2))
                        mm.then_inc(down_done, 1)

                def step(g, par):
                    if known(g, GROUPS):
                        pe.wait_ge(lo_ready, piece(GROUPS - 1, 2, 2))
                        pe.wait_ge(f_lo_ready, UNITS * g)
                        down(g, par, 0, GROUP_D)
                        return
                    first = 0
                    for u in range(UNITS):
                        if u == 0:
                            pe.wait_ge(lo_ready, 2 if known(g, 0) else piece(g, 0, 0))
                        if u == 3:
                            pe.wait_ge(lo_ready, piece(g, 2, 0))
                        unit(g, u)
                        if not known(g, 0) and DOWN_AFTER[u]:
                            if first == 0:
                                pe.wait_ge(lo_ready, piece(g, 1, 0))
                                pe.wait_ge(f_lo_ready, UNITS * g)
                            down(g, par, first, DOWN_AFTER[u])
                            first += DOWN_AFTER[u]

                over_steps(pe, step)


def final_norm(nc, A, x_mid, acc):
    with ExitStack() as ctx:
        sb = lambda n, s, d=F32: ctx.enter_context(nc.sbuf_tensor(n, s, d))
        sem = lambda n: nc.alloc_semaphore("p7_" + n)
        x_m, y = sb("x_m7", [128, 3, D_MODEL]), sb("y7", [128, 3, D_MODEL])
        scratch, g_post = sb("scratch7", [128, D_MODEL]), sb("g_post7", [128, D_MODEL])
        stat, mhalf = sb("stat7", [128, 3, TT]), sb("mhalf7", [128, 1])
        x_landed, y_stored = ([sem(f"{n}{i}") for i in range(3)] for n in ("x_landed", "y_stored"))
        g_landed, half_set, squared, mean_ready, rstd_ready, scaled, y_ready = map(
            sem, ("g_landed", "half_set", "squared", "mean_ready", "rstd_ready", "scaled", "y_ready"))
        rows = lambda t: slice(128 - tile_rows(t), 128)

        with nc.Block() as block:

            @block.sync
            def _(sp):
                sp.dma_start(g_post[:, :], A["g_post_ffn"][0].partition_broadcast(128)).then_inc(g_landed, 16)

                def store(t):
                    sp.wait_ge(y_ready, t + 1)
                    out = (A["y_prompt"][0, t * 128:t * 128 + 128, :] if t < PT
                           else A["y_sample"].rearrange("b t d -> (b t) d"))
                    sp.dma_start(out, y[rows(t), t % 3, :]).then_inc(y_stored[t % 3], 16)

                for t in range(TT):
                    if t >= 3:
                        store(t - 3)
                    sp.dma_start(x_m[rows(t), t % 3, :],
                                 x_mid[t * 128:t * 128 + tile_rows(t), :]).then_inc(x_landed[t % 3], 16)
                for t in range(TT - 3, TT):
                    store(t)
                for i in range(3):
                    sp.wait_ge(y_stored[i], 48)

            @block.gpsimd
            def _(pool):
                pool.memset(mhalf[:, :], -0.5).then_inc(half_set, 1)
                pool.wait_ge(half_set, 1)
                for t in range(TT):
                    if t == PT:
                        pool.wait_ge(rstd_ready, t)
                    pool.wait_ge(mean_ready, t + 1)
                    pool.tensor_tensor(stat[rows(t), 2, t:t + 1], stat[rows(t), 1, t:t + 1], mhalf[rows(t), :],
                                       ALU.pow).then_inc(rstd_ready, 1)

            @block.scalar
            def _(act):
                for t in range(TT):
                    if t >= 1:
                        act.wait_ge(squared, t)
                    act.activation(scratch[rows(t), :], acc[rows(t), t, :], ACT.Square,
                                   accum_out=stat[rows(t), 0, t:t + 1]).then_inc(squared, 1)

            @block.vector
            def _(dve):
                def mean(t):
                    dve.wait_ge(squared, t + 1)
                    dve.tensor_scalar(stat[rows(t), 1, t:t + 1], stat[rows(t), 0, t:t + 1], 1.0 / D_MODEL, EPS,
                                      ALU.mult, ALU.add).then_inc(mean_ready, 1)

                dve.wait_ge(g_landed, 16)
                mean(0)
                for t in range(TT):
                    if t + 1 < TT:
                        mean(t + 1)
                    dve.wait_ge(rstd_ready, t + 1)
                    if t >= 3:
                        dve.wait_ge(y_stored[t % 3], 16 * (t // 3))
                    dve.scalar_tensor_tensor(y[rows(t), t % 3, :], acc[rows(t), t, :], stat[rows(t), 2, t:t + 1],
                                             g_post[rows(t), :], ALU.mult, ALU.mult).then_inc(scaled, 1)
                    dve.wait_ge(scaled, t + 1)
                    dve.wait_ge(x_landed[t % 3], 16 * (t // 3) + 16)
                    dve.tensor_tensor(y[rows(t), t % 3, :], y[rows(t), t % 3, :], x_m[rows(t), t % 3, :],
                                      ALU.add).then_inc(y_ready, 1)


OUTPUTS = {
    "y_prompt": (1, SEQ, D_MODEL), "y_sample": (DEC_B, DEC_T, D_MODEL),
    "state_p": (1, 1, NH, HD, HD), "k_prompt": (1, 1, SEQ, NH, HD), "v_prompt": (1, 1, SEQ, NH, HD),
    "state_s": (1, DEC_B, NH, HD, HD), "ks_sample": (1, DEC_B, L, NH, HD), "vs_sample": (1, DEC_B, L, NH, HD),
}


def hymba_layer(nc, A):
    scratch = lambda n, s: nc.dram_tensor(n, s, F32, kind="Internal").ap()
    z, mix = scratch("z_scratch", [NTOK, ZC]), scratch("mix_scratch", [NTOK, D_MODEL])
    x_mid, tab = scratch("x_mid_scratch", [NTOK, D_MODEL]), scratch("tab_scratch", [NH, 128, TABW])
    with nc.sbuf_tensor("h_hi", [128, KT, NTOK], F32R) as h_hi, \
         nc.sbuf_tensor("h_lo", [128, KT, NTOK], F32R) as h_lo:
        with nc.sbuf_tensor("ident", [128, 128], F32) as ident:
            with nc.cleanup_on_exit():
                in_projection(nc, A, z, h_hi, h_lo, ident)
            retention(nc, A, z, mix, ident, A["state_p"][0, 0], A["state_s"][0])
            with nc.sbuf_tensor("bias_s", [128, STILES, NH, DEC_T], F32) as bias_s:
                distance_tables(nc, A, tab, bias_s)
                prompt_attention(nc, A, z, mix, tab, ident)
                sample_attention(nc, A, z, mix, bias_s, ident)
            out_projection(nc, A, mix, x_mid, h_hi, h_lo, ident)
        with nc.sbuf_tensor("acc", [128, TT, D_MODEL], F32) as acc:
            ffn(nc, A, z, h_hi, h_lo, acc)
            final_norm(nc, A, x_mid, acc)


def kernel(**inputs):
    import concourse.bacc as bacc
    from concourse.bass_utils import run_bass_kernel_spmd

    nc = bacc.Bacc("TRN2", target_bir_lowering=False, num_devices=1)
    arrays = {n: np.ascontiguousarray(a) for n, a in inputs.items()}
    arrays.update(shape_constants())
    A = {n: nc.dram_tensor(n, a.shape, mybir.dt.from_np(a.dtype), kind="ExternalInput").ap() for n, a in arrays.items()}
    for n, shape in OUTPUTS.items():
        A[n] = nc.dram_tensor(n, shape, F32, kind="ExternalOutput").ap()
    hymba_layer(nc, A)
    got = run_bass_kernel_spmd(nc, [arrays], core_ids=[0])
    return tuple(got.results[0][n] for n in OUTPUTS)
```

```python
import numpy as np
from contextlib import ExitStack

import concourse.bass as bass
from concourse import mybir

F32 = mybir.dt.float32
F32R = mybir.dt.float32r
ALU = mybir.AluOpType
ACT = mybir.ActivationFunctionType
AXX = mybir.AxisListType.X

D_MODEL, SEQ, DEC_B, DEC_T, PAST = 1024, 1024, 8, 8, 8192
HD, NH, NPAIR = 64, 8, 4
WID = NH * HD
ZC = 7 * WID
L = 2048
D_FF = 2816
NS = DEC_B * DEC_T
NTOK = SEQ + NS
KT = D_MODEL // 128
PT = SEQ // 128
TT = PT + 1
EPS, GN_EPS = 1e-6, 1e-5
NEG = -1e30
N_BUCKETS, MAX_DISTANCE = 32, 2048
WIDE, REST, STILES = 8, 1536, 11
TABW = 1152
TABC = 896 + 127


def t5_bucket(dist):
    me = N_BUCKETS // 2
    d = np.maximum(dist, 1).astype(np.float32)
    big = me + (np.log(d / np.float32(me)) / np.float32(np.log(MAX_DISTANCE / me))
                * np.float32(N_BUCKETS - me)).astype(np.int32)
    return np.where(dist < me, dist, np.minimum(big, N_BUCKETS - 1))


def pattern_rows(dist):
    d = np.asarray(dist)
    ok = d >= 0
    c = ((d <= 128).astype(int) + ((d <= 512) & (d % 4 == 0)) + ((d <= 2048) & (d % 16 == 0))) * ok
    rows = np.zeros((N_BUCKETS + 1,) + d.shape, np.float32)
    b = t5_bucket(np.maximum(d, 0))
    for n in range(N_BUCKETS):
        rows[n] = (b == n) & (c > 0)
    rows[N_BUCKETS] = np.where(c > 0, np.log(np.maximum(c, 1)), NEG)
    return rows


def shape_constants():
    c = {}
    f64 = np.float64
    inv = (10000.0 ** (-np.arange(0, HD, 2) / HD)).astype(np.float32)
    pos = np.zeros((TT, 128), np.float32)
    pos[:PT] = np.arange(SEQ).reshape(PT, 128)
    pos[PT, :NS] = PAST + np.arange(NS) % DEC_T
    ang = (pos[:, :, None] * inv[None, None, :]).astype(np.float32).astype(f64)
    rope = np.zeros((128, TT, 2, HD), np.float32)
    rope[:, :, 0] = np.concatenate([np.cos(ang), np.cos(ang)], -1).transpose(1, 0, 2)
    rope[:, :, 1] = np.concatenate([-np.sin(ang), np.sin(ang)], -1).transpose(1, 0, 2)
    c["c_rope"] = rope
    lg = np.log1p(-np.exp2(-5.0 - np.arange(NH))).astype(f64)
    i = np.arange(128)
    rel = i[None, :] - i[:, None]
    dec = np.where(rel[None] >= 0, np.exp(np.maximum(rel, 0)[None] * lg[:, None, None]), 0) / 8
    c["c_decay"] = dec.transpose(1, 0, 2).astype(np.float32)
    cross = np.exp((i + 1)[None, :] * lg[:, None])
    pairs = np.repeat(lg.reshape(NPAIR, 2).T, HD, 0)
    c["c_cross"] = np.exp(pairs[:, :, None] * (i + 1)).astype(np.float32)
    c["c_kdec"] = (np.exp((127 - i)[:, None] * lg[None]) / 8).astype(np.float32)
    c["c_chunk"] = np.exp(128 * pairs).astype(np.float32)
    n = np.arange(NS)
    same = (n[:, None] // DEC_T == n[None, :] // DEC_T)
    rs = n[None, :] - n[:, None]
    c["c_decay_s"] = (np.where(same & (rs >= 0), np.exp(np.maximum(rs, 0)[None] * lg[:, None, None]), 0)
                      / 8).transpose(1, 0, 2).astype(np.float32)
    c["c_cross_s"] = np.exp(pairs[:, :, None] * (n % DEC_T + 1)).astype(np.float32)
    c["c_kdec_s"] = (np.exp((DEC_T - 1 - n % DEC_T)[:, None] * lg[None]) / 8).astype(np.float32)
    c["c_chunk_s"] = np.exp(DEC_T * pairs).astype(np.float32)
    c["c_bmask"] = (n[:, None] // DEC_T == np.arange(DEC_B)[None]).astype(np.float32)
    c["c_ident"] = np.eye(128, dtype=np.float32)
    c["c_dist_p"] = pattern_rows(TABC - np.arange(TABW))
    p = np.arange(128)
    rows = [16 * p + j for j in range(WIDE)]
    rows += [REST + 16 * (p // 4) + 8 + 2 * (p % 4) + j for j in range(2)]
    rows += [np.where(p < DEC_T, L + p, 10 * L)]
    rows = np.stack(rows)
    dist = L + np.arange(DEC_T)[None, :, None] - rows[:, None, :]
    c["c_dist_s"] = pattern_rows(dist.transpose(1, 0, 2))
    row = np.arange(128)
    c["c_own"] = (row[:, None] % (NH * DEC_T) // DEC_T == np.arange(WID)[None] // HD).astype(np.float32)
    c["c_sum_t"] = (row[:, None] % DEC_T == row[None]).astype(np.float32)
    return {k: np.ascontiguousarray(v) for k, v in c.items()}


def tile_rows(t):
    return 128 if t < PT else NS


def spread(ap, shape):
    return ap.unsqueeze(2).broadcast_to(shape)


def known(t, value):
    return isinstance(t, int) and t == value


def in_projection(nc, A, z, h_hi, h_lo, ident):
    GROUPS = ZC // WID
    HK = KT // 2
    w_v = A["w_in"][0].rearrange("(q k p) n -> q p k n", q=2, p=128)
    x_v = [A["x_prompt"][0, t * 128:(t + 1) * 128, :] for t in range(PT)]
    x_v.append(A["x_sample"].rearrange("b t d -> (b t) d"))
    with ExitStack() as ctx:
        sb = lambda n, s, d=F32: ctx.enter_context(nc.sbuf_tensor(n, s, d))
        ps = lambda n, s: ctx.enter_context(nc.psum_tensor(n, s, F32))
        sem = lambda n: nc.alloc_semaphore("p1_" + n)
        w_raw = sb("w_raw", [128, 2, HK, WID])
        w_hi, w_lo = sb("w_hi", [128, 2, KT, WID], F32R), sb("w_lo", [128, 2, KT, WID], F32R)
        xt = sb("xt", [128, 2, D_MODEL])
        xn = sb("xn", [128, 2, D_MODEL])
        hg = sb("hg", [128, 2, HK, 128])
        g_rows, gT = sb("g_rows", [KT, 128]), sb("gT", [128, KT])
        stat, mhalf = sb("stat", [128, 3, TT]), sb("mhalf", [128, 1])
        z_out = sb("z_out", [128, 3, WID])
        t_ps = [ps(f"t_ps{i}", [128, HK, 128]) for i in range(2)]
        z_ps = [ps(f"z_ps{i}", [128, WID]) for i in range(3)]
        x_landed = [sem(f"x_landed{i}") for i in range(2)]
        w_landed = [sem(f"w_landed{i}") for i in range(2)]
        g_landed, i_landed, g_turned, g_ready = map(sem, ("g_landed", "i_landed", "g_turned", "g_ready"))
        half_set, squared, mean_ready, rstd_ready, xn_ready = map(
            sem, ("half_set", "squared", "mean_ready", "rstd_ready", "xn_ready"))
        turned, hg_ready, hi_ready, lo_ready = map(sem, ("turned", "hg_ready", "hi_ready", "lo_ready"))
        w_hi_ready, w_lo_ready = sem("w_hi_ready"), sem("w_lo_ready")
        z_done, z_evac = sem("z_done"), sem("z_evac")
        z_stored = [sem(f"z_stored{i}") for i in range(3)]

        with nc.Block() as block:

            @block.sync
            def _(sp):
                def load_weights(c):
                    for q in range(2):
                        if not isinstance(c, int) or c > 0:
                            sp.wait_ge(w_lo_ready, 2 * c + q - 1)
                        sp.dma_start(w_raw[:, q], w_v[q][:, :, bass.ds(c * WID, WID)]).then_inc(w_landed[q], 16)

                def store_z(c, t):
                    n = tile_rows(t)
                    sp.wait_ge(z_evac, TT * c + t + 1)
                    sp.dma_start(z[t * 128:t * 128 + n, bass.ds(c * WID, WID)],
                                 z_out[128 - n:128, t % 3, :]).then_inc(z_stored[t % 3], 16)

                sp.dma_start(xt[:, 0, :], x_v[0]).then_inc(x_landed[0], 16)
                sp.dma_start(ident[:, :], A["c_ident"]).then_inc(i_landed, 16)
                sp.dma_start(g_rows[:, :], A["g_pre_mix"][0].rearrange("(k p) -> k p", p=128)).then_inc(g_landed, 16)
                sp.dma_start(xt[:, 1, :], x_v[1]).then_inc(x_landed[1], 16)
                load_weights(0)
                for t in range(2, TT):
                    sp.wait_ge(xn_ready, t - 1)
                    sp.dma_start(xt[0:tile_rows(t), t % 2, :], x_v[t]).then_inc(x_landed[t % 2], 16)
                load_weights(1)
                for t in range(TT):
                    store_z(0, t)
                with sp.Fori(1, GROUPS - 1) as c:
                    load_weights(c + 1)
                    for t in range(TT):
                        store_z(c, t)
                for t in range(TT):
                    store_z(GROUPS - 1, t)
                for m in range(3):
                    sp.wait_ge(z_stored[m], 16 * 3 * GROUPS)

            @block.gpsimd
            def _(pool):
                pool.memset(mhalf[:, :], -0.5).then_inc(half_set, 1)
                pool.wait_ge(half_set, 1)

                def rstd(t):
                    n = tile_rows(t)
                    pool.wait_ge(mean_ready, t + 1)
                    pool.tensor_tensor(stat[0:n, 2, t:t + 1], stat[0:n, 1, t:t + 1], mhalf[0:n, :],
                                       ALU.pow).then_inc(rstd_ready, 1)

                rstd(0)
                for t in range(TT):
                    if t + 1 < TT:
                        rstd(t + 1)
                    n = tile_rows(t)
                    for q in range(2):
                        pool.wait_ge(hi_ready, 2 * t + q + 1)
                        cut = (slice(None), slice(HK * q, HK * q + HK), slice(t * 128, t * 128 + n))
                        pool.tensor_tensor(h_lo[cut], hg[:, q, :, 0:n], h_hi[cut].bitcast(F32),
                                           ALU.subtract).then_inc(lo_ready, 1)

            @block.scalar
            def _(act):
                def square(t):
                    n = tile_rows(t)
                    act.wait_ge(x_landed[t % 2], 16 * (t // 2 + 1))
                    if t >= 2:
                        act.wait_ge(turned, 2 * (t - 1))
                    act.activation(xn[0:n, t % 2, :], xt[0:n, t % 2, :], ACT.Square,
                                   accum_out=stat[0:n, 0, t:t + 1]).then_inc(squared, 1)

                def split_weights(c, par, q):
                    act.wait_ge(w_landed[q], 16 * c + 16)
                    if not isinstance(c, int) or c >= 2:
                        act.wait_ge(z_done, TT * c - TT)
                    act.copy(w_hi[:, par, HK * q:HK * q + HK, :], w_raw[:, q]).then_inc(w_hi_ready, 1)

                def evacuate(c, t):
                    n = tile_rows(t)
                    act.wait_ge(z_done, TT * c + t + 1)
                    if not isinstance(c, int) or c > 0 or t >= 3:
                        act.wait_ge(z_stored[t % 3], 48 * c + 16 * (t // 3))
                    act.copy(z_out[128 - n:128, t % 3, :], z_ps[t % 3][128 - n:128, :]).then_inc(z_evac, 1)

                def group(c, par, last=False):
                    for t in range(TT):
                        evacuate(c, t)
                        if not last and t in (1, 4):
                            split_weights(c + 1, 1 - par, t // 4)

                square(0)
                square(1)
                split_weights(0, 0, 0)
                split_weights(0, 0, 1)
                for t in range(TT):
                    n = tile_rows(t)
                    for q in range(2):
                        act.wait_ge(hg_ready, 2 * t + q + 1)
                        act.copy(h_hi[:, HK * q:HK * q + HK, t * 128:t * 128 + n],
                                 hg[:, q, :, 0:n]).then_inc(hi_ready, 1)
                    if t + 2 < TT:
                        square(t + 2)
                    if t >= 1:
                        evacuate(0, t - 1)
                    if t in (4, 6):
                        split_weights(1, 1, t // 5)
                evacuate(0, TT - 1)
                with act.Fori(0, (GROUPS - 3) // 2) as i:
                    group(2 * i + 1, 1)
                    group(2 * i + 2, 0)
                group(GROUPS - 2, 1)
                group(GROUPS - 1, 0, last=True)

            @block.vector
            def _(dve):
                def normalise(t):
                    n = tile_rows(t)
                    dve.wait_ge(squared, t + 1)
                    dve.tensor_scalar(stat[0:n, 1, t:t + 1], stat[0:n, 0, t:t + 1], 1.0 / D_MODEL, EPS,
                                      ALU.mult, ALU.add).then_inc(mean_ready, 1)
                    dve.wait_ge(rstd_ready, t + 1)
                    dve.tensor_scalar(xn[0:n, t % 2, :], xt[0:n, t % 2, :], stat[0:n, 2, t:t + 1], None,
                                      ALU.mult).then_inc(xn_ready, 1)

                def split_weights(c, par, q):
                    dve.wait_ge(w_hi_ready, 2 * c + q + 1)
                    cut = (slice(None), par, slice(HK * q, HK * q + HK))
                    dve.tensor_tensor(w_lo[cut], w_raw[:, q], w_hi[cut].bitcast(F32),
                                      ALU.subtract).then_inc(w_lo_ready, 1)

                normalise(0)
                dve.wait_ge(g_turned, 1)
                dve.tensor_copy(gT[:, :], t_ps[1][:, 0, 0:KT]).then_inc(g_ready, 1)
                dve.wait_ge(g_ready, 1)
                for t in range(TT):
                    n = tile_rows(t)
                    if t + 1 < TT:
                        normalise(t + 1)
                    for q in range(2):
                        dve.wait_ge(turned, 2 * t + q + 1)
                        if t >= 1:
                            dve.wait_ge(lo_ready, 2 * t + q - 1)
                        dve.tensor_tensor(hg[:, q, :, 0:n], t_ps[q][:, :, 0:n],
                                          spread(gT[:, HK * q:HK * q + HK], [128, HK, n]),
                                          ALU.mult).then_inc(hg_ready, 1)
                    if t == 0:
                        split_weights(0, 0, 0)
                        split_weights(0, 0, 1)
                split_weights(1, 1, 0)
                split_weights(1, 1, 1)
                with dve.Fori(0, (GROUPS - 3) // 2) as i:
                    for par in (0, 1):
                        for q in range(2):
                            split_weights(2 * i + 2 + par, par, q)
                for q in range(2):
                    split_weights(GROUPS - 1, 0, q)

            @block.tensor
            def _(pe):
                def turn(t):
                    n = tile_rows(t)
                    pe.wait_ge(xn_ready, t + 1)
                    for q in range(2):
                        if t >= 1:
                            pe.wait_ge(hg_ready, 2 * t + q - 1)
                        for k in range(HK):
                            col = (HK * q + k) * 128
                            mm = pe.transpose(t_ps[q][:, k, 0:n], xn[0:n, t % 2, col:col + 128], ident[0:n, 0:n])
                        mm.then_inc(turned, 1)

                def project(c, par, t):
                    if not isinstance(c, int) or c > 0 or t >= 3:
                        pe.wait_ge(z_evac, TT * c + t - 2)
                    end = t * 128 + tile_rows(t)
                    first, last = (0, 0), (KT - 1, 2)
                    for k in range(KT):
                        for n, (x, w) in enumerate(((h_hi, w_hi), (h_hi, w_lo), (h_lo, w_hi))):
                            mm = pe.matmul(z_ps[t % 3][:, :], x[:, k, end - 128:end], w[:, par, k, :],
                                           start=(k, n) == first, stop=(k, n) == last)
                    mm.then_inc(z_done, 1)

                pe.wait_ge(i_landed, 16)
                pe.wait_ge(g_landed, 16)
                pe.transpose(t_ps[1][:, 0, 0:KT], g_rows[:, :], ident[0:KT, 0:KT]).then_inc(g_turned, 1)
                pe.wait_ge(g_ready, 1)
                turn(0)
                for t in range(TT):
                    if t + 1 < TT:
                        turn(t + 1)
                    pe.wait_ge(lo_ready, 2 * t + 2)
                    if t == 0:
                        pe.wait_ge(w_lo_ready, 2)
                    project(0, 0, t)
                with pe.Fori(0, (GROUPS - 1) // 2) as i:
                    for par in (1, 0):
                        c = 2 * i + 2 - par
                        pe.wait_ge(w_lo_ready, 2 * c + 2)
                        for t in range(TT):
                            project(c, par, t)


def by(t):
    return t + 2


def diagonal(t4, par):
    return t4[HD * par:HD * par + HD, :, HD * par:HD * par + HD]


def retention(nc, A, z, mix, ident, state_p, state_s):
    with ExitStack() as ctx:
        sb = lambda n, s, d=F32: ctx.enter_context(nc.sbuf_tensor(n, s, d))
        ps = lambda n, s: ctx.enter_context(nc.psum_tensor(n, s, F32))
        sem = lambda n: nc.alloc_semaphore("p2_" + n)
        zr = sb("zr", [128, 2, 4, NH, HD])
        rope = sb("rope", [128, TT, 2, HD])
        decay, cross = sb("decay", [128, NH, 128]), sb("cross", [128, NPAIR, 128])
        kdec, chunk = sb("kdec", [128, NH]), sb("chunk", [128, NPAIR])
        decay_s, cross_s = sb("decay_s", [NS, NH, NS]), sb("cross_s", [128, NPAIR, NS])
        kdec_s, chunk_s = sb("kdec_s", [NS, NH]), sb("chunk_s", [128, NPAIR])
        bmask = sb("bmask", [NS, DEC_B])
        g_row = sb("g_row", [128, WID])
        t1, t2 = sb("t1", [128, 2 * NH, HD]), sb("t2", [128, 2 * NH, HD])
        qk = sb("qk", [128, 2 * NH, HD])
        qT = sb("qT2", [128, NPAIR, 128])
        kT = sb("kT2", [128, 2, NPAIR, 128])
        qd = sb("qd", [128, NPAIR, 128])
        kd = sb("kd", [128, NH, HD])
        inT = sb("inT", [128, 2, NPAIR, 128])
        S = sb("S", [128, 2, NPAIR, 128])
        Sg = sb("Sg", [128, NPAIR, 128])
        swish, gate = sb("swish", [128, WID]), sb("gate", [128, WID])
        oc, sq, on = (sb(n, [128, NH, HD]) for n in ("oc", "sq", "on"))
        stat, mhalf = sb("stat2", [128, 5, NH]), sb("mhalf2", [128, NH])
        mixr = sb("mixr", [128, 2, WID])
        S_in = sb("S_in", [128, DEC_B, NPAIR, 128])
        S_out = sb("S_out", [128, DEC_B, NPAIR, HD])
        qdm = sb("qdm", [128, NPAIR, DEC_B * NS])
        vm = sb("vm", [NS, DEC_B, WID])
        qk_ps = [ps(f"qk_ps{i}", [128, NPAIR, 128]) for i in range(2)]
        in_ps = [ps(f"in_ps{i}", [128, NPAIR, 128]) for i in range(2)]
        o_ps, su_ps = ps("o_ps", [128, NH, HD]), ps("su_ps", [128, NPAIR, 128])

        qk_landed, vg_landed = ([sem(f"{n}_landed{i}") for i in range(2)] for n in ("qk", "vg"))
        rope_landed, tab_landed, state_landed = map(sem, ("rope_landed", "tab_landed", "state_landed"))
        names = ("t1_ready", "qk_ready", "qk_turned", "qkT_ready", "qd_ready", "kd_ready", "inner_done",
                 "inT_ready", "update_done", "S_ready", "Sg_ready", "o_done", "swish_ready", "gate_ready",
                 "oc_ready", "sq_ready", "var_ready", "rstd_ready", "on_ready", "mix_ready")
        (t1_ready, qk_ready, qk_turned, qkT_ready, qd_ready, kd_ready, inner_done, inT_ready, update_done,
         S_ready, Sg_ready, o_done, swish_ready, gate_ready, oc_ready, sq_ready, var_ready, rstd_ready,
         on_ready, mix_ready) = map(sem, names)
        cleared, dve_step, vm_ready, sout_ready = map(sem, ("cleared", "dve_step", "vm_ready", "sout_ready"))
        mix_stored = [sem(f"mix_stored{i}") for i in range(2)]
        state_stored = sem("state_stored")
        TABS, SAMPLE = 10, PT

        def over_tiles(eng, step):
            step(0, 0)
            with eng.Fori(0, PT // 2 - 1) as i:
                step(2 * i + 1, 1, i)
                step(2 * i + 2, 0, i)
            step(PT - 1, 1, PT // 2 - 1)

        def lap(t, par, i):
            return 16 if known(t, 0) else 16 * i + 32 - 16 * par

        def next_lap(t, i):
            return 16 if known(t, 0) else 16 * i + 32

        def one_sequence(eng, b):
            shape = [NS, b.stop - b.start, WID]
            eng.wait_ge(vg_landed[0], 16 * PT // 2 + 16)
            eng.tensor_tensor(vm[:, b, :], zr[0:NS, 0, 2].rearrange("p h d -> p (h d)").unsqueeze(1).broadcast_to(shape),
                              spread(bmask[:, b], shape), ALU.mult).then_inc(vm_ready, 1)

        with nc.Block() as block:

            @block.sync
            def _(sp):
                def load_qk(t, par, rows=128):
                    sp.dma_start(zr[0:rows, par, 0:2].rearrange("p a h d -> p (a h d)"),
                                 z[bass.ds(t * 128, rows), 0:2 * WID]).then_inc(qk_landed[par], 16)

                def load_vg(t, par, rows=128):
                    sp.dma_start(zr[0:rows, par, 2:4].rearrange("p a h d -> p (a h d)"),
                                 z[bass.ds(t * 128, rows), 2 * WID:4 * WID]).then_inc(vg_landed[par], 16)

                def store(t, par, rows=128):
                    sp.wait_ge(mix_ready, by(t))
                    sp.dma_start(mix[bass.ds(t * 128, rows), 0:WID], mixr[0:rows, par, :]).then_inc(mix_stored[par], 16)

                load_qk(0, 0)
                sp.dma_start(rope[:, :, :, :], A["c_rope"]).then_inc(rope_landed, 16)
                for dst, name in ((kdec, "c_kdec"), (cross, "c_cross"), (decay, "c_decay"), (chunk, "c_chunk"),
                                  (decay_s, "c_decay_s"), (cross_s, "c_cross_s"), (kdec_s, "c_kdec_s"),
                                  (chunk_s, "c_chunk_s"), (bmask, "c_bmask")):
                    sp.dma_start(dst[:], A[name]).then_inc(tab_landed, 16)
                sp.dma_start(g_row[:, :], A["g_ret"][0].rearrange("h d -> (h d)").partition_broadcast(128)).then_inc(tab_landed, 16)
                load_qk(1, 1)
                load_vg(0, 0)
                load_vg(1, 1)
                sp.wait_ge(cleared, 5)
                for par in range(2):
                    sp.dma_start(S_in[HD * par:HD * par + HD, :, :, HD * par:HD * par + HD],
                                 A["state_ret"][0].rearrange("b (p r) d e -> r d b p e", r=2)[par]).then_inc(state_landed, 16)

                def step(t, par):
                    if not known(t, PT - 1):
                        sp.wait_ge(qk_ready, by(t))
                        load_qk(t + 2, par, NS if known(t, SAMPLE - 2) else 128)
                    if not known(t, 0):
                        store(t - 1, 1 - par)
                        load_vg(t + 1, 1 - par, NS if known(t, SAMPLE - 1) else 128)

                step(0, 0)
                with sp.Fori(0, PT // 2 - 2) as i:
                    step(2 * i + 1, 1)
                    step(2 * i + 2, 0)
                for t in range(PT - 3, PT):
                    step(t, t % 2)
                store(PT - 1, 1)
                for par in range(2):
                    sp.dma_start(state_p.rearrange("(p r) d e -> r d p e", r=2)[par],
                                 diagonal(S[:, PT % 2], par)).then_inc(state_stored, 16)
                store(SAMPLE, 0, NS)
                sp.wait_ge(sout_ready, 8)
                for par in range(2):
                    sp.dma_start(state_s.rearrange("b (p r) d e -> r d b p e", r=2)[par],
                                 S_out[HD * par:HD * par + HD]).then_inc(state_stored, 16)
                sp.wait_ge(state_stored, 64)
                sp.wait_ge(mix_stored[0], 96)
                sp.wait_ge(mix_stored[1], 80)

            @block.gpsimd
            def _(pool):
                for s in (t1_ready, kd_ready, gate_ready, Sg_ready, rstd_ready, on_ready):
                    pool.sem_inc(s, 1)
                pool.memset(mhalf[:, :], -0.5).then_inc(cleared, 1)
                pool.memset(S[:, :, :, :], 0.0).then_inc(cleared, 1)
                pool.memset(kT[:, :, :, :], 0.0).then_inc(cleared, 1)
                pool.memset(qdm[:, :, :], 0.0).then_inc(cleared, 1)
                pool.memset(S_in[:, :, :, :], 0.0).then_inc(cleared, 1)
                pool.wait_ge(rope_landed, 16)

                def cosine(t, par, lap):
                    pool.wait_ge(qk_landed[par], lap)
                    pool.wait_ge(qk_ready, by(t - 1))
                    pool.tensor_tensor(t1[:, :, :], zr[:, par, 0:2].rearrange("p a h d -> p (a h) d"),
                                       rope[:, t, 0, :].unsqueeze(1).broadcast_to([128, 2 * NH, HD]),
                                       ALU.mult).then_inc(t1_ready, 1)

                def decayed_keys(t, rows, kdec):
                    pool.wait_ge(qk_ready, by(t))
                    pool.wait_ge(update_done, by(t - 1))
                    pool.tensor_tensor(kd[0:rows], qk[0:rows, NH:2 * NH, :], spread(kdec[:, :], [rows, NH, HD]),
                                       ALU.mult).then_inc(kd_ready, 1)

                def decayed_state(t, par):
                    pool.wait_ge(S_ready, by(t - 1))
                    pool.tensor_tensor(Sg[:, :, :], S[:, par], spread(chunk[:, :], [128, NPAIR, 128]),
                                       ALU.mult).then_inc(Sg_ready, 1)

                def gain(t):
                    pool.wait_ge(swish_ready, by(t))
                    pool.wait_ge(mix_ready, by(t - 1))
                    pool.tensor_tensor(gate[:, :], swish[:, :], g_row[:, :], ALU.mult).then_inc(gate_ready, 1)

                def late(t):
                    pool.wait_ge(var_ready, by(t))
                    pool.tensor_tensor(stat[:, 4, :], stat[:, 3, :], mhalf[:, :], ALU.pow).then_inc(rstd_ready, 1)
                    pool.wait_ge(rstd_ready, by(t))
                    pool.tensor_tensor(on[:, :, :], oc[:, :, :], spread(stat[:, 4, :], [128, NH, HD]),
                                       ALU.mult).then_inc(on_ready, 1)

                cosine(0, 0, 16)
                pool.wait_ge(tab_landed, 16 * TABS)

                def step(t, par, i=0):
                    decayed_keys(t, 128, kdec)
                    cosine(t + 1, 1 - par, next_lap(t, i))
                    decayed_state(t, par)
                    if not known(t, 0):
                        gain(t - 1)
                        late(t - 1)

                over_tiles(pool, step)
                decayed_keys(SAMPLE, NS, kdec_s)
                gain(PT - 1)
                late(PT - 1)
                one_sequence(pool, slice(DEC_B // 2 + 1, DEC_B))
                gain(SAMPLE)
                late(SAMPLE)

            @block.scalar
            def _(act):
                for s in (swish_ready, qkT_ready, sq_ready):
                    act.sem_inc(s, 1)
                for s in mix_stored:
                    act.sem_inc(s, 16)
                act.wait_ge(cleared, 3)

                def swish_gate(t, par, lap):
                    act.wait_ge(vg_landed[par], lap)
                    act.wait_ge(gate_ready, by(t - 1))
                    act.activation(swish[:, :], zr[:, par, 3].rearrange("p h d -> p (h d)"), ACT.Silu).then_inc(swish_ready, 1)

                def evacuate(t, rows):
                    act.wait_ge(qk_turned, by(t))
                    act.wait_ge(inner_done, by(t - 1))
                    act.wait_ge(qd_ready, by(t - 1))
                    act.copy(qT[:, :, 0:rows], qk_ps[0][:, :, 0:rows])
                    for r in range(2):
                        d = slice(HD * r, HD * r + HD)
                        x = act.copy(kT[d, r, :, 0:rows], qk_ps[1][d, :, 0:rows])
                    x.then_inc(qkT_ready, 1)

                def square(t):
                    act.wait_ge(oc_ready, by(t))
                    act.activation(sq[:, :, :], oc[:, :, :], ACT.Square).then_inc(sq_ready, 1)

                def step(t, par, i=0):
                    evacuate(t, 128)
                    if not known(t, 0):
                        square(t - 1)
                    swish_gate(t, par, lap(t, par, i))

                over_tiles(act, step)
                evacuate(SAMPLE, NS)
                square(PT - 1)
                swish_gate(SAMPLE, 0, 16 * PT // 2 + 16)
                square(SAMPLE)

            @block.vector
            def _(dve):
                for s in (qk_ready, qd_ready, inT_ready, S_ready, oc_ready, var_ready, mix_ready):
                    dve.sem_inc(s, 1)
                dve.sem_inc(dve_step, 1)
                dve.wait_ge(rope_landed, 16)

                def rotate(t, par, lap, steps):
                    dve.wait_ge(qk_landed[par], lap)
                    dve.wait_ge(qk_ready, by(t - 1))
                    x = zr[:, par, 0:2].rearrange("p a h d -> p (a h) d")
                    for a, b in ((0, 32), (32, 0)):
                        dve.tensor_tensor(t2[:, :, a:a + 32], x[:, :, b:b + 32],
                                          rope[:, t, 1, a:a + 32].unsqueeze(1).broadcast_to([128, 2 * NH, 32]),
                                          ALU.mult).then_inc(dve_step, 1)
                    dve.wait_ge(dve_step, steps)
                    dve.wait_ge(t1_ready, by(t))
                    dve.wait_ge(qk_turned, by(t - 1))
                    dve.wait_ge(kd_ready, by(t - 1))
                    dve.tensor_tensor(qk[:, :, :], t1[:, :, :], t2[:, :, :], ALU.add).then_inc(qk_ready, 1)

                def scores(t, rows, cross, decay):
                    dve.wait_ge(qkT_ready, by(t))
                    dve.wait_ge(o_done, by(t - 1))
                    q = qT[:, :, 0:rows]
                    if rows == 128:
                        dve.tensor_tensor(qd[:, :, :], q, cross[:, :, :], ALU.mult).then_inc(qd_ready, 1)
                    else:
                        dve.wait_ge(cleared, 4)
                        own = bass.AP(tensor=qdm[:].tensor, offset=qdm[:].offset,
                                      ap=[list(qdm[:].ap[0]), [DEC_B * NS, NPAIR], [NS + DEC_T, DEC_B], [1, DEC_T]])
                        split = lambda x: x.rearrange("p a (b t) -> p a b t", b=DEC_B)
                        dve.tensor_tensor(own, split(q), split(cross[:, :, :]), ALU.mult).then_inc(qd_ready, 1)
                    dve.wait_ge(inner_done, by(t))
                    for r in range(2):
                        x = dve.tensor_tensor(inT[0:rows, r, :, 0:rows], in_ps[r][0:rows, :, 0:rows],
                                              decay[:, r:NH:2, :], ALU.mult)
                    x.then_inc(inT_ready, 1)

                def new_state(t, S_next):
                    dve.wait_ge(update_done, by(t))
                    dve.wait_ge(Sg_ready, by(t))
                    for r in range(2):
                        x = dve.tensor_tensor(diagonal(S_next, r), diagonal(Sg, r), diagonal(su_ps, r), ALU.add)
                    x.then_inc(S_ready, 1)

                def centre(t, rows, steps):
                    dve.wait_ge(o_done, by(t))
                    dve.tensor_reduce(stat[0:rows, 0, :], o_ps[0:rows], AXX, ALU.add).then_inc(dve_step, 1)
                    dve.wait_ge(dve_step, steps)
                    dve.tensor_scalar(stat[0:rows, 1, :], stat[0:rows, 0, :], -1.0 / HD, None, ALU.mult).then_inc(dve_step, 1)
                    dve.wait_ge(dve_step, steps + 1)
                    dve.wait_ge(on_ready, by(t - 1))
                    dve.tensor_tensor(oc[0:rows], o_ps[0:rows], spread(stat[0:rows, 1, :], [rows, NH, HD]),
                                      ALU.add).then_inc(oc_ready, 1)

                def variance(t, steps):
                    dve.wait_ge(sq_ready, by(t))
                    dve.tensor_reduce(stat[:, 2, :], sq[:, :, :], AXX, ALU.add).then_inc(dve_step, 1)
                    dve.wait_ge(dve_step, steps)
                    dve.tensor_scalar(stat[:, 3, :], stat[:, 2, :], 1.0 / HD, GN_EPS, ALU.mult, ALU.add).then_inc(var_ready, 1)

                def finish(t, par, stored):
                    dve.wait_ge(on_ready, by(t))
                    dve.wait_ge(gate_ready, by(t))
                    dve.wait_ge(mix_stored[par], stored)
                    dve.tensor_tensor(mixr[:, par, :], on[:, :, :].rearrange("p h d -> p (h d)"), gate[:, :],
                                      ALU.mult).then_inc(mix_ready, 1)

                rotate(0, 0, 16, 3)
                dve.wait_ge(tab_landed, 16 * TABS)
                dve.wait_ge(cleared, 2)

                def step(t, par, i=0):
                    rotate(t + 1, 1 - par, next_lap(t, i), 5 if known(t, 0) else 5 * t + 4)
                    scores(t, 128, cross, decay)
                    if not known(t, 0):
                        variance(t - 1, 5 * t + 5)
                    new_state(t, S[:, 1 - par])
                    if not known(t, 0):
                        finish(t - 1, 1 - par, 16 * i + 16)
                    centre(t, 128, 5 * t + 6)

                over_tiles(dve, step)
                scores(SAMPLE, NS, cross_s, decay_s)
                variance(PT - 1, 5 * PT + 3)
                finish(PT - 1, 1, 16 * PT // 2)
                one_sequence(dve, slice(0, DEC_B // 2 + 1))
                centre(SAMPLE, NS, 5 * PT + 4)
                variance(SAMPLE, 5 * PT + 6)
                dve.wait_ge(state_landed, 32)
                for p in range(NPAIR):
                    dve.wait_ge(update_done, by(SAMPLE) + p)
                    for r in range(2):
                        rows = slice(HD * r, HD * r + HD)
                        dve.scalar_tensor_tensor(S_out[rows, :, p], S_in[rows, :, p, HD * r:HD * r + HD],
                                                 chunk_s[rows, p:p + 1],
                                                 su_ps[rows].rearrange("d a (c e) -> d (a c) e", e=HD),
                                                 ALU.mult, ALU.add).then_inc(sout_ready, 1)
                finish(SAMPLE, 0, 16 * PT // 2 + 16)

            @block.tensor
            def _(pe):
                for s in (qk_turned, inner_done, update_done, o_done):
                    pe.sem_inc(s, 1)

                def turn(t):
                    pe.wait_ge(qk_ready, by(t))
                    pe.wait_ge(qkT_ready, by(t - 1))
                    for g in range(2):
                        for p in range(NPAIR):
                            h = g * NH + 2 * p
                            mm = pe.transpose(qk_ps[g][:, p, :], qk[:, h:h + 2, :].rearrange("t h d -> t (h d)"), ident[:, :])
                    mm.then_inc(qk_turned, 1)

                def inner(t, rows):
                    pe.wait_ge(qkT_ready, by(t))
                    pe.wait_ge(inT_ready, by(t - 1))
                    for p in range(NPAIR):
                        for r in range(2):
                            mm = pe.matmul(in_ps[r][0:rows, p, 0:rows], kT[:, r, p, 0:rows], qT[:, p, 0:rows],
                                           start=True, stop=True)
                    mm.then_inc(inner_done, 1)

                def step(t, par, i=0):
                    inner(t, 128)
                    pe.wait_ge(vg_landed[par], lap(t, par, i))
                    pe.wait_ge(kd_ready, by(t))
                    pe.wait_ge(S_ready, by(t - 1))
                    for p in range(NPAIR):
                        mm = pe.matmul(su_ps[:, p, :], kd[:, 2 * p:2 * p + 2, :].rearrange("t h d -> t (h d)"),
                                       zr[:, par, 2, 2 * p:2 * p + 2, :].rearrange("t h d -> t (h d)"), start=True, stop=True)
                    mm.then_inc(update_done, 1)
                    turn(t + 1)
                    pe.wait_ge(qd_ready, by(t))
                    pe.wait_ge(inT_ready, by(t))
                    pe.wait_ge(oc_ready, by(t - 1))
                    for p in range(NPAIR):
                        pe.matmul(o_ps[:, 2 * p:2 * p + 2, :].rearrange("t h d -> t (h d)"), qd[:, p, :], S[:, par, p, :],
                                  start=True, stop=False)
                        for r in range(2):
                            mm = pe.matmul(o_ps[:, 2 * p + r, :], inT[:, r, p, :], zr[:, par, 2, 2 * p + r, :],
                                           start=False, stop=(r == 1))
                    mm.then_inc(o_done, 1)

                pe.wait_ge(cleared, 2)
                turn(0)
                over_tiles(pe, step)
                inner(SAMPLE, NS)
                pe.wait_ge(state_landed, 32)
                pe.wait_ge(qd_ready, by(SAMPLE))
                pe.wait_ge(inT_ready, by(SAMPLE))
                pe.wait_ge(oc_ready, by(SAMPLE - 1))
                pe.wait_ge(vg_landed[0], 16 * PT // 2 + 16)
                for p in range(NPAIR):
                    for b in range(DEC_B):
                        pe.matmul(o_ps[0:NS, 2 * p:2 * p + 2, :].rearrange("t h d -> t (h d)"),
                                  qdm[:, p, b * NS:b * NS + NS], S_in[:, b, p, :], start=(b == 0), stop=False)
                    for r in range(2):
                        mm = pe.matmul(o_ps[0:NS, 2 * p + r, :], inT[0:NS, r, p, 0:NS], zr[0:NS, 0, 2, 2 * p + r, :],
                                       start=False, stop=(r == 1))
                mm.then_inc(o_done, 1)
                pe.wait_ge(kd_ready, by(SAMPLE))
                pe.wait_ge(vm_ready, 2)
                pe.wait_ge(S_ready, by(PT - 1))
                for p in range(NPAIR):
                    if p:
                        pe.wait_ge(sout_ready, 2 * p)
                    for r in range(2):
                        mm = pe.matmul(su_ps[HD * r:HD * r + HD].rearrange("d a (c e) -> d (a c) e", e=HD),
                                       kd[0:NS, 2 * p + r, :], vm[:, :, HD * (2 * p + r):HD * (2 * p + r + 1)],
                                       start=True, stop=True)
                    mm.then_inc(update_done, 1)


def distance_tables(nc, A, tab, bias_s):
    K = N_BUCKETS + 1
    KEYS = STILES * 128
    with ExitStack() as ctx:
        sb = lambda n, s, d=F32: ctx.enter_context(nc.sbuf_tensor(n, s, d))
        ps = lambda n, s: ctx.enter_context(nc.psum_tensor(n, s, F32))
        sem = lambda n: nc.alloc_semaphore("p0_" + n)
        rel = sb("rel", [K, NH])
        rel_t = sb("rel_t", [K, DEC_T, 2, NH, DEC_T])
        dist_p, dist_s = sb("dist_p", [K, TABW]), sb("dist_s", [K, DEC_T, KEYS])
        row = sb("row", [NH, TABW])
        r_ps = [ps(f"r_ps{i}", [NH, TABW // 3]) for i in range(3)]
        b_ps = [ps(f"b_ps{i}", [128, 512]) for i in range(3)]
        landed, samples_landed, ones_set = sem("landed"), sem("samples_landed"), sem("ones_set")
        rows_done, row_ready, bias_done, bias_ready, stored, rel_t_ready = map(
            sem, ("rows_done", "row_ready", "bias_done", "bias_ready", "stored", "rel_t_ready"))

        with nc.Block() as block:

            @block.sync
            def _(sp):
                sp.dma_start(rel[0:N_BUCKETS, :], A["rel_bias"]).then_inc(landed, 16)
                sp.dma_start(dist_p[:, :], A["c_dist_p"]).then_inc(landed, 16)
                sp.dma_start(dist_s[:, :, :], A["c_dist_s"].rearrange("n t j k -> n t (j k)")).then_inc(samples_landed, 16)
                sp.wait_ge(row_ready, 3)
                sp.dma_start(tab, row[:, :].unsqueeze(1).broadcast_to([NH, 128, TABW])).then_inc(stored, 16)
                sp.wait_ge(stored, 16)

            @block.vector
            def _(dve):
                dve.memset(rel[N_BUCKETS:K, :], 1.0).then_inc(ones_set, 1)
                dve.memset(rel_t[:, :, :, :, :], 0.0).then_inc(ones_set, 1)
                dve.wait_ge(landed, 32)
                dve.wait_ge(ones_set, 2)
                for t in range(DEC_T):
                    dve.tensor_copy(rel_t[:, t, :, :, t], rel[:, :].unsqueeze(1).broadcast_to([K, 2, NH])).then_inc(rel_t_ready, 1)
                dve.wait_ge(rows_done, 1)
                for n in range(3):
                    w = TABW // 3
                    dve.tensor_copy(row[:, n * w:n * w + w], r_ps[n][:, :]).then_inc(row_ready, 1)
                for n in range(3):
                    dve.wait_ge(bias_done, n + 1)
                    w = min(512, KEYS - 512 * n)
                    dve.tensor_copy(bias_s[:, 512 * n:512 * n + w], b_ps[n][:, 0:w]).then_inc(bias_ready, 1)

            @block.tensor
            def _(pe):
                pe.wait_ge(ones_set, 1)
                pe.wait_ge(landed, 32)
                for n in range(3):
                    w = TABW // 3
                    mm = pe.matmul(r_ps[n][:, :], rel[:, :], dist_p[:, n * w:n * w + w], start=True, stop=True)
                mm.then_inc(rows_done, 1)
                pe.wait_ge(samples_landed, 16)
                pe.wait_ge(rel_t_ready, DEC_T)
                for n in range(3):
                    w = min(512, KEYS - 512 * n)
                    for t in range(DEC_T):
                        mm = pe.matmul(b_ps[n][:, 0:w], rel_t[:, t].rearrange("n c h t -> n (c h t)"),
                                       dist_s[:, t, 512 * n:512 * n + w], start=(t == 0), stop=(t == DEC_T - 1))
                    mm.then_inc(bias_done, 1)


def prompt_attention(nc, A, z, mix, tab, ident):
    UNITS = 2 * PT
    at = lambda p, u: UNITS * p + u + 3
    with ExitStack() as ctx:
        sb = lambda n, s, d=F32: ctx.enter_context(nc.sbuf_tensor(n, s, d))
        ps = lambda n, s: ctx.enter_context(nc.psum_tensor(n, s, F32))
        sem = lambda n: nc.alloc_semaphore("p3_" + n)
        q_n, k_n = sb("q_n", [128, PT, 128]), sb("k_n", [128, PT, 128])
        v_all = sb("v_all", [128, PT, WID])
        bias = sb("bias", [128, NH, SEQ])
        qT, kT = sb("qT", [128, SEQ]), sb("kT", [128, 2, SEQ])
        S, P_T = sb("S3", [128, 2, SEQ]), sb("P_T", [128, 2, PT, 128])
        O = sb("O", [128, PT, 128])
        least, total, share = (sb(n, [128, UNITS]) for n in ("least", "total", "share"))
        S_ps = [ps(f"S_ps{i}", [128, SEQ]) for i in range(2)]
        T_ps = [ps(f"T_ps{i}", [128, 4, 128]) for i in range(2)]
        O_ps, prep_ps = ps("O_ps", [128, 128]), ps("prep_ps", [128, 4, 128])
        pair_landed, prep_done, prep_ready = sem("pair_landed"), sem("prep_done"), sem("prep_ready")
        zeros_set, N_ready = sem("zeros_set"), sem("N_ready")
        S_done, E_ready, P_ready, T_done, PT_low, PT_high, share_ready, V_done, O_ready = map(
            sem, ("S_done", "E_ready", "P_ready", "T_done", "PT_low", "PT_high", "share_ready", "V_done", "O_ready"))
        O_stored, bias_landed = sem("O_stored"), sem("bias_landed")
        high = lambda p, u: PT * p + (u - PT) + 3

        with nc.Block() as block:

            @block.sync
            def _(sp):
                rows = z[0:SEQ, :].rearrange("(t p) c -> p t c", p=128)

                def load(p):
                    for n, dst in enumerate((q_n[:, :, :], k_n[:, :, :], v_all[:, :, bass.ds(p * 128, 128)])):
                        sp.dma_start(dst, rows[:, :, bass.ds((4 + n) * WID + p * 128, 128)]).then_inc(pair_landed, 16)

                def store(p):
                    sp.wait_ge(O_ready, at(p, UNITS - 1))
                    sp.dma_start(mix[0:SEQ, bass.ds(WID + p * 128, 128)].rearrange("(t p) c -> p t c", p=128),
                                 O[:, :, :]).then_inc(O_stored, 16)

                load(0)
                for h in range(NH):
                    sp.dma_start(bias[:, h, :], bass.AP(tensor=tab.tensor, offset=h * 128 * TABW + 127, ap=[[TABW - 1, 128], [1, SEQ]])
                                 ).then_inc(bias_landed, 16)
                with sp.Fori(0, NPAIR - 1) as p:
                    sp.wait_ge(pair_landed, 48 * p + 48)
                    sp.wait_ge(prep_done, 4 * p + 4)
                    load(p + 1)
                    store(p)
                store(NPAIR - 1)
                sp.wait_ge(O_stored, 16 * NPAIR)

            @block.scalar
            def _(act):
                for s in (P_ready, PT_high, O_ready):
                    act.sem_inc(s, 2)
                act.sem_inc(prep_ready, 1)

                def exp(p, u):
                    n = (u // 2 + 1) * 128
                    act.wait_ge(E_ready, at(p, u))
                    act.activation(S[:, u % 2, 0:n], S[:, u % 2, 0:n], ACT.Exp, bias=least[:, u:u + 1], scale=-1.0,
                                   accum_out=total[:, u:u + 1]).then_inc(P_ready, 1)

                def evacuate(p, u):
                    nt = u // 2 + 1
                    if nt > 4:
                        act.wait_ge(T_done, at(p, u))
                        act.wait_ge(V_done, at(p, u - 2))
                        act.copy(P_T[:, u % 2, 4:nt, :], T_ps[1][:, 0:nt - 4, :]).then_inc(PT_high, 1)

                def scale(p, u):
                    act.wait_ge(V_done, at(p, u))
                    act.wait_ge(share_ready, at(p, u))
                    if u == 0:
                        act.wait_ge(O_stored, 16 * p)
                    own = slice(HD * (u % 2), HD * (u % 2) + HD)
                    act.activation(O[:, u // 2, own], O_ps[:, own], ACT.Copy, scale=share[:, u:u + 1]).then_inc(O_ready, 1)

                def pair(p):
                    for g in range(4):
                        act.wait_ge(prep_done, 4 * p + g + 1)
                        if g == 0:
                            act.wait_ge(S_done, at(p - 1, UNITS - 1))
                        src, cols = prep_ps[:].rearrange("c t p -> c (t p)"), slice(512 * (g % 2), 512 * (g % 2) + 512)
                        if g < 2:
                            act.mul(qT[:, cols], src, HD ** -0.5).then_inc(prep_ready, 1)
                        else:
                            act.copy(kT[0:HD, 0, cols], src[0:HD, :])
                            act.copy(kT[HD:128, 1, cols], src[HD:128, :]).then_inc(prep_ready, 1)
                    for u in range(UNITS + 2):
                        if u < UNITS:
                            exp(p, u)
                        if 1 <= u <= UNITS:
                            evacuate(p, u - 1)
                        if u >= 2:
                            scale(p, u - 2)

                act.wait_ge(zeros_set, 1)
                with act.Fori(0, NPAIR) as p:
                    pair(p)

            @block.vector
            def _(dve):
                dve.memset(kT[:, :, :], 0.0).then_inc(zeros_set, 1)
                for s in (N_ready, E_ready, PT_low, share_ready):
                    dve.sem_inc(s, 2)

                def scores(p, u):
                    n = (u // 2 + 1) * 128
                    dve.wait_ge(S_done, at(p, u))
                    dve.wait_ge(T_done, at(p, u - 2))
                    dve.scalar_tensor_tensor(
                        S[:, u % 2, 0:n], S_ps[u % 2][:, 0:n], -1.0,
                        bias[:, bass.ds(2 * p + u % 2, 1), SEQ - n:SEQ].rearrange("q h k -> q (h k)"),
                        ALU.mult, ALU.subtract).then_inc(N_ready, 1)
                    dve.wait_ge(N_ready, at(p, u))
                    dve.tensor_reduce(least[:, u:u + 1], S[:, u % 2, 0:n], AXX, ALU.min).then_inc(E_ready, 1)

                def evacuate(p, u):
                    nt = min(u // 2 + 1, 4)
                    dve.wait_ge(T_done, at(p, u))
                    dve.wait_ge(V_done, at(p, u - 2))
                    dve.tensor_copy(P_T[:, u % 2, 0:nt, :], T_ps[0][:, 0:nt, :]).then_inc(PT_low, 1)

                def reciprocal(p, u):
                    dve.wait_ge(P_ready, at(p, u))
                    dve.wait_ge(O_ready, at(p, u - 2))
                    dve.reciprocal(share[:, u:u + 1], total[:, u:u + 1]).then_inc(share_ready, 1)

                dve.wait_ge(bias_landed, 16 * NH)
                with dve.Fori(0, NPAIR) as p:
                    for u in range(UNITS + 1):
                        if u < UNITS:
                            scores(p, u)
                        if u >= 1:
                            evacuate(p, u - 1)
                            reciprocal(p, u - 1)

            @block.tensor
            def _(pe):
                for s in (S_done, T_done, V_done):
                    pe.sem_inc(s, 2)

                def scores(p, u):
                    n = (u // 2 + 1) * 128
                    q0 = (u // 2) * 128
                    pe.wait_ge(E_ready, at(p, u - 2))
                    for k in range(0, n, 512):
                        m = min(n, k + 512)
                        mm = pe.matmul(S_ps[u % 2][:, k:m], qT[:, q0:q0 + 128], kT[:, u % 2, k:m], start=True, stop=True)
                    mm.then_inc(S_done, 1)

                def turn(p, u):
                    pe.wait_ge(P_ready, at(p, u))
                    pe.wait_ge(PT_low, at(p, u - 1))
                    if u > PT:
                        pe.wait_ge(PT_high, high(p, u - 1))
                    for k in range(u // 2 + 1):
                        mm = pe.transpose(T_ps[k // 4][:, k % 4, :], S[:, u % 2, k * 128:k * 128 + 128], ident[:, :])
                    mm.then_inc(T_done, 1)

                def values(p, u):
                    nt = u // 2 + 1
                    pe.wait_ge(PT_low, at(p, u))
                    if u >= PT:
                        pe.wait_ge(PT_high, high(p, u))
                    pe.wait_ge(O_ready, at(p, u - 1))
                    for k in range(nt):
                        mm = pe.matmul(O_ps[:, :], P_T[:, u % 2, k, :], v_all[:, k, bass.ds(p * 128, 128)],
                                       start=(k == 0), stop=(k == nt - 1))
                    mm.then_inc(V_done, 1)

                with pe.Fori(0, NPAIR) as p:
                    pe.wait_ge(pair_landed, 48 * p + 48)
                    for g in range(4):
                        pe.wait_ge(prep_ready, 4 * p + g + 1)
                        for t in range(4):
                            mm = pe.transpose(prep_ps[:, t, :], (q_n, k_n)[g // 2][:, 4 * (g % 2) + t, :], ident[:, :])
                        mm.then_inc(prep_done, 1)
                    pe.wait_ge(prep_ready, 4 * p + 5)
                    scores(p, 0)
                    scores(p, 1)
                    for u in range(UNITS + 1):
                        if u + 2 < UNITS:
                            scores(p, u + 2)
                        if u < UNITS:
                            turn(p, u)
                        if u >= 1:
                            values(p, u - 1)


def sample_attention(nc, A, z, mix, bias_s, ident):
    RING, C, GROUPS = 4, NH * DEC_T, 3
    KEYS = STILES * 128
    PER = STILES + GROUPS
    tiles = lambda g: range(4 * g, min(4 * g + 4, STILES))
    keys = lambda g: slice(512 * g, min(512 * g + 512, KEYS))

    def entry(b, i):
        return i if known(b, 0) else PER * b - GROUPS + i

    def slot(b, par, i):
        return (i if known(b, 0) else PER * par - GROUPS + i) % RING

    def key_at(b, j):
        return j if known(b, 0) or j < 5 else j + GROUPS

    def prob_at(b, g):
        return g if known(b, DEC_B) else 5 + g

    with ExitStack() as ctx:
        sb = lambda n, s, d=F32: ctx.enter_context(nc.sbuf_tensor(n, s, d))
        ps = lambda n, s: ctx.enter_context(nc.psum_tensor(n, s, F32))
        sem = lambda n: nc.alloc_semaphore("p4_" + n)
        K, V = sb("K", [128, 2, STILES, WID]), sb("V", [128, STILES, WID])
        K_hi, K_lo = (sb(n, [128, NPAIR, STILES, 128], F32R) for n in ("K_hi", "K_lo"))
        V_hi, V_lo = (sb(n, [128, STILES, WID], F32R) for n in ("V_hi", "V_lo"))
        q_n, q_b = sb("q_n4", [NS, WID]), sb("q_b", [128, 2, NPAIR, DEC_T])
        q_s = sb("q_s", [128, 2, NPAIR, DEC_B, DEC_T])
        Q_hi, Q_lo = (sb(n, [128, 2, NPAIR * (128 + 2 * DEC_T)], F32R) for n in ("Q_hi", "Q_lo"))
        nought = sb("nought", [128, NPAIR, 2, DEC_T])
        E, P_T = sb("E4", [128, KEYS]), sb("P_T4", [128, STILES, 2, C], F32R)
        mins, least = sb("mins", [128, GROUPS]), sb("least4", [128, 1])
        total, share = sb("total4", [128, 1]), sb("share4", [128, 1])
        own, sum_t = sb("own", [128, WID]), sb("sum_t", [128, 128])
        O, out = sb("O4", [128, WID]), sb("out4", [DEC_T, 2, WID])
        T_ps = [ps(f"T4_ps{i}", [128, 4, 128]) for i in range(RING)]
        S_ps = [ps(f"S4_ps{i}", [128, 512]) for i in range(GROUPS)]
        O_ps = ps("O_ps4", [128, WID])
        K_landed, V_landed, stored = ([sem(f"{n}{i}") for i in range(m)]
                                      for n, m in (("K_landed", 2), ("V_landed", GROUPS), ("stored", 2)))
        (q_landed, set_up, q_turned, q_ready, qb_ready, Qhi_ready, Q_ready, turned, hi_ready, lo_ready, S_done, N_ready, min_ready,
         least_ready, P_ready, Vhi_ready, Vlo_ready, V_done, share_ready, O_ready, sum_done, out_ready) = map(
            sem, ("q_landed", "set_up", "q_turned", "q_ready", "qb_ready", "Qhi_ready", "Q_ready", "turned", "hi_ready", "lo_ready",
                  "S_done", "N_ready", "min_ready", "least_ready", "P_ready", "Vhi_ready", "Vlo_ready", "V_done",
                  "share_ready", "O_ready", "sum_done", "out_ready"))

        def over_sequences(eng, step):
            step(0, 0)
            with eng.Fori(0, DEC_B // 2 - 1) as i:
                step(2 * i + 1, 1, i)
                step(2 * i + 2, 0, i)
            step(DEC_B - 1, 1, DEC_B // 2 - 1)
            step(DEC_B, 0, DEC_B // 2 - 1)

        with nc.Block() as block:

            @block.sync
            def _(sp):
                window = lambda name, b: A[name][0].rearrange("b l h d -> (b l) (h d)")[bass.ds(b * L, L), :]
                wide = lambda name, b, j, n: window(name, b).rearrange("(p x) c -> p (x c)", x=16)[:, j * WID:(j + n) * WID]
                rest = lambda name, b: window(name, b)[REST:L, :].rearrange("(g x) c -> g (x c)", x=16)[:, WIDE * WID:] \
                    .rearrange("g (x c) -> g x c", x=4)
                new = lambda b, c: z[bass.ds(SEQ + b * DEC_T, DEC_T), c * WID:c * WID + WID]

                def load_keys(b, par):
                    if not isinstance(b, int) or b >= 2:
                        sp.wait_ge(turned, entry(b, 0) - PER)
                    sp.dma_start(K[:, par, 0:WIDE, :].rearrange("p j c -> p (j c)"),
                                 wide("cache_k_win", b, 0, WIDE)).then_inc(K_landed[par], 16)
                    sp.dma_start(K[:, par, WIDE:WIDE + 2, :].rearrange("p j c -> p (j c)"),
                                 rest("cache_k_win", b)).then_inc(K_landed[par], 16)
                    sp.dma_start(K[0:DEC_T, par, STILES - 1, :], new(b, 5)).then_inc(K_landed[par], 16)

                def load_values(b):
                    for g in range(GROUPS):
                        if not known(b, 0):
                            sp.wait_ge(Vlo_ready, GROUPS * b + g - 2)
                        if g < 2:
                            sp.dma_start(V[:, 4 * g:4 * g + 4, :].rearrange("p j c -> p (j c)"),
                                         wide("cache_v_win", b, 4 * g, 4)).then_inc(V_landed[g], 16)
                        else:
                            sp.dma_start(V[:, WIDE:WIDE + 2, :].rearrange("p j c -> p (j c)"),
                                         rest("cache_v_win", b)).then_inc(V_landed[g], 16)
                            sp.dma_start(V[0:DEC_T, STILES - 1, :], new(b, 6)).then_inc(V_landed[g], 16)

                def store(b, par):
                    sp.wait_ge(out_ready, by(b))
                    sp.dma_start(mix[bass.ds(SEQ + b * DEC_T, DEC_T), WID:2 * WID], out[:, par, :]).then_inc(stored[par], 16)

                sp.dma_start(q_n[:, :], z[SEQ:NTOK, 4 * WID:5 * WID]).then_inc(q_landed, 16)
                sp.wait_ge(set_up, 3)
                load_keys(0, 0)
                sp.wait_ge(K_landed[0], 48)
                load_values(0)
                load_keys(1, 1)
                sp.dma_start(own[:, :], A["c_own"]).then_inc(q_landed, 16)
                sp.dma_start(sum_t[:, :], A["c_sum_t"]).then_inc(q_landed, 16)
                load_values(1)
                load_keys(2, 0)
                with sp.Fori(1, DEC_B // 2 - 1) as i:
                    for par in range(2):
                        load_values(2 * i + par)
                        load_keys(2 * i + par + 1, 1 - par)
                        store(2 * i + par - 2, par)
                load_values(DEC_B - 2)
                load_keys(DEC_B - 1, 1)
                load_values(DEC_B - 1)
                for b in range(DEC_B - 4, DEC_B):
                    store(b, b % 2)
                sp.wait_ge(stored[0], 8 * DEC_B + 16)
                sp.wait_ge(stored[1], 8 * DEC_B + 16)

            @block.gpsimd
            def _(pool):
                pool.memset(K[:, 0, STILES - 1, :], 0.0).then_inc(set_up, 1)
                pool.memset(K[:, 1, STILES - 1, :], 0.0).then_inc(set_up, 1)
                pool.memset(V[:, STILES - 1, :], 0.0).then_inc(set_up, 1)
                pool.memset(Q_hi[:, :, :].bitcast(F32), 0.0).then_inc(set_up, 1)
                pool.memset(Q_lo[:, :, :].bitcast(F32), 0.0).then_inc(set_up, 1)
                pool.memset(q_s[:, :, :, :, :], 0.0).then_inc(set_up, 1)
                pool.memset(nought[:, :, :, :], 0.0).then_inc(set_up, 1)
                pool.wait_ge(set_up, 7)
                pool.wait_ge(q_ready, 2)

                def queries(b, par):
                    if not known(b, 0):
                        pool.wait_ge(Q_ready, 2 * b)
                    pool.tensor_copy(q_b[:, :, :, :], q_s[:, :, :, bass.ds(b, 1), :].rearrange("d r p b t -> d r p (b t)")
                                     ).then_inc(qb_ready, 1)
                    pool.wait_ge(qb_ready, b + 1)
                    block_of = lambda t, r: t[:, par, :].rearrange("d (p x) -> d p x", p=NPAIR)[:, :, 0:128] \
                        .rearrange("d p (c x) -> d p c x", c=2)[:, :, :, DEC_T * r:DEC_T * r + DEC_T]
                    both = lambda r: q_b[:, r].unsqueeze(2).broadcast_to([128, NPAIR, 2, DEC_T])
                    for r in range(2):
                        pool.tensor_tensor(block_of(Q_hi, r), both(r), nought[:, :, :, :], ALU.add).then_inc(Qhi_ready, 1)
                    pool.wait_ge(Qhi_ready, 2 * b + 2)
                    for r in range(2):
                        pool.tensor_tensor(block_of(Q_lo, r), both(r), block_of(Q_hi, r).bitcast(F32),
                                           ALU.subtract).then_inc(Q_ready, 1)

                def step(b, par, i=0):
                    if known(b, DEC_B):
                        return
                    if not known(b, DEC_B - 1):
                        if not known(b, 0):
                            pool.wait_ge(S_done, GROUPS * b)
                        queries(b + 1, 1 - par)
                    for g in range(GROUPS):
                        pool.wait_ge(Vhi_ready, GROUPS * b + g + 1)
                        cut = (slice(None), slice(4 * g, min(4 * g + 4, STILES)))
                        pool.tensor_tensor(V_lo[cut], V[cut], V_hi[cut].bitcast(F32), ALU.subtract).then_inc(Vlo_ready, 1)

                queries(0, 0)
                over_sequences(pool, step)

            @block.scalar
            def _(act):
                def keys_high(b, par, j):
                    i = key_at(b, j)
                    act.wait_ge(turned, entry(b, i) + 1)
                    if not known(b, 0) and j % 4 == 0:
                        act.wait_ge(S_done, GROUPS * b - 2 + j // 4)
                    act.copy(K_hi[:, :, j, :], T_ps[slot(b, par, i)][:, :, :]).then_inc(hi_ready, 1)

                def exp(b):
                    act.wait_ge(least_ready, b + 1)
                    act.wait_ge(share_ready, by(b - 1))
                    act.activation(E[:, :], E[:, :], ACT.Exp, bias=least[:, 0:1], scale=-1.0,
                                   accum_out=total[:, 0:1]).then_inc(P_ready, 1)

                def probs_high(b, par, g):
                    i, n = prob_at(b, g), len(tiles(g))
                    act.wait_ge(turned, entry(b, i) + 1)
                    act.wait_ge(V_done, GROUPS * b + g - 2)
                    act.copy(P_T[:, 4 * g:4 * g + n, 0, :], T_ps[slot(b, par, i)][:, 0:n, 0:C]).then_inc(hi_ready, 1)

                def values_high(b, g, lap):
                    act.wait_ge(V_landed[g], lap * (32 if g == 2 else 16))
                    act.wait_ge(V_done, GROUPS * b + g + 1)
                    cut = (slice(None), slice(4 * g, min(4 * g + 4, STILES)))
                    act.copy(V_hi[cut], V[cut]).then_inc(Vhi_ready, 1)

                def evacuate(b, par, i):
                    act.wait_ge(sum_done, by(b))
                    act.wait_ge(stored[par], 16 * i + 16)
                    act.copy(out[:, par, :], O_ps[0:DEC_T, :]).then_inc(out_ready, 1)

                def step(b, par, i=0):
                    begins, ends = not known(b, DEC_B), not known(b, 0)
                    if begins:
                        for j in range(5):
                            keys_high(b, par, j)
                    if ends:
                        exp(b - 1)
                        for g in range(GROUPS):
                            probs_high(b, par, g)
                    if begins:
                        for j in range(5, STILES):
                            keys_high(b, par, j)
                            if j == 7:
                                values_high(b, 0, b + 1)
                        values_high(b, 1, b + 1)
                        values_high(b, 2, b + 1)
                    if ends:
                        evacuate(b - 1, 1 - par, i)

                act.sem_inc(stored[0], 16)
                act.sem_inc(stored[1], 16)
                act.wait_ge(q_turned, 1)
                act.wait_ge(set_up, 6)
                for r in range(2):
                    d = slice(HD * r, HD * r + HD)
                    act.mul(q_s[d, r].rearrange("d p b t -> d p (b t)"),
                            O_ps[d, 0:NPAIR * NS].rearrange("d (p n) -> d p n", p=NPAIR), HD ** -0.5).then_inc(q_ready, 1)
                act.sem_inc(out_ready, 1)
                over_sequences(act, step)

            @block.vector
            def _(dve):
                dve.wait_ge(q_landed, 48)
                dve.sem_inc(share_ready, 1)
                dve.sem_inc(O_ready, 1)

                def keys_low(b, par, j):
                    i = key_at(b, j)
                    dve.wait_ge(hi_ready, entry(b, i) + 1)
                    dve.tensor_tensor(K_lo[:, :, j, :], T_ps[slot(b, par, i)][:, :, :], K_hi[:, :, j, :].bitcast(F32),
                                      ALU.subtract).then_inc(lo_ready, 1)

                def probs_low(b, par, g):
                    i, n = prob_at(b, g), len(tiles(g))
                    dve.wait_ge(hi_ready, entry(b, i) + 1)
                    cut = (slice(None), slice(4 * g, 4 * g + n))
                    dve.tensor_tensor(P_T[cut][:, :, 1, :], T_ps[slot(b, par, i)][:, 0:n, C:2 * C],
                                      P_T[cut][:, :, 0, :].bitcast(F32), ALU.subtract).then_inc(lo_ready, 1)

                def add_bias(b, g):
                    w = keys(g)
                    dve.wait_ge(S_done, GROUPS * b + g + 1)
                    if g == 0 and not known(b, 0):
                        dve.wait_ge(turned, entry(b, prob_at(b, GROUPS)))
                    dve.scalar_tensor_tensor(E[:, w], S_ps[g][:, 0:w.stop - w.start], -1.0, bias_s[:, w],
                                             ALU.mult, ALU.subtract).then_inc(N_ready, 1)
                    if g == 0 and not known(b, 0):
                        dve.wait_ge(least_ready, b)
                    dve.wait_ge(N_ready, GROUPS * b + g + 1)
                    dve.tensor_reduce(mins[:, g:g + 1], E[:, w], AXX, ALU.min).then_inc(min_ready, 1)

                def find_least(b):
                    dve.wait_ge(min_ready, GROUPS * b + GROUPS)
                    if not known(b, 0):
                        dve.wait_ge(P_ready, b)
                    dve.tensor_reduce(least[:, :], mins[:, :], AXX, ALU.min).then_inc(least_ready, 1)

                def normalise(b):
                    dve.wait_ge(P_ready, b + 1)
                    dve.wait_ge(O_ready, by(b - 1))
                    dve.reciprocal(share[:, :], total[:, :]).then_inc(share_ready, 1)
                    dve.wait_ge(share_ready, by(b))
                    dve.wait_ge(V_done, GROUPS * (b + 2))
                    dve.wait_ge(sum_done, by(b - 1))
                    dve.scalar_tensor_tensor(O[:, :], O_ps[:, :], share[:, 0:1], own[:, :], ALU.mult,
                                             ALU.mult).then_inc(O_ready, 1)

                def step(b, par, i=0):
                    begins, ends = not known(b, DEC_B), not known(b, 0)
                    if begins:
                        for j in range(5):
                            keys_low(b, par, j)
                    if ends:
                        for g in range(GROUPS):
                            probs_low(b, par, g)
                    if begins:
                        add_bias(b, 0)
                        for j in range(5, 8):
                            keys_low(b, par, j)
                        add_bias(b, 1)
                        for j in range(8, STILES):
                            keys_low(b, par, j)
                    if ends:
                        normalise(b - 1)
                    if begins:
                        add_bias(b, 2)
                        find_least(b)

                over_sequences(dve, step)

            @block.tensor
            def _(pe):
                pe.sem_inc(V_done, GROUPS)
                pe.sem_inc(sum_done, 1)

                def free(b, i):
                    if not known(b, 0) or i >= RING:
                        pe.wait_ge(lo_ready, entry(b, i) - RING + 1)

                def turn_keys(b, par, j):
                    i = key_at(b, j)
                    free(b, i)
                    for p in range(NPAIR):
                        mm = pe.transpose(T_ps[slot(b, par, i)][:, p, :], K[:, par, j, 128 * p:128 * p + 128], ident[:, :])
                    mm.then_inc(turned, 1)

                def turn_probs(b, par, g):
                    i = prob_at(b, g)
                    if g == 0:
                        pe.wait_ge(P_ready, b)
                    free(b, i)
                    for n, j in enumerate(tiles(g)):
                        mm = pe.transpose(T_ps[slot(b, par, i)][:, n, :], E[:, 128 * j:128 * j + 128], ident[:, :])
                    mm.then_inc(turned, 1)

                def scores(b, par, g):
                    w = keys(g)
                    pe.wait_ge(lo_ready, entry(b, key_at(b, tiles(g)[-1])) + 1)
                    if g == 0:
                        pe.wait_ge(Q_ready, 2 * b + 2)
                    if not known(b, 0):
                        pe.wait_ge(N_ready, GROUPS * b - 2 + g)
                    for p in range(NPAIR):
                        for m, (q, k) in enumerate(((Q_hi, K_hi), (Q_hi, K_lo), (Q_lo, K_hi))):
                            mm = pe.matmul(S_ps[g][:, 0:w.stop - w.start], q[:, par, 128 * p:128 * p + 128],
                                           k[:, p, :, :].rearrange("d j n -> d (j n)")[:, w],
                                           start=(p, m) == (0, 0), stop=(p, m) == (NPAIR - 1, 2))
                    mm.then_inc(S_done, 1)

                def values(b, g):
                    pe.wait_ge(lo_ready, entry(b, prob_at(b, g)) + 1)
                    pe.wait_ge(Vlo_ready, GROUPS * b - 2 + g)
                    if g == 0:
                        pe.wait_ge(out_ready, b)
                    for j in tiles(g):
                        for m, v in enumerate((V_hi, V_lo)):
                            mm = pe.matmul(O_ps[:, :], P_T[:, j].rearrange("k c n -> k (c n)"), v[:, j, :],
                                           start=(j, m) == (0, 0), stop=(j, m) == (STILES - 1, 1))
                    mm.then_inc(V_done, 1)

                def sum_heads(b):
                    pe.wait_ge(O_ready, by(b))
                    pe.matmul(O_ps[:, :], sum_t[:, :], O[:, :], start=True, stop=True).then_inc(sum_done, 1)

                def step(b, par, i=0):
                    begins, ends = not known(b, DEC_B), not known(b, 0)
                    if begins:
                        pe.wait_ge(K_landed[par], 48 if known(b, 0) else 48 * i + 48 * (2 - par))
                        for j in range(5):
                            turn_keys(b, par, j)
                        scores(b, par, 0)
                    if ends:
                        for g in range(GROUPS):
                            turn_probs(b, par, g)
                    if begins:
                        for j in range(5, 8):
                            turn_keys(b, par, j)
                    if ends:
                        values(b, 0)
                    if begins:
                        scores(b, par, 1)
                    if ends:
                        values(b, 1)
                    if begins:
                        for j in range(8, STILES):
                            turn_keys(b, par, j)
                    if ends:
                        values(b, 2)
                    if begins:
                        scores(b, par, 2)
                    if ends:
                        sum_heads(b - 1)

                pe.wait_ge(q_landed, 48)
                for p in range(NPAIR):
                    mm = pe.transpose(O_ps[:, NS * p:NS * p + NS], q_n[:, 128 * p:128 * p + 128], ident[0:NS, 0:NS])
                mm.then_inc(q_turned, 1)
                pe.wait_ge(q_ready, 2)
                over_sequences(pe, step)


def out_projection(nc, A, mix, x_mid, h_hi, h_lo, ident):
    HK = KT // 2
    w_v = A["w_out"][0].rearrange("(q k p) n -> q p k n", q=4, p=128)
    with ExitStack() as ctx:
        sb = lambda n, s, d=F32: ctx.enter_context(nc.sbuf_tensor(n, s, d))
        ps = lambda n, s: ctx.enter_context(nc.psum_tensor(n, s, F32))
        sem = lambda n: nc.alloc_semaphore("p5_" + n)
        RAW = 3
        w_raw = sb("wo_raw", [128, RAW, D_MODEL])
        w_hi, w_lo = sb("wo_hi", [128, KT, D_MODEL], F32R), sb("wo_lo", [128, KT, D_MODEL], F32R)
        m_n, x_n = sb("m_n", [128, 2, D_MODEL]), sb("x_n", [128, 2, D_MODEL])
        m_hi, m_lo = sb("m_hi", [128, 2, KT, 128], F32R), sb("m_lo", [128, 2, KT, 128], F32R)
        y, xm, xn = sb("y5", [128, D_MODEL]), sb("xm", [128, 2, D_MODEL]), sb("xn5", [128, D_MODEL])
        hg = sb("hg5", [128, 2, HK, 128])
        g_post, g_rows, gT = sb("g_post", [128, D_MODEL]), sb("g_rows5", [KT, 128]), sb("gT5", [128, KT])
        stat, mhalf = sb("stat5", [128, 6]), sb("mhalf5", [128, 1])
        m_ps = [ps(f"m5_ps{i}", [128, HK, 128]) for i in range(2)]
        x_ps = [ps(f"x5_ps{i}", [128, HK, 128]) for i in range(2)]
        y_ps = [ps(f"y5_ps{i}", [128, D_MODEL]) for i in range(2)]
        m_landed, x_landed, xm_stored = ([sem(f"{n}{i}") for i in range(2)] for n in ("m_landed", "x_landed", "xm_stored"))
        w_landed = [sem(f"w_landed{i}") for i in range(RAW)]
        g_landed, w_hi_ready, w_lo_ready, set_up, g_turned, g_ready = map(
            sem, ("g_landed", "w_hi_ready", "w_lo_ready", "set_up", "g_turned", "g_ready"))
        (m_turned, m_hi_ready, m_lo_ready, y_done, y_squared, y_mean, y_rstd, y_ready, xm_ready, xm_squared, xm_mean,
         xm_rstd, xn_ready, x_turned, hg_ready, hi_ready, lo_ready) = map(
            sem, ("m_turned", "m_hi_ready", "m_lo_ready", "y_done", "y_squared", "y_mean", "y_rstd", "y_ready", "xm_ready",
                  "xm_squared", "xm_mean", "xm_rstd", "xn_ready", "x_turned", "hg_ready", "hi_ready", "lo_ready"))
        half = lambda t, q: 2 * t + q + 3
        S = PT

        def over_tiles(eng, step):
            step(0, 0)
            step(1, 1)
            with eng.Fori(1, PT // 2) as i:
                for par in range(2):
                    step(2 * i + par, par, i)
            step(S, 0)

        with nc.Block() as block:

            @block.sync
            def _(sp):
                def load(t, par, x_rows, rows=128):
                    if not isinstance(t, int) or t >= 2:
                        sp.wait_ge(m_turned, by(t - 2))
                    sp.dma_start(m_n[0:rows, par, :], mix[bass.ds(t * 128, rows), :]).then_inc(m_landed[par], 16)
                    if not isinstance(t, int) or t >= 2:
                        sp.wait_ge(xm_ready, by(t - 2))
                    sp.dma_start(x_n[0:rows, par, :], x_rows).then_inc(x_landed[par], 16)

                def store(t, par, rows=128):
                    sp.wait_ge(xm_ready, by(t))
                    sp.dma_start(x_mid[bass.ds(t * 128, rows), :], xm[0:rows, par, :]).then_inc(xm_stored[par], 16)

                x_p = A["x_prompt"][0]
                load(0, 0, x_p[0:128, :])
                sp.dma_start(g_rows[:, :], A["g_pre_ffn"][0].rearrange("(k p) -> k p", p=128)).then_inc(g_landed, 16)
                sp.dma_start(g_post[:, :], A["g_post_mix"][0].partition_broadcast(128)).then_inc(g_landed, 16)
                for k in range(KT):
                    if k >= RAW:
                        sp.wait_ge(w_lo_ready, k - RAW + 1)
                    sp.dma_start(w_raw[:, k % RAW, :], A["w_out"][0, k * 128:k * 128 + 128, :]).then_inc(w_landed[k % RAW], 16)
                load(1, 1, x_p[128:256, :])
                with sp.Fori(0, PT // 2 - 1) as i:
                    for par in range(2):
                        load(2 * i + 2 + par, par, x_p[bass.ds(i * 256 + 256 + 128 * par, 128), :])
                        store(2 * i + par, par)
                load(S, 0, A["x_sample"].rearrange("b t d -> (b t) d"), NS)
                store(PT - 2, 0)
                store(PT - 1, 1)
                store(S, 0, NS)
                sp.wait_ge(xm_stored[0], 80)
                sp.wait_ge(xm_stored[1], 64)

            @block.gpsimd
            def _(pool):
                pool.memset(mhalf[:, :], -0.5).then_inc(set_up, 1)
                for s in (y_rstd, xm_ready, xm_rstd):
                    pool.sem_inc(s, 1)
                pool.sem_inc(lo_ready, 2)
                pool.wait_ge(set_up, 1)

                def residual(t, par, i=0):
                    pool.wait_ge(y_mean, by(t))
                    pool.tensor_tensor(stat[:, 2:3], stat[:, 1:2], mhalf[:, :], ALU.pow).then_inc(y_rstd, 1)
                    pool.wait_ge(y_ready, by(t))
                    pool.wait_ge(x_landed[par], 16 * PT // 2 + 16 if known(t, S) else 16 * i + 16)
                    if known(t, S) or not known(i, 0):
                        pool.wait_ge(xm_stored[par], 16 * PT // 2 if known(t, S) else 16 * i)
                    pool.wait_ge(xn_ready, by(t - 1))
                    pool.tensor_tensor(xm[:, par, :], y[:, :], x_n[:, par, :], ALU.add).then_inc(xm_ready, 1)
                    pool.wait_ge(xm_mean, by(t))
                    pool.tensor_tensor(stat[:, 5:6], stat[:, 4:5], mhalf[:, :], ALU.pow).then_inc(xm_rstd, 1)

                def low(t, n=128):
                    for q in range(2):
                        pool.wait_ge(hi_ready, half(t, q))
                        cut = (slice(None), slice(HK * q, HK * q + HK), bass.ds(t * 128, n))
                        pool.tensor_tensor(h_lo[cut], hg[:, q, :, 0:n], h_hi[cut].bitcast(F32), ALU.subtract).then_inc(lo_ready, 1)

                residual(0, 0)
                residual(1, 1)
                low(0)
                with pool.Fori(1, PT // 2) as i:
                    for par in range(2):
                        residual(2 * i + par, par, i)
                        low(2 * i + par - 1)
                residual(S, 0)
                low(S - 1)
                low(S, NS)

            @block.scalar
            def _(act):
                for s in (m_hi_ready, y_squared, xm_squared):
                    act.sem_inc(s, 1)
                act.sem_inc(hi_ready, 2)

                def mix_high(t, par):
                    act.wait_ge(m_turned, by(t))
                    if not isinstance(t, int) or t >= 2:
                        act.wait_ge(y_done, by(t - 2))
                    for q in range(2):
                        x = act.copy(m_hi[:, par, HK * q:HK * q + HK, :], m_ps[q][:, :, :])
                    x.then_inc(m_hi_ready, 1)

                def square_y(t, par):
                    act.wait_ge(y_done, by(t))
                    act.wait_ge(xm_ready, by(t - 1))
                    act.activation(y[:, :], y_ps[par][:, :], ACT.Square, accum_out=stat[:, 0:1]).then_inc(y_squared, 1)

                def square_x(t, par):
                    act.wait_ge(xm_ready, by(t))
                    act.wait_ge(x_turned, half(t - 1, 1))
                    act.activation(xn[:, :], xm[:, par, :], ACT.Square, accum_out=stat[:, 3:4]).then_inc(xm_squared, 1)

                def high(t, n=128):
                    for q in range(2):
                        act.wait_ge(hg_ready, half(t, q))
                        act.copy(h_hi[:, HK * q:HK * q + HK, bass.ds(t * 128, n)], hg[:, q, :, 0:n]).then_inc(hi_ready, 1)

                def step(t, par, i=0):
                    if not known(t, S):
                        mix_high(t + 1, 1 - par)
                    square_y(t, par)
                    if not known(t, 0):
                        high(t - 1)
                    square_x(t, par)

                mix_high(0, 0)
                for k in range(KT):
                    act.wait_ge(w_landed[k % RAW], 16 * (k // RAW) + 16)
                    act.copy(w_hi[:, k, :], w_raw[:, k % RAW, :]).then_inc(w_hi_ready, 1)
                over_tiles(act, step)
                high(S, NS)

            @block.vector
            def _(dve):
                for s in (m_lo_ready, y_mean, y_ready, xm_mean, xn_ready):
                    dve.sem_inc(s, 1)
                dve.sem_inc(hg_ready, 2)
                dve.wait_ge(g_turned, 1)
                dve.tensor_copy(gT[:, :], x_ps[0][:, 0, 0:KT]).then_inc(g_ready, 1)
                dve.wait_ge(g_ready, 1)
                dve.wait_ge(g_landed, 32)

                def mix_low(t, par):
                    dve.wait_ge(m_hi_ready, by(t))
                    for q in range(2):
                        cut = (slice(None), par, slice(HK * q, HK * q + HK))
                        x = dve.tensor_tensor(m_lo[cut], m_ps[q][:, :, :], m_hi[cut].bitcast(F32), ALU.subtract)
                    x.then_inc(m_lo_ready, 1)

                def scale_y(t, par):
                    dve.wait_ge(y_squared, by(t))
                    dve.tensor_scalar(stat[:, 1:2], stat[:, 0:1], 1.0 / D_MODEL, EPS, ALU.mult, ALU.add).then_inc(y_mean, 1)
                    dve.wait_ge(y_rstd, by(t))
                    dve.scalar_tensor_tensor(y[:, :], y_ps[par][:, :], stat[:, 2:3], g_post[:, :], ALU.mult, ALU.mult).then_inc(y_ready, 1)

                def scale_x(t, par):
                    dve.wait_ge(xm_squared, by(t))
                    dve.tensor_scalar(stat[:, 4:5], stat[:, 3:4], 1.0 / D_MODEL, EPS, ALU.mult, ALU.add).then_inc(xm_mean, 1)
                    dve.wait_ge(xm_rstd, by(t))
                    dve.tensor_scalar(xn[:, :], xm[:, par, :], stat[:, 5:6], None, ALU.mult).then_inc(xn_ready, 1)

                def gain(t):
                    for q in range(2):
                        dve.wait_ge(x_turned, half(t, q))
                        dve.wait_ge(lo_ready, half(t - 1, q))
                        dve.tensor_tensor(hg[:, q], x_ps[q][:, :, :], spread(gT[:, HK * q:HK * q + HK], [128, HK, 128]),
                                          ALU.mult).then_inc(hg_ready, 1)

                def step(t, par, i=0):
                    if not known(t, S):
                        mix_low(t + 1, 1 - par)
                    scale_y(t, par)
                    if not known(t, 0):
                        gain(t - 1)
                    scale_x(t, par)

                mix_low(0, 0)
                for k in range(KT):
                    dve.wait_ge(w_hi_ready, k + 1)
                    dve.tensor_tensor(w_lo[:, k, :], w_raw[:, k % RAW, :], w_hi[:, k, :].bitcast(F32), ALU.subtract).then_inc(w_lo_ready, 1)
                over_tiles(dve, step)
                gain(S)

            @block.tensor
            def _(pe):
                for s in (m_turned, y_done):
                    pe.sem_inc(s, 1)
                pe.sem_inc(x_turned, 2)

                def turn_mix(t, par, lap):
                    pe.wait_ge(m_landed[par], lap)
                    pe.wait_ge(m_lo_ready, by(t - 1))
                    for k in range(KT):
                        mm = pe.transpose(m_ps[k // HK][:, k % HK, :], m_n[:, par, 128 * k:128 * k + 128], ident[:, :])
                    mm.then_inc(m_turned, 1)

                def project(t, par):
                    pe.wait_ge(m_lo_ready, by(t))
                    pe.wait_ge(y_ready, by(t - 2)) if (not isinstance(t, int) or t >= 2) else None
                    for c in range(0, D_MODEL, 512):
                        for k in range(KT):
                            if known(t, 0) and c == 0:
                                pe.wait_ge(w_lo_ready, k + 1)
                            for n, (x, w) in enumerate(((m_hi, w_hi), (m_hi, w_lo), (m_lo, w_hi))):
                                mm = pe.matmul(y_ps[par][:, c:c + 512], x[:, par, k, :], w[:, k, c:c + 512],
                                               start=(k, n) == (0, 0), stop=(k, n) == (KT - 1, 2))
                    mm.then_inc(y_done, 1)

                def turn_x(t):
                    pe.wait_ge(xn_ready, by(t))
                    for q in range(2):
                        pe.wait_ge(hg_ready, half(t - 1, q))
                        for k in range(HK):
                            c = (HK * q + k) * 128
                            mm = pe.transpose(x_ps[q][:, k, :], xn[:, c:c + 128], ident[:, :])
                        mm.then_inc(x_turned, 1)

                def step(t, par, i=0):
                    if not known(t, S):
                        lap = 16 if known(t, 0) else 32 if known(t, 1) else 16 * i + 16 + 16 * par
                        turn_mix(t + 1, 1 - par, lap)
                    project(t, par)
                    if not known(t, 0):
                        turn_x(t - 1)

                pe.wait_ge(g_landed, 32)
                pe.transpose(x_ps[0][:, 0, 0:KT], g_rows[:, :], ident[0:KT, 0:KT]).then_inc(g_turned, 1)
                pe.wait_ge(g_ready, 1)
                turn_mix(0, 0, 16)
                over_tiles(pe, step)
                turn_x(S)


def ffn(nc, A, z, h_hi, h_lo, acc):
    HK, SUB, GROUP_D = KT // 2, 2, 2 * TT
    GROUPS = D_FF // (128 * SUB)
    CHUNKS = ((0, 364), (364, 362), (726, 362))
    UNITS = SUB * len(CHUNKS)
    DOWN_AFTER = (0, 3, 4, 4, 4, 3)
    SHARE = (L - DEC_T) // ((GROUPS - 1) * UNITS)
    gu_v = A["w_gu"][0].rearrange("(q k p) n -> q p k n", q=2, p=128)
    keep = lambda a: a[0].rearrange("b l h d -> b (l h d)")
    with ExitStack() as ctx:
        sb = lambda n, s, d=F32: ctx.enter_context(nc.sbuf_tensor(n, s, d))
        ps = lambda n, s: ctx.enter_context(nc.psum_tensor(n, s, F32))
        sem = lambda n: nc.alloc_semaphore("p6_" + n)
        raw = sb("raw6", [128, 2, D_MODEL])
        gu_hi, gu_lo = (sb(n, [128, SUB, KT, 2, 128], F32R) for n in ("gu_hi", "gu_lo"))
        wd_hi, wd_lo = (sb(n, [128, SUB, D_MODEL], F32R) for n in ("wd_hi", "wd_lo"))
        s_t, f_t = sb("s_t", [128, 364]), sb("f_t", [128, 364])
        f_hi, f_lo = (sb(n, [128, 2, SUB, NTOK], F32R) for n in ("f_hi", "f_lo"))
        gate_ps = [ps(f"gate_ps{i}", [128, 512]) for i in range(2)]
        up_ps = [ps(f"up_ps{i}", [128, 512]) for i in range(2)]
        d_ps = [ps(f"d_ps{i}", [128, 512]) for i in range(4)]
        landed = [sem(f"landed{i}") for i in range(2)]
        (hi_ready, lo_ready, unit_done, silu_ready, f_ready, f_hi_ready, f_lo_ready, down_done, added, zeroed,
         kept) = map(sem, ("hi_ready", "lo_ready", "unit_done", "silu_ready", "f_ready", "f_hi_ready", "f_lo_ready",
                           "down_done", "added", "zeroed", "kept"))
        piece = lambda g, e, p: 6 * g + 2 * e + p
        raw_gu = lambda p: raw[:, p, :].rearrange("q (k h n) -> q k h n", k=HK, h=2)

        def over_steps(eng, step):
            step(0, 0)
            with eng.Fori(0, (GROUPS - 3) // 2) as i:
                step(2 * i + 1, 1)
                step(2 * i + 2, 0)
            step(GROUPS - 2, 1)
            step(GROUPS - 1, 0)
            step(GROUPS, 1)

        with nc.Block() as block:

            @block.sync
            def _(sp):
                def load_gu(g, e, tile):
                    for p in range(2):
                        if not known(g, 0) or e > 0:
                            sp.wait_ge(lo_ready, piece(g, e, p) - 1)
                        for h in range(2):
                            sp.dma_start(raw_gu(p)[:, :, h, :],
                                         gu_v[p][:, :, bass.ds(tile * 128 + h * D_FF, 128)]).then_inc(landed[p], 16)

                def load_down(g, e, group):
                    for p in range(2):
                        sp.wait_ge(lo_ready, piece(g, e, p) - 1)
                        sp.dma_start(raw[:, p, :], A["w_down"][0, bass.ds((group * 2 + p) * 128, 128), :]).then_inc(landed[p], 16)

                def step(g, par):
                    if known(g, GROUPS):
                        load_down(GROUPS - 1, 2, GROUPS - 1)
                        return
                    if not known(g, 0):
                        load_down(g, 0, g - 1)
                    load_gu(g, 1, 2 * g + 1)
                    if not known(g, GROUPS - 1):
                        load_gu(g, 2, 2 * g + 2)

                load_gu(0, 0, 0)
                over_steps(sp, step)

            @block.gpsimd
            def _(pool):
                def copy_out(out, a):
                    pool.dma_start(out, a).then_inc(kept, 16)

                def step(g, par):
                    if known(g, GROUPS):
                        return
                    for u in range(UNITS):
                        if not known(g, 0):
                            rows = bass.ds(((g - 1) * UNITS + u) * (SHARE * WID), SHARE * WID)
                            past = bass.ds(((g - 1) * UNITS + u) * (SHARE * WID) + DEC_T * WID, SHARE * WID)
                            copy_out(keep(A["ks_sample"])[:, rows], keep(A["cache_k_win"])[:, past])
                            copy_out(keep(A["vs_sample"])[:, rows], keep(A["cache_v_win"])[:, past])
                        c, n = CHUNKS[u % 3]
                        cut = (slice(None), par, u // 3, slice(c, c + n))
                        pool.wait_ge(f_hi_ready, UNITS * g + u + 1)
                        pool.tensor_tensor(f_lo[cut], f_t[:, 0:n], f_hi[cut].bitcast(F32), ALU.subtract).then_inc(f_lo_ready, 1)

                pool.memset(acc[:, :, :], 0.0).then_inc(zeroed, 1)
                for n, (p_out, s_out) in enumerate((("k_prompt", "ks_sample"), ("v_prompt", "vs_sample"))):
                    cols = slice((5 + n) * WID, (6 + n) * WID)
                    copy_out(A[p_out][0, 0].rearrange("s h d -> s (h d)"), z[0:SEQ, cols])
                    copy_out(A[s_out][0, :, L - DEC_T:L].rearrange("b t h d -> b t (h d)"),
                             z[SEQ:NTOK, cols].rearrange("(b t) c -> b t c", b=DEC_B))
                over_steps(pool, step)
                pool.wait_ge(kept, 16 * (4 + 2 * (GROUPS - 1) * UNITS))

            @block.scalar
            def _(act):
                def split(dst, src, out, lap):
                    for p in dst:
                        act.wait_ge(landed[p], lap)
                        act.copy(out(p), src(p)).then_inc(hi_ready, 1)

                gu = lambda s: lambda p: gu_hi[:, s, HK * p:HK * p + HK]
                raw_wd = lambda p: raw[:, p, :]
                wd = lambda p: wd_hi[:, p, :]

                def unit(g, par, u):
                    c, n = CHUNKS[u % 3]
                    act.wait_ge(unit_done, UNITS * g + u + 1)
                    if not (known(g, 0) and u == 0):
                        act.wait_ge(f_ready, UNITS * g + u)
                    act.activation(s_t[:, 0:n], gate_ps[u % 2][:, 0:n], ACT.Silu).then_inc(silu_ready, 1)
                    act.wait_ge(f_ready, UNITS * g + u + 1)
                    act.copy(f_hi[:, par, u // 3, c:c + n], f_t[:, 0:n]).then_inc(f_hi_ready, 1)

                def step(g, par):
                    if known(g, GROUPS):
                        act.wait_ge(down_done, GROUP_D * g)
                        split((0, 1), raw_wd, wd, 80 * g)
                        return
                    if not known(g, 0):
                        act.wait_ge(down_done, GROUP_D * g)
                        split((0, 1), raw_wd, wd, 80 * g + 32)
                    unit(g, par, 0)
                    if not known(g, 0):
                        act.wait_ge(unit_done, UNITS * g)
                    split((0, 1), raw_gu, gu(1), 80 * g + 64)
                    unit(g, par, 1)
                    unit(g, par, 2)
                    for u in (3, 4):
                        if not known(g, GROUPS - 1):
                            act.wait_ge(unit_done, UNITS * g + 3)
                            split((u - 3,), raw_gu, gu(0), 80 * g + 96)
                        unit(g, par, u)
                    unit(g, par, 5)

                split((0, 1), raw_gu, gu(0), 32)
                over_steps(act, step)

            @block.vector
            def _(dve):
                dve.sem_inc(added, 4)

                def split(n, dst, src, hi, lo):
                    for p in dst:
                        dve.wait_ge(hi_ready, n + p + 1)
                        dve.tensor_tensor(lo(p), src(p), hi(p).bitcast(F32), ALU.subtract).then_inc(lo_ready, 1)

                raw_wd = lambda p: raw[:, p, :]
                wd = lambda t: lambda p: t[:, p, :]
                gu = lambda t, s: lambda p: t[:, s, HK * p:HK * p + HK]

                def unit(g, u):
                    c, n = CHUNKS[u % 3]
                    dve.wait_ge(silu_ready, UNITS * g + u + 1)
                    if not (known(g, 0) and u == 0):
                        dve.wait_ge(f_lo_ready, UNITS * g + u)
                    dve.tensor_tensor(f_t[:, 0:n], s_t[:, 0:n], up_ps[u % 2][:, 0:n], ALU.mult).then_inc(f_ready, 1)

                def add(g, par, first, count):
                    for j in range(first, first + count):
                        lo = 64 if j // 2 == PT else 0
                        cut = (slice(lo, 128), j // 2, slice(j % 2 * 512, j % 2 * 512 + 512))
                        dve.wait_ge(down_done, GROUP_D * g + j + 1)
                        dve.tensor_tensor(acc[cut], acc[cut], d_ps[(2 * (1 - par) + j) % 4][lo:128, :], ALU.add).then_inc(added, 1)

                def step(g, par):
                    if known(g, GROUPS):
                        split(piece(GROUPS - 1, 2, 0), (0, 1), raw_wd, wd(wd_hi), wd(wd_lo))
                        add(g, par, 0, GROUP_D)
                        return
                    if not known(g, 0):
                        split(piece(g, 0, 0), (0, 1), raw_wd, wd(wd_hi), wd(wd_lo))
                    unit(g, 0)
                    split(piece(g, 1, 0), (0, 1), raw_gu, gu(gu_hi, 1), gu(gu_lo, 1))
                    first = 0
                    for u in range(1, UNITS):
                        if u in (3, 4) and not known(g, GROUPS - 1):
                            split(piece(g, 2, 0), (u - 3,), raw_gu, gu(gu_hi, 0), gu(gu_lo, 0))
                        unit(g, u)
                        if not known(g, 0):
                            add(g, par, first, DOWN_AFTER[u])
                            first += DOWN_AFTER[u]

                split(0, (0, 1), raw_gu, gu(gu_hi, 0), gu(gu_lo, 0))
                dve.wait_ge(zeroed, 1)
                over_steps(dve, step)

            @block.tensor
            def _(pe):
                pe.sem_inc(down_done, GROUP_D)

                def unit(g, u):
                    s, (c, n) = u // 3, CHUNKS[u % 3]
                    if not known(g, 0) or u >= 2:
                        pe.wait_ge(f_ready, UNITS * g + u - 1)
                    for h, bank in enumerate((gate_ps, up_ps)):
                        for k in range(KT):
                            for m, (w, x) in enumerate(((gu_hi, h_hi), (gu_hi, h_lo), (gu_lo, h_hi))):
                                mm = pe.matmul(bank[u % 2][:, 0:n], w[:, s, k, h, :], x[:, k, c:c + n],
                                               start=(k, m) == (0, 0), stop=(k, m) == (KT - 1, 2))
                    mm.then_inc(unit_done, 1)

                def down(g, par, first, count):
                    for j in range(first, first + count):
                        end, col = min(j // 2 * 128 + 128, NTOK), j % 2 * 512
                        pe.wait_ge(added, GROUP_D * (g - 1) + j + 1)
                        for s in range(SUB):
                            for m, (x, w) in enumerate(((f_hi, wd_hi), (f_hi, wd_lo), (f_lo, wd_hi))):
                                mm = pe.matmul(d_ps[(2 * (1 - par) + j) % 4][:, :], x[:, 1 - par, s, end - 128:end],
                                               w[:, s, col:col + 512], start=(s, m) == (0, 0), stop=(s, m) == (SUB - 1, 2))
                        mm.then_inc(down_done, 1)

                def step(g, par):
                    if known(g, GROUPS):
                        pe.wait_ge(lo_ready, piece(GROUPS - 1, 2, 2))
                        pe.wait_ge(f_lo_ready, UNITS * g)
                        down(g, par, 0, GROUP_D)
                        return
                    first = 0
                    for u in range(UNITS):
                        if u == 0:
                            pe.wait_ge(lo_ready, 2 if known(g, 0) else piece(g, 0, 0))
                        if u == 3:
                            pe.wait_ge(lo_ready, piece(g, 2, 0))
                        unit(g, u)
                        if not known(g, 0) and DOWN_AFTER[u]:
                            if first == 0:
                                pe.wait_ge(lo_ready, piece(g, 1, 0))
                                pe.wait_ge(f_lo_ready, UNITS * g)
                            down(g, par, first, DOWN_AFTER[u])
                            first += DOWN_AFTER[u]

                over_steps(pe, step)


def final_norm(nc, A, x_mid, acc):
    with ExitStack() as ctx:
        sb = lambda n, s, d=F32: ctx.enter_context(nc.sbuf_tensor(n, s, d))
        sem = lambda n: nc.alloc_semaphore("p7_" + n)
        x_m, y = sb("x_m7", [128, 3, D_MODEL]), sb("y7", [128, 3, D_MODEL])
        scratch, g_post = sb("scratch7", [128, D_MODEL]), sb("g_post7", [128, D_MODEL])
        stat, mhalf = sb("stat7", [128, 3, TT]), sb("mhalf7", [128, 1])
        x_landed, y_stored = ([sem(f"{n}{i}") for i in range(3)] for n in ("x_landed", "y_stored"))
        g_landed, half_set, squared, mean_ready, rstd_ready, scaled, y_ready = map(
            sem, ("g_landed", "half_set", "squared", "mean_ready", "rstd_ready", "scaled", "y_ready"))
        rows = lambda t: slice(128 - tile_rows(t), 128)

        with nc.Block() as block:

            @block.sync
            def _(sp):
                sp.dma_start(g_post[:, :], A["g_post_ffn"][0].partition_broadcast(128)).then_inc(g_landed, 16)

                def store(t):
                    sp.wait_ge(y_ready, t + 1)
                    out = (A["y_prompt"][0, t * 128:t * 128 + 128, :] if t < PT
                           else A["y_sample"].rearrange("b t d -> (b t) d"))
                    sp.dma_start(out, y[rows(t), t % 3, :]).then_inc(y_stored[t % 3], 16)

                for t in range(TT):
                    if t >= 3:
                        store(t - 3)
                    sp.dma_start(x_m[rows(t), t % 3, :],
                                 x_mid[t * 128:t * 128 + tile_rows(t), :]).then_inc(x_landed[t % 3], 16)
                for t in range(TT - 3, TT):
                    store(t)
                for i in range(3):
                    sp.wait_ge(y_stored[i], 48)

            @block.gpsimd
            def _(pool):
                pool.memset(mhalf[:, :], -0.5).then_inc(half_set, 1)
                pool.wait_ge(half_set, 1)
                for t in range(TT):
                    if t == PT:
                        pool.wait_ge(rstd_ready, t)
                    pool.wait_ge(mean_ready, t + 1)
                    pool.tensor_tensor(stat[rows(t), 2, t:t + 1], stat[rows(t), 1, t:t + 1], mhalf[rows(t), :],
                                       ALU.pow).then_inc(rstd_ready, 1)

            @block.scalar
            def _(act):
                for t in range(TT):
                    if t >= 1:
                        act.wait_ge(squared, t)
                    act.activation(scratch[rows(t), :], acc[rows(t), t, :], ACT.Square,
                                   accum_out=stat[rows(t), 0, t:t + 1]).then_inc(squared, 1)

            @block.vector
            def _(dve):
                def mean(t):
                    dve.wait_ge(squared, t + 1)
                    dve.tensor_scalar(stat[rows(t), 1, t:t + 1], stat[rows(t), 0, t:t + 1], 1.0 / D_MODEL, EPS,
                                      ALU.mult, ALU.add).then_inc(mean_ready, 1)

                dve.wait_ge(g_landed, 16)
                mean(0)
                for t in range(TT):
                    if t + 1 < TT:
                        mean(t + 1)
                    dve.wait_ge(rstd_ready, t + 1)
                    if t >= 3:
                        dve.wait_ge(y_stored[t % 3], 16 * (t // 3))
                    dve.scalar_tensor_tensor(y[rows(t), t % 3, :], acc[rows(t), t, :], stat[rows(t), 2, t:t + 1],
                                             g_post[rows(t), :], ALU.mult, ALU.mult).then_inc(scaled, 1)
                    dve.wait_ge(scaled, t + 1)
                    dve.wait_ge(x_landed[t % 3], 16 * (t // 3) + 16)
                    dve.tensor_tensor(y[rows(t), t % 3, :], y[rows(t), t % 3, :], x_m[rows(t), t % 3, :],
                                      ALU.add).then_inc(y_ready, 1)


OUTPUTS = {
    "y_prompt": (1, SEQ, D_MODEL), "y_sample": (DEC_B, DEC_T, D_MODEL),
    "state_p": (1, 1, NH, HD, HD), "k_prompt": (1, 1, SEQ, NH, HD), "v_prompt": (1, 1, SEQ, NH, HD),
    "state_s": (1, DEC_B, NH, HD, HD), "ks_sample": (1, DEC_B, L, NH, HD), "vs_sample": (1, DEC_B, L, NH, HD),
}


def hymba_layer(nc, A):
    scratch = lambda n, s: nc.dram_tensor(n, s, F32, kind="Internal").ap()
    z, mix = scratch("z_scratch", [NTOK, ZC]), scratch("mix_scratch", [NTOK, D_MODEL])
    x_mid, tab = scratch("x_mid_scratch", [NTOK, D_MODEL]), scratch("tab_scratch", [NH, 128, TABW])
    with nc.sbuf_tensor("ident", [128, 128], F32) as ident:
        with nc.cleanup_on_exit():
            with nc.sbuf_tensor("h_hi", [128, KT, NTOK], F32R) as h_hi, \
                 nc.sbuf_tensor("h_lo", [128, KT, NTOK], F32R) as h_lo:
                in_projection(nc, A, z, h_hi, h_lo, ident)
        retention(nc, A, z, mix, ident, A["state_p"][0, 0], A["state_s"][0])
        with nc.sbuf_tensor("bias_s", [128, STILES * 128], F32) as bias_s:
            distance_tables(nc, A, tab, bias_s)
            prompt_attention(nc, A, z, mix, tab, ident)
            sample_attention(nc, A, z, mix, bias_s, ident)
        with nc.sbuf_tensor("h2_hi", [128, KT, NTOK], F32R) as h_hi, nc.sbuf_tensor("h2_lo", [128, KT, NTOK], F32R) as h_lo:
            out_projection(nc, A, mix, x_mid, h_hi, h_lo, ident)
            with nc.sbuf_tensor("acc", [128, TT, D_MODEL], F32) as acc:
                ffn(nc, A, z, h_hi, h_lo, acc)
                final_norm(nc, A, x_mid, acc)


def kernel(**inputs):
    import concourse.bacc as bacc
    from concourse.bass_utils import run_bass_kernel_spmd

    nc = bacc.Bacc("TRN2", target_bir_lowering=False, num_devices=1)
    arrays = {n: np.ascontiguousarray(a) for n, a in inputs.items()}
    arrays.update(shape_constants())
    A = {n: nc.dram_tensor(n, a.shape, mybir.dt.from_np(a.dtype), kind="ExternalInput").ap() for n, a in arrays.items()}
    for n, shape in OUTPUTS.items():
        A[n] = nc.dram_tensor(n, shape, F32, kind="ExternalOutput").ap()
    hymba_layer(nc, A)
    got = run_bass_kernel_spmd(nc, [arrays], core_ids=[0])
    return tuple(got.results[0][n] for n in OUTPUTS)
```

```python
import numpy as np
from contextlib import ExitStack

import concourse.bass as bass
from concourse import mybir

F32 = mybir.dt.float32
F32R = mybir.dt.float32r
ALU = mybir.AluOpType
ACT = mybir.ActivationFunctionType
AXX = mybir.AxisListType.X

D_MODEL, SEQ, DEC_B, DEC_T, PAST = 1024, 1024, 8, 8, 8192
HD, NH, NPAIR = 64, 8, 4
WID = NH * HD
ZC = 7 * WID
L = 2048
D_FF = 2816
NS = DEC_B * DEC_T
NTOK = SEQ + NS
KT = D_MODEL // 128
PT = SEQ // 128
TT = PT + 1
EPS, GN_EPS = 1e-6, 1e-5
NEG = -1e30
N_BUCKETS, MAX_DISTANCE = 32, 2048
WIDE, REST, STILES = 8, 1536, 11
TABW = 1152
TABC = 896 + 127


def t5_bucket(dist):
    me = N_BUCKETS // 2
    d = np.maximum(dist, 1).astype(np.float32)
    big = me + (np.log(d / np.float32(me)) / np.float32(np.log(MAX_DISTANCE / me))
                * np.float32(N_BUCKETS - me)).astype(np.int32)
    return np.where(dist < me, dist, np.minimum(big, N_BUCKETS - 1))


def pattern_rows(dist):
    d = np.asarray(dist)
    ok = d >= 0
    c = ((d <= 128).astype(int) + ((d <= 512) & (d % 4 == 0)) + ((d <= 2048) & (d % 16 == 0))) * ok
    rows = np.zeros((N_BUCKETS + 1,) + d.shape, np.float32)
    b = t5_bucket(np.maximum(d, 0))
    for n in range(N_BUCKETS):
        rows[n] = (b == n) & (c > 0)
    rows[N_BUCKETS] = np.where(c > 0, np.log(np.maximum(c, 1)), NEG)
    return rows


def shape_constants():
    c = {}
    f64 = np.float64
    inv = (10000.0 ** (-np.arange(0, HD, 2) / HD)).astype(np.float32)
    pos = np.zeros((TT, 128), np.float32)
    pos[:PT] = np.arange(SEQ).reshape(PT, 128)
    pos[PT, :NS] = PAST + np.arange(NS) % DEC_T
    ang = (pos[:, :, None] * inv[None, None, :]).astype(np.float32).astype(f64)
    rope = np.zeros((128, TT, 2, HD), np.float32)
    rope[:, :, 0] = np.concatenate([np.cos(ang), np.cos(ang)], -1).transpose(1, 0, 2)
    rope[:, :, 1] = np.concatenate([-np.sin(ang), np.sin(ang)], -1).transpose(1, 0, 2)
    c["c_rope"] = rope
    lg = np.log1p(-np.exp2(-5.0 - np.arange(NH))).astype(f64)
    i = np.arange(128)
    rel = i[None, :] - i[:, None]
    dec = np.where(rel[None] >= 0, np.exp(np.maximum(rel, 0)[None] * lg[:, None, None]), 0) / 8
    c["c_decay"] = dec.transpose(1, 0, 2).astype(np.float32)
    cross = np.exp((i + 1)[None, :] * lg[:, None])
    pairs = np.repeat(lg.reshape(NPAIR, 2).T, HD, 0)
    c["c_cross"] = np.exp(pairs[:, :, None] * (i + 1)).astype(np.float32)
    c["c_kdec"] = (np.exp((127 - i)[:, None] * lg[None]) / 8).astype(np.float32)
    c["c_chunk"] = np.exp(128 * pairs).astype(np.float32)
    n = np.arange(NS)
    same = (n[:, None] // DEC_T == n[None, :] // DEC_T)
    rs = n[None, :] - n[:, None]
    c["c_decay_s"] = (np.where(same & (rs >= 0), np.exp(np.maximum(rs, 0)[None] * lg[:, None, None]), 0)
                      / 8).transpose(1, 0, 2).astype(np.float32)
    c["c_cross_s"] = np.exp(pairs[:, :, None] * (n % DEC_T + 1)).astype(np.float32)
    c["c_kdec_s"] = (np.exp((DEC_T - 1 - n % DEC_T)[:, None] * lg[None]) / 8).astype(np.float32)
    c["c_chunk_s"] = np.exp(DEC_T * pairs).astype(np.float32)
    c["c_bmask"] = (n[:, None] // DEC_T == np.arange(DEC_B)[None]).astype(np.float32)
    c["c_ident"] = np.eye(128, dtype=np.float32)
    c["c_dist_p"] = pattern_rows(TABC - np.arange(TABW))
    p = np.arange(128)
    rows = [16 * p + j for j in range(WIDE)]
    rows += [REST + 16 * (p // 4) + 8 + 2 * (p % 4) + j for j in range(2)]
    rows += [np.where(p < DEC_T, L + p, 10 * L)]
    rows = np.stack(rows)
    dist = L + np.arange(DEC_T)[None, :, None] - rows[:, None, :]
    by_t = np.zeros((9, N_BUCKETS + 1, STILES * 128), np.float32)
    by_t[:DEC_T] = pattern_rows(dist.transpose(1, 0, 2)).reshape(N_BUCKETS + 1, DEC_T, -1).transpose(1, 0, 2)
    c["c_dist_s"] = by_t.reshape(3, 3 * (N_BUCKETS + 1), -1).transpose(1, 0, 2)
    c["c_whose"] = np.repeat(np.eye(3, dtype=np.float32), N_BUCKETS + 1, 0)
    row = np.arange(128)
    c["c_own"] = (row[:, None] % (NH * DEC_T) // DEC_T == np.arange(WID)[None] // HD).astype(np.float32)
    c["c_sum_t"] = (row[:, None] % DEC_T == row[None]).astype(np.float32)
    return {k: np.ascontiguousarray(v) for k, v in c.items()}


EARLY_ROWS, EARLY_COPIES = 720, 18


def copy_windows(eng, A, kept, row, n):
    flat = lambda name: A[name][0].rearrange("b l h d -> b (l h d)")
    for new, old in (("ks_sample", "cache_k_win"), ("vs_sample", "cache_v_win")):
        eng.dma_start(flat(new)[:, bass.ds(row * WID, n * WID)],
                      flat(old)[:, bass.ds(row * WID + DEC_T * WID, n * WID)]).then_inc(kept, 16)


def tile_rows(t):
    return 128 if t < PT else NS


def spread(ap, shape):
    return ap.unsqueeze(2).broadcast_to(shape)


def known(t, value):
    return isinstance(t, int) and t == value


def in_projection(nc, A, z, h_hi, h_lo, ident, kept):
    GROUPS = ZC // WID
    HK = KT // 2
    w_v = A["w_in"][0].rearrange("(q k p) n -> q p k n", q=2, p=128)
    x_v = [A["x_prompt"][0, t * 128:(t + 1) * 128, :] for t in range(PT)]
    x_v.append(A["x_sample"].rearrange("b t d -> (b t) d"))
    with ExitStack() as ctx:
        sb = lambda n, s, d=F32: ctx.enter_context(nc.sbuf_tensor(n, s, d))
        ps = lambda n, s: ctx.enter_context(nc.psum_tensor(n, s, F32))
        sem = lambda n: nc.alloc_semaphore("p1_" + n)
        w_raw = sb("w_raw", [128, 2, HK, WID])
        w_hi, w_lo = sb("w_hi", [128, 2, KT, WID], F32R), sb("w_lo", [128, 2, KT, WID], F32R)
        xt = sb("xt", [128, 2, D_MODEL])
        xn = sb("xn", [128, 2, D_MODEL])
        hg = sb("hg", [128, 2, HK, 128])
        g_rows, gT = sb("g_rows", [KT, 128]), sb("gT", [128, KT])
        stat, mhalf = sb("stat", [128, 3, TT]), sb("mhalf", [128, 1])
        z_out = sb("z_out", [128, 3, WID])
        t_ps = [ps(f"t_ps{i}", [128, HK, 128]) for i in range(2)]
        z_ps = [ps(f"z_ps{i}", [128, WID]) for i in range(3)]
        x_landed = [sem(f"x_landed{i}") for i in range(2)]
        w_landed = [sem(f"w_landed{i}") for i in range(2)]
        g_landed, i_landed, g_turned, g_ready = map(sem, ("g_landed", "i_landed", "g_turned", "g_ready"))
        half_set, squared, mean_ready, rstd_ready, xn_ready = map(
            sem, ("half_set", "squared", "mean_ready", "rstd_ready", "xn_ready"))
        turned, hg_ready, hi_ready, lo_ready = map(sem, ("turned", "hg_ready", "hi_ready", "lo_ready"))
        w_hi_ready, w_lo_ready = sem("w_hi_ready"), sem("w_lo_ready")
        z_done, z_evac = sem("z_done"), sem("z_evac")
        z_stored = [sem(f"z_stored{i}") for i in range(3)]

        with nc.Block() as block:

            @block.sync
            def _(sp):
                def load_weights(c):
                    for q in range(2):
                        if not isinstance(c, int) or c > 0:
                            sp.wait_ge(w_lo_ready, 2 * c + q - 1)
                        sp.dma_start(w_raw[:, q], w_v[q][:, :, bass.ds(c * WID, WID)]).then_inc(w_landed[q], 16)

                def store_z(c, t):
                    n = tile_rows(t)
                    sp.wait_ge(z_evac, TT * c + t + 1)
                    sp.dma_start(z[t * 128:t * 128 + n, bass.ds(c * WID, WID)],
                                 z_out[128 - n:128, t % 3, :]).then_inc(z_stored[t % 3], 16)

                sp.dma_start(xt[:, 0, :], x_v[0]).then_inc(x_landed[0], 16)
                sp.dma_start(ident[:, :], A["c_ident"]).then_inc(i_landed, 16)
                sp.dma_start(g_rows[:, :], A["g_pre_mix"][0].rearrange("(k p) -> k p", p=128)).then_inc(g_landed, 16)
                sp.dma_start(xt[:, 1, :], x_v[1]).then_inc(x_landed[1], 16)
                load_weights(0)
                for t in range(2, TT):
                    sp.wait_ge(xn_ready, t - 1)
                    sp.dma_start(xt[0:tile_rows(t), t % 2, :], x_v[t]).then_inc(x_landed[t % 2], 16)
                    if t == 4:
                        load_weights(1)
                    if t >= 4:
                        store_z(0, t - 4)
                for t in range(TT - 4, TT):
                    store_z(0, t)
                with sp.Fori(1, GROUPS - 1) as c:
                    load_weights(c + 1)
                    for t in range(TT):
                        store_z(c, t)
                for t in range(TT):
                    store_z(GROUPS - 1, t)
                for m in range(3):
                    sp.wait_ge(z_stored[m], 16 * 3 * GROUPS)

            @block.gpsimd
            def _(pool):
                pool.memset(mhalf[:, :], -0.5).then_inc(half_set, 1)
                pool.wait_ge(half_set, 1)

                def rstd(t):
                    n = tile_rows(t)
                    pool.wait_ge(mean_ready, t + 1)
                    pool.tensor_tensor(stat[0:n, 2, t:t + 1], stat[0:n, 1, t:t + 1], mhalf[0:n, :],
                                       ALU.pow).then_inc(rstd_ready, 1)

                rstd(0)
                for t in range(TT):
                    if t + 1 < TT:
                        rstd(t + 1)
                    n = tile_rows(t)
                    for q in range(2):
                        pool.wait_ge(hi_ready, 2 * t + q + 1)
                        cut = (slice(None), slice(HK * q, HK * q + HK), slice(t * 128, t * 128 + n))
                        pool.tensor_tensor(h_lo[cut], hg[:, q, :, 0:n], h_hi[cut].bitcast(F32),
                                           ALU.subtract).then_inc(lo_ready, 1)
                share = EARLY_ROWS // EARLY_COPIES
                with pool.Fori(1, GROUPS) as c:
                    for n in range(3):
                        pool.wait_ge(z_done, TT * c + 3 * n - 4)
                        copy_windows(pool, A, kept, (3 * (c - 1) + n) * share, share)

            @block.scalar
            def _(act):
                def square(t):
                    n = tile_rows(t)
                    act.wait_ge(x_landed[t % 2], 16 * (t // 2 + 1))
                    if t >= 2:
                        act.wait_ge(turned, 2 * (t - 1))
                    act.activation(xn[0:n, t % 2, :], xt[0:n, t % 2, :], ACT.Square,
                                   accum_out=stat[0:n, 0, t:t + 1]).then_inc(squared, 1)

                def split_weights(c, par, q):
                    act.wait_ge(w_landed[q], 16 * c + 16)
                    if not isinstance(c, int) or c >= 2:
                        act.wait_ge(z_done, TT * c - TT)
                    act.copy(w_hi[:, par, HK * q:HK * q + HK, :], w_raw[:, q]).then_inc(w_hi_ready, 1)

                def evacuate(c, t):
                    n = tile_rows(t)
                    act.wait_ge(z_done, TT * c + t + 1)
                    if not isinstance(c, int) or c > 0 or t >= 3:
                        act.wait_ge(z_stored[t % 3], 48 * c + 16 * (t // 3))
                    act.copy(z_out[128 - n:128, t % 3, :], z_ps[t % 3][128 - n:128, :]).then_inc(z_evac, 1)

                def group(c, par, last=False):
                    for t in range(TT):
                        evacuate(c, t)
                        if not last and t in (1, 4):
                            split_weights(c + 1, 1 - par, t // 4)

                square(0)
                square(1)
                split_weights(0, 0, 0)
                split_weights(0, 0, 1)
                for t in range(TT):
                    n = tile_rows(t)
                    for q in range(2):
                        act.wait_ge(hg_ready, 2 * t + q + 1)
                        act.copy(h_hi[:, HK * q:HK * q + HK, t * 128:t * 128 + n],
                                 hg[:, q, :, 0:n]).then_inc(hi_ready, 1)
                    if t + 2 < TT:
                        square(t + 2)
                    if t >= 1:
                        evacuate(0, t - 1)
                    if t in (4, 6):
                        split_weights(1, 1, t // 5)
                evacuate(0, TT - 1)
                with act.Fori(0, (GROUPS - 3) // 2) as i:
                    group(2 * i + 1, 1)
                    group(2 * i + 2, 0)
                group(GROUPS - 2, 1)
                group(GROUPS - 1, 0, last=True)

            @block.vector
            def _(dve):
                def normalise(t):
                    n = tile_rows(t)
                    dve.wait_ge(squared, t + 1)
                    dve.tensor_scalar(stat[0:n, 1, t:t + 1], stat[0:n, 0, t:t + 1], 1.0 / D_MODEL, EPS,
                                      ALU.mult, ALU.add).then_inc(mean_ready, 1)
                    dve.wait_ge(rstd_ready, t + 1)
                    dve.tensor_scalar(xn[0:n, t % 2, :], xt[0:n, t % 2, :], stat[0:n, 2, t:t + 1], None,
                                      ALU.mult).then_inc(xn_ready, 1)

                def split_weights(c, par, q):
                    dve.wait_ge(w_hi_ready, 2 * c + q + 1)
                    cut = (slice(None), par, slice(HK * q, HK * q + HK))
                    dve.tensor_tensor(w_lo[cut], w_raw[:, q], w_hi[cut].bitcast(F32),
                                      ALU.subtract).then_inc(w_lo_ready, 1)

                normalise(0)
                dve.wait_ge(g_turned, 1)
                dve.tensor_copy(gT[:, :], t_ps[1][:, 0, 0:KT]).then_inc(g_ready, 1)
                dve.wait_ge(g_ready, 1)
                for t in range(TT):
                    n = tile_rows(t)
                    if t + 1 < TT:
                        normalise(t + 1)
                    for q in range(2):
                        dve.wait_ge(turned, 2 * t + q + 1)
                        if t >= 1:
                            dve.wait_ge(lo_ready, 2 * t + q - 1)
                        dve.tensor_tensor(hg[:, q, :, 0:n], t_ps[q][:, :, 0:n],
                                          spread(gT[:, HK * q:HK * q + HK], [128, HK, n]),
                                          ALU.mult).then_inc(hg_ready, 1)
                    if t == 0:
                        split_weights(0, 0, 0)
                        split_weights(0, 0, 1)
                    if t in (4, 6):
                        split_weights(1, 1, t // 5)
                with dve.Fori(0, (GROUPS - 3) // 2) as i:
                    for par in (0, 1):
                        for q in range(2):
                            split_weights(2 * i + 2 + par, par, q)
                for q in range(2):
                    split_weights(GROUPS - 1, 0, q)

            @block.tensor
            def _(pe):
                def turn(t):
                    n = tile_rows(t)
                    pe.wait_ge(xn_ready, t + 1)
                    for q in range(2):
                        if t >= 1:
                            pe.wait_ge(hg_ready, 2 * t + q - 1)
                        for k in range(HK):
                            col = (HK * q + k) * 128
                            mm = pe.transpose(t_ps[q][:, k, 0:n], xn[0:n, t % 2, col:col + 128], ident[0:n, 0:n])
                        mm.then_inc(turned, 1)

                def project(c, par, t):
                    if not isinstance(c, int) or c > 0 or t >= 3:
                        pe.wait_ge(z_evac, TT * c + t - 2)
                    end = t * 128 + tile_rows(t)
                    first, last = (0, 0), (KT - 1, 2)
                    for k in range(KT):
                        for n, (x, w) in enumerate(((h_hi, w_hi), (h_hi, w_lo), (h_lo, w_hi))):
                            mm = pe.matmul(z_ps[t % 3][:, :], x[:, k, end - 128:end], w[:, par, k, :],
                                           start=(k, n) == first, stop=(k, n) == last)
                    mm.then_inc(z_done, 1)

                pe.wait_ge(i_landed, 16)
                pe.wait_ge(g_landed, 16)
                pe.transpose(t_ps[1][:, 0, 0:KT], g_rows[:, :], ident[0:KT, 0:KT]).then_inc(g_turned, 1)
                pe.wait_ge(g_ready, 1)
                turn(0)
                for t in range(TT):
                    if t + 1 < TT:
                        turn(t + 1)
                    pe.wait_ge(lo_ready, 2 * t + 2)
                    if t == 0:
                        pe.wait_ge(w_lo_ready, 2)
                    project(0, 0, t)
                with pe.Fori(0, (GROUPS - 1) // 2) as i:
                    for par in (1, 0):
                        c = 2 * i + 2 - par
                        pe.wait_ge(w_lo_ready, 2 * c + 2)
                        for t in range(TT):
                            project(c, par, t)


def by(t):
    return t + 2


def diagonal(t4, par):
    return t4[HD * par:HD * par + HD, :, HD * par:HD * par + HD]


class DistanceTables:
    K, W, KEYS = N_BUCKETS + 1, TABW // 3, STILES * 128
    rows = staticmethod(lambda g: 66 if g == 2 else 99)

    def __init__(self, nc, ctx, A, tab, bias_p, bias_s):
        sb = lambda n, s, d=F32: ctx.enter_context(nc.sbuf_tensor(n, s, d))
        sem = lambda n: nc.alloc_semaphore("p0_" + n)
        self.A, self.tab, self.bias_p, self.bias_s = A, tab, bias_p, bias_s
        self.rel = sb("rel", [3 * self.K, NH])
        self.whose = sb("whose", [3 * self.K, 3])
        self.rel_t = sb("rel_t", [3 * self.K, 3, 2, NH, DEC_T])
        self.dist_p, self.dist_s = sb("dist_p", [self.K, TABW]), sb("dist_s", [3 * self.K, 3, self.KEYS])
        self.row = sb("row", [NH, TABW])
        self.ps = ctx.enter_context(nc.psum_tensor("table_ps", [128, 512], F32))
        (self.landed, self.samples_landed, self.ones_set, self.rel_t_ready, self.row_done, self.row_ready,
         self.bias_done, self.bias_ready, self.stored, self.bias_landed) = map(
            sem, ("landed", "samples_landed", "ones_set", "rel_t_ready", "row_done", "row_ready", "bias_done",
                  "bias_ready", "stored", "bias_landed"))

    def load(self, sp):
        sp.wait_ge(self.ones_set, 1)
        for n in range(3):
            sp.dma_start(self.rel[n * self.K:n * self.K + N_BUCKETS, :], self.A["rel_bias"]).then_inc(self.landed, 16)
        sp.dma_start(self.whose[:, :], self.A["c_whose"]).then_inc(self.landed, 16)
        sp.dma_start(self.dist_p[:, :], self.A["c_dist_p"]).then_inc(self.landed, 16)

    def load_samples(self, sp):
        sp.dma_start(self.dist_s[:, :, :], self.A["c_dist_s"]).then_inc(self.samples_landed, 16)

    def spread_rows(self, eng):
        eng.wait_ge(self.row_ready, 3)
        eng.dma_start(self.tab, self.row[:, :].unsqueeze(1).broadcast_to([NH, 128, TABW])).then_inc(self.stored, 16)

    def load_bias(self, eng):
        eng.wait_ge(self.stored, 16)
        for h in range(NH):
            eng.dma_start(self.bias_p[:, h, :], bass.AP(tensor=self.tab.tensor, offset=h * 128 * TABW + 127,
                                                        ap=[[TABW - 1, 128], [1, SEQ]])).then_inc(self.bias_landed, 16)

    def finish(self, sp):
        sp.wait_ge(self.bias_landed, 16 * NH)

    def clear(self, dve):
        dve.memset(self.rel[:, :], 1.0).then_inc(self.ones_set, 1)
        dve.memset(self.rel_t[:, :, :, :, :], 0.0).then_inc(self.ones_set, 1)

    def build_rows(self, dve):
        dve.wait_ge(self.landed, 80)
        dve.wait_ge(self.ones_set, 2)
        for g in range(3):
            n = min(3, DEC_T - 3 * g)
            shape = [3 * self.K, 2, NH, n]
            dve.tensor_tensor(self.rel_t[:, g, :, :, 3 * g:3 * g + n],
                              self.rel[:, :].unsqueeze(1).unsqueeze(3).broadcast_to(shape),
                              self.whose[:, 0:n].unsqueeze(1).unsqueeze(1).broadcast_to(shape), ALU.mult).then_inc(self.rel_t_ready, 1)
        for n in range(3):
            dve.wait_ge(self.row_done, n + 1)
            dve.tensor_copy(self.row[:, n * self.W:(n + 1) * self.W], self.ps[0:NH, 0:self.W]).then_inc(self.row_ready, 1)

    def build_samples(self, dve, n):
        dve.wait_ge(self.bias_done, n + 1)
        w = min(512, self.KEYS - 512 * n)
        dve.tensor_copy(self.bias_s[:, 512 * n:512 * n + w], self.ps[:, 0:w]).then_inc(self.bias_ready, 1)

    def row_products(self, pe):
        pe.wait_ge(self.landed, 80)
        for n in range(3):
            if n:
                pe.wait_ge(self.row_ready, n)
            pe.matmul(self.ps[0:NH, 0:self.W], self.rel[0:self.K, :], self.dist_p[:, n * self.W:(n + 1) * self.W],
                      start=True, stop=True).then_inc(self.row_done, 1)

    def sample_products(self, pe, n):
        w = min(512, self.KEYS - 512 * n)
        if n == 0:
            pe.wait_ge(self.samples_landed, 16)
            pe.wait_ge(self.rel_t_ready, 3)
            pe.wait_ge(self.row_ready, 3)
        else:
            pe.wait_ge(self.bias_ready, n)
        for g in range(3):
            k = self.rows(g)
            mm = pe.matmul(self.ps[:, 0:w], self.rel_t[0:k, g].rearrange("n c h t -> n (c h t)"),
                           self.dist_s[0:k, g, 512 * n:512 * n + w], start=(g == 0), stop=(g == 2))
        mm.then_inc(self.bias_done, 1)


def retention(nc, A, z, mix, ident, state_p, state_s, tab, bias_p, bias_s, ahead):
    with ExitStack() as ctx:
        sb = lambda n, s, d=F32: ctx.enter_context(nc.sbuf_tensor(n, s, d))
        ps = lambda n, s: ctx.enter_context(nc.psum_tensor(n, s, F32))
        sem = lambda n: nc.alloc_semaphore("p2_" + n)
        zr = sb("zr", [128, 2, 4, NH, HD])
        rope = sb("rope", [128, TT, 2, HD])
        decay, cross = sb("decay", [128, NH, 128]), sb("cross", [128, NPAIR, 128])
        kdec, chunk = sb("kdec", [128, NH]), sb("chunk", [128, NPAIR])
        decay_s, cross_s = sb("decay_s", [NS, NH, NS]), sb("cross_s", [128, NPAIR, NS])
        kdec_s, chunk_s = sb("kdec_s", [NS, NH]), sb("chunk_s", [128, NPAIR])
        bmask = sb("bmask", [NS, DEC_B])
        g_row = sb("g_row", [128, WID])
        t1, t2 = sb("t1", [128, 2 * NH, HD]), sb("t2", [128, 2 * NH, HD])
        qk = sb("qk", [128, 2 * NH, HD])
        qT = sb("qT2", [128, NPAIR, 128])
        kT = sb("kT2", [128, 2, NPAIR, 128])
        qd = sb("qd", [128, NPAIR, 128])
        kd = sb("kd", [128, NH, HD])
        inT = sb("inT", [128, 2, NPAIR, 128])
        S = sb("S", [128, 2, NPAIR, 128])
        Sg = sb("Sg", [128, NPAIR, 128])
        swish, gate = sb("swish", [128, WID]), sb("gate", [128, WID])
        oc, sq, on = (sb(n, [128, NH, HD]) for n in ("oc", "sq", "on"))
        stat, mhalf = sb("stat2", [128, 5, NH]), sb("mhalf2", [128, NH])
        mixr = sb("mixr", [128, 2, WID])
        S_in = sb("S_in", [128, DEC_B, NPAIR, 128])
        S_out = sb("S_out", [128, DEC_B, NPAIR, HD])
        qdm = sb("qdm", [128, NPAIR, DEC_B * NS])
        vm = sb("vm", [NS, DEC_B, WID])
        qk_ps = [ps(f"qk_ps{i}", [128, NPAIR, 128]) for i in range(2)]
        in_ps = [ps(f"in_ps{i}", [128, NPAIR, 128]) for i in range(2)]
        o_ps, su_ps = ps("o_ps", [128, NH, HD]), ps("su_ps", [128, NPAIR, 128])

        qk_landed, vg_landed = ([sem(f"{n}_landed{i}") for i in range(2)] for n in ("qk", "vg"))
        rope_landed, tab_landed, state_landed = map(sem, ("rope_landed", "tab_landed", "state_landed"))
        names = ("t1_ready", "qk_ready", "qk_turned", "qkT_ready", "qd_ready", "kd_ready", "inner_done",
                 "inT_ready", "update_done", "S_ready", "Sg_ready", "o_done", "swish_ready", "gate_ready",
                 "oc_ready", "sq_ready", "var_ready", "rstd_ready", "on_ready", "mix_ready")
        (t1_ready, qk_ready, qk_turned, qkT_ready, qd_ready, kd_ready, inner_done, inT_ready, update_done,
         S_ready, Sg_ready, o_done, swish_ready, gate_ready, oc_ready, sq_ready, var_ready, rstd_ready,
         on_ready, mix_ready) = map(sem, names)
        cleared, dve_step, vm_ready, sout_ready = map(sem, ("cleared", "dve_step", "vm_ready", "sout_ready"))
        mix_stored = [sem(f"mix_stored{i}") for i in range(2)]
        state_stored = sem("state_stored")
        TABS, SAMPLE = 10, PT
        tables = DistanceTables(nc, ctx, A, tab, bias_p, bias_s)

        def over_tiles(eng, step):
            step(0, 0)
            with eng.Fori(0, PT // 2 - 1) as i:
                step(2 * i + 1, 1, i)
                step(2 * i + 2, 0, i)
            step(PT - 1, 1, PT // 2 - 1)

        def lap(t, par, i):
            return 16 if known(t, 0) else 16 * i + 32 - 16 * par

        def next_lap(t, i):
            return 16 if known(t, 0) else 16 * i + 32

        def one_sequence(eng, b):
            shape = [NS, b.stop - b.start, WID]
            eng.wait_ge(vg_landed[0], 16 * PT // 2 + 16)
            eng.tensor_tensor(vm[:, b, :], zr[0:NS, 0, 2].rearrange("p h d -> p (h d)").unsqueeze(1).broadcast_to(shape),
                              spread(bmask[:, b], shape), ALU.mult).then_inc(vm_ready, 1)

        with nc.Block() as block:

            @block.sync
            def _(sp):
                def load_qk(t, par, rows=128):
                    sp.dma_start(zr[0:rows, par, 0:2].rearrange("p a h d -> p (a h d)"),
                                 z[bass.ds(t * 128, rows), 0:2 * WID]).then_inc(qk_landed[par], 16)

                def load_vg(t, par, rows=128):
                    sp.dma_start(zr[0:rows, par, 2:4].rearrange("p a h d -> p (a h d)"),
                                 z[bass.ds(t * 128, rows), 2 * WID:4 * WID]).then_inc(vg_landed[par], 16)

                def store(t, par, rows=128):
                    sp.wait_ge(mix_ready, by(t))
                    sp.dma_start(mix[bass.ds(t * 128, rows), 0:WID], mixr[0:rows, par, :]).then_inc(mix_stored[par], 16)

                load_qk(0, 0)
                sp.dma_start(rope[:, :, :, :], A["c_rope"]).then_inc(rope_landed, 16)
                for dst, name in ((kdec, "c_kdec"), (cross, "c_cross"), (decay, "c_decay"), (chunk, "c_chunk"),
                                  (decay_s, "c_decay_s"), (cross_s, "c_cross_s"), (kdec_s, "c_kdec_s"),
                                  (chunk_s, "c_chunk_s"), (bmask, "c_bmask")):
                    sp.dma_start(dst[:], A[name]).then_inc(tab_landed, 16)
                sp.dma_start(g_row[:, :], A["g_ret"][0].rearrange("h d -> (h d)").partition_broadcast(128)).then_inc(tab_landed, 16)
                load_qk(1, 1)
                load_vg(0, 0)
                load_vg(1, 1)
                tables.load(sp)
                sp.wait_ge(cleared, 5)
                for par in range(2):
                    sp.dma_start(S_in[HD * par:HD * par + HD, :, :, HD * par:HD * par + HD],
                                 A["state_ret"][0].rearrange("b (p r) d e -> r d b p e", r=2)[par]).then_inc(state_landed, 16)

                def step(t, par):
                    if not known(t, PT - 1):
                        sp.wait_ge(qk_ready, by(t))
                        load_qk(t + 2, par, NS if known(t, SAMPLE - 2) else 128)
                    if not known(t, 0):
                        store(t - 1, 1 - par)
                        load_vg(t + 1, 1 - par, NS if known(t, SAMPLE - 1) else 128)

                tables.load_samples(sp)
                step(0, 0)
                with sp.Fori(0, PT // 2 - 2) as i:
                    step(2 * i + 1, 1)
                    step(2 * i + 2, 0)
                for t in range(PT - 3, PT):
                    step(t, t % 2)
                store(PT - 1, 1)
                ahead(sp)
                for par in range(2):
                    sp.dma_start(state_p.rearrange("(p r) d e -> r d p e", r=2)[par],
                                 diagonal(S[:, PT % 2], par)).then_inc(state_stored, 16)
                store(SAMPLE, 0, NS)
                sp.wait_ge(sout_ready, 8)
                for par in range(2):
                    sp.dma_start(state_s.rearrange("b (p r) d e -> r d b p e", r=2)[par],
                                 S_out[HD * par:HD * par + HD]).then_inc(state_stored, 16)
                tables.finish(sp)
                sp.wait_ge(state_stored, 64)
                sp.wait_ge(mix_stored[0], 96)
                sp.wait_ge(mix_stored[1], 80)

            @block.gpsimd
            def _(pool):
                for s in (t1_ready, kd_ready, gate_ready, Sg_ready, rstd_ready, on_ready):
                    pool.sem_inc(s, 1)
                pool.memset(mhalf[:, :], -0.5).then_inc(cleared, 1)
                pool.memset(S[:, :, :, :], 0.0).then_inc(cleared, 1)
                pool.memset(kT[:, :, :, :], 0.0).then_inc(cleared, 1)
                pool.wait_ge(rope_landed, 16)

                def cosine(t, par, lap):
                    pool.wait_ge(qk_landed[par], lap)
                    pool.wait_ge(qk_ready, by(t - 1))
                    pool.tensor_tensor(t1[:, :, :], zr[:, par, 0:2].rearrange("p a h d -> p (a h) d"),
                                       rope[:, t, 0, :].unsqueeze(1).broadcast_to([128, 2 * NH, HD]),
                                       ALU.mult).then_inc(t1_ready, 1)

                def decayed_keys(t, rows, kdec):
                    pool.wait_ge(qk_ready, by(t))
                    pool.wait_ge(update_done, by(t - 1))
                    pool.tensor_tensor(kd[0:rows], qk[0:rows, NH:2 * NH, :], spread(kdec[:, :], [rows, NH, HD]),
                                       ALU.mult).then_inc(kd_ready, 1)

                def decayed_state(t, par):
                    pool.wait_ge(S_ready, by(t - 1))
                    pool.tensor_tensor(Sg[:, :, :], S[:, par], spread(chunk[:, :], [128, NPAIR, 128]),
                                       ALU.mult).then_inc(Sg_ready, 1)

                def gain(t):
                    pool.wait_ge(swish_ready, by(t))
                    pool.wait_ge(mix_ready, by(t - 1))
                    pool.tensor_tensor(gate[:, :], swish[:, :], g_row[:, :], ALU.mult).then_inc(gate_ready, 1)

                def late(t):
                    pool.wait_ge(var_ready, by(t))
                    pool.tensor_tensor(stat[:, 4, :], stat[:, 3, :], mhalf[:, :], ALU.pow).then_inc(rstd_ready, 1)
                    pool.wait_ge(rstd_ready, by(t))
                    pool.tensor_tensor(on[:, :, :], oc[:, :, :], spread(stat[:, 4, :], [128, NH, HD]),
                                       ALU.mult).then_inc(on_ready, 1)

                cosine(0, 0, 16)
                pool.memset(qdm[:, :, :], 0.0).then_inc(cleared, 1)
                pool.memset(S_in[:, :, :, :], 0.0).then_inc(cleared, 1)
                tables.spread_rows(pool)
                pool.wait_ge(tab_landed, 16 * TABS)

                def step(t, par, i=0):
                    decayed_keys(t, 128, kdec)
                    cosine(t + 1, 1 - par, next_lap(t, i))
                    decayed_state(t, par)
                    if not known(t, 0):
                        gain(t - 1)
                        late(t - 1)

                over_tiles(pool, step)
                decayed_keys(SAMPLE, NS, kdec_s)
                gain(PT - 1)
                late(PT - 1)
                one_sequence(pool, slice(DEC_B // 2 + 1, DEC_B))
                gain(SAMPLE)
                late(SAMPLE)

            @block.scalar
            def _(act):
                for s in (swish_ready, qkT_ready, sq_ready):
                    act.sem_inc(s, 1)
                for s in mix_stored:
                    act.sem_inc(s, 16)
                act.wait_ge(cleared, 3)

                def swish_gate(t, par, lap):
                    act.wait_ge(vg_landed[par], lap)
                    act.wait_ge(gate_ready, by(t - 1))
                    act.activation(swish[:, :], zr[:, par, 3].rearrange("p h d -> p (h d)"), ACT.Silu).then_inc(swish_ready, 1)

                def evacuate(t, rows):
                    act.wait_ge(qk_turned, by(t))
                    act.wait_ge(inner_done, by(t - 1))
                    act.wait_ge(qd_ready, by(t - 1))
                    act.copy(qT[:, :, 0:rows], qk_ps[0][:, :, 0:rows])
                    for r in range(2):
                        d = slice(HD * r, HD * r + HD)
                        x = act.copy(kT[d, r, :, 0:rows], qk_ps[1][d, :, 0:rows])
                    x.then_inc(qkT_ready, 1)

                def square(t):
                    act.wait_ge(oc_ready, by(t))
                    act.activation(sq[:, :, :], oc[:, :, :], ACT.Square).then_inc(sq_ready, 1)

                def step(t, par, i=0):
                    evacuate(t, 128)
                    if not known(t, 0):
                        square(t - 1)
                    swish_gate(t, par, lap(t, par, i))

                over_tiles(act, step)
                tables.load_bias(act)
                evacuate(SAMPLE, NS)
                square(PT - 1)
                swish_gate(SAMPLE, 0, 16 * PT // 2 + 16)
                square(SAMPLE)

            @block.vector
            def _(dve):
                for s in (qk_ready, qd_ready, inT_ready, S_ready, oc_ready, var_ready, mix_ready):
                    dve.sem_inc(s, 1)
                dve.sem_inc(dve_step, 1)
                dve.wait_ge(rope_landed, 16)

                def rotate(t, par, lap, steps):
                    dve.wait_ge(qk_landed[par], lap)
                    dve.wait_ge(qk_ready, by(t - 1))
                    x = zr[:, par, 0:2].rearrange("p a h d -> p (a h) d")
                    for a, b in ((0, 32), (32, 0)):
                        dve.tensor_tensor(t2[:, :, a:a + 32], x[:, :, b:b + 32],
                                          rope[:, t, 1, a:a + 32].unsqueeze(1).broadcast_to([128, 2 * NH, 32]),
                                          ALU.mult).then_inc(dve_step, 1)
                    dve.wait_ge(dve_step, steps)
                    dve.wait_ge(t1_ready, by(t))
                    dve.wait_ge(qk_turned, by(t - 1))
                    dve.wait_ge(kd_ready, by(t - 1))
                    dve.tensor_tensor(qk[:, :, :], t1[:, :, :], t2[:, :, :], ALU.add).then_inc(qk_ready, 1)

                def scores(t, rows, cross, decay):
                    dve.wait_ge(qkT_ready, by(t))
                    dve.wait_ge(o_done, by(t - 1))
                    q = qT[:, :, 0:rows]
                    if rows == 128:
                        dve.tensor_tensor(qd[:, :, :], q, cross[:, :, :], ALU.mult).then_inc(qd_ready, 1)
                    else:
                        dve.wait_ge(cleared, 4)
                        own = bass.AP(tensor=qdm[:].tensor, offset=qdm[:].offset,
                                      ap=[list(qdm[:].ap[0]), [DEC_B * NS, NPAIR], [NS + DEC_T, DEC_B], [1, DEC_T]])
                        split = lambda x: x.rearrange("p a (b t) -> p a b t", b=DEC_B)
                        dve.tensor_tensor(own, split(q), split(cross[:, :, :]), ALU.mult).then_inc(qd_ready, 1)
                    dve.wait_ge(inner_done, by(t))
                    for r in range(2):
                        x = dve.tensor_tensor(inT[0:rows, r, :, 0:rows], in_ps[r][0:rows, :, 0:rows],
                                              decay[:, r:NH:2, :], ALU.mult)
                    x.then_inc(inT_ready, 1)

                def new_state(t, S_next):
                    dve.wait_ge(update_done, by(t))
                    dve.wait_ge(Sg_ready, by(t))
                    for r in range(2):
                        x = dve.tensor_tensor(diagonal(S_next, r), diagonal(Sg, r), diagonal(su_ps, r), ALU.add)
                    x.then_inc(S_ready, 1)

                def centre(t, rows, steps):
                    dve.wait_ge(o_done, by(t))
                    dve.tensor_reduce(stat[0:rows, 0, :], o_ps[0:rows], AXX, ALU.add).then_inc(dve_step, 1)
                    dve.wait_ge(dve_step, steps)
                    dve.tensor_scalar(stat[0:rows, 1, :], stat[0:rows, 0, :], -1.0 / HD, None, ALU.mult).then_inc(dve_step, 1)
                    dve.wait_ge(dve_step, steps + 1)
                    dve.wait_ge(on_ready, by(t - 1))
                    dve.tensor_tensor(oc[0:rows], o_ps[0:rows], spread(stat[0:rows, 1, :], [rows, NH, HD]),
                                      ALU.add).then_inc(oc_ready, 1)

                def variance(t, steps):
                    dve.wait_ge(sq_ready, by(t))
                    dve.tensor_reduce(stat[:, 2, :], sq[:, :, :], AXX, ALU.add).then_inc(dve_step, 1)
                    dve.wait_ge(dve_step, steps)
                    dve.tensor_scalar(stat[:, 3, :], stat[:, 2, :], 1.0 / HD, GN_EPS, ALU.mult, ALU.add).then_inc(var_ready, 1)

                def finish(t, par, stored):
                    dve.wait_ge(on_ready, by(t))
                    dve.wait_ge(gate_ready, by(t))
                    dve.wait_ge(mix_stored[par], stored)
                    dve.tensor_tensor(mixr[:, par, :], on[:, :, :].rearrange("p h d -> p (h d)"), gate[:, :],
                                      ALU.mult).then_inc(mix_ready, 1)

                tables.clear(dve)
                rotate(0, 0, 16, 3)
                tables.build_rows(dve)
                dve.wait_ge(tab_landed, 16 * TABS)
                dve.wait_ge(cleared, 2)

                def step(t, par, i=0):
                    rotate(t + 1, 1 - par, next_lap(t, i), 5 if known(t, 0) else 5 * t + 4)
                    scores(t, 128, cross, decay)
                    if not known(t, 0):
                        variance(t - 1, 5 * t + 5)
                    new_state(t, S[:, 1 - par])
                    if not known(t, 0):
                        finish(t - 1, 1 - par, 16 * i + 16)
                    centre(t, 128, 5 * t + 6)

                over_tiles(dve, step)
                scores(SAMPLE, NS, cross_s, decay_s)
                variance(PT - 1, 5 * PT + 3)
                finish(PT - 1, 1, 16 * PT // 2)
                one_sequence(dve, slice(0, DEC_B // 2 + 1))
                tables.build_samples(dve, 0)
                centre(SAMPLE, NS, 5 * PT + 4)
                variance(SAMPLE, 5 * PT + 6)
                tables.build_samples(dve, 1)
                dve.wait_ge(state_landed, 32)
                for p in range(NPAIR):
                    if p == 1:
                        tables.build_samples(dve, 2)
                    dve.wait_ge(update_done, by(SAMPLE) + p)
                    for r in range(2):
                        rows = slice(HD * r, HD * r + HD)
                        dve.scalar_tensor_tensor(S_out[rows, :, p], S_in[rows, :, p, HD * r:HD * r + HD],
                                                 chunk_s[rows, p:p + 1],
                                                 su_ps[rows].rearrange("d a (c e) -> d (a c) e", e=HD),
                                                 ALU.mult, ALU.add).then_inc(sout_ready, 1)
                finish(SAMPLE, 0, 16 * PT // 2 + 16)

            @block.tensor
            def _(pe):
                for s in (qk_turned, inner_done, update_done, o_done):
                    pe.sem_inc(s, 1)

                def turn(t):
                    pe.wait_ge(qk_ready, by(t))
                    pe.wait_ge(qkT_ready, by(t - 1))
                    for g in range(2):
                        for p in range(NPAIR):
                            h = g * NH + 2 * p
                            mm = pe.transpose(qk_ps[g][:, p, :], qk[:, h:h + 2, :].rearrange("t h d -> t (h d)"), ident[:, :])
                    mm.then_inc(qk_turned, 1)

                def inner(t, rows):
                    pe.wait_ge(qkT_ready, by(t))
                    pe.wait_ge(inT_ready, by(t - 1))
                    for p in range(NPAIR):
                        for r in range(2):
                            mm = pe.matmul(in_ps[r][0:rows, p, 0:rows], kT[:, r, p, 0:rows], qT[:, p, 0:rows],
                                           start=True, stop=True)
                    mm.then_inc(inner_done, 1)

                def step(t, par, i=0):
                    inner(t, 128)
                    pe.wait_ge(vg_landed[par], lap(t, par, i))
                    pe.wait_ge(kd_ready, by(t))
                    pe.wait_ge(S_ready, by(t - 1))
                    for p in range(NPAIR):
                        mm = pe.matmul(su_ps[:, p, :], kd[:, 2 * p:2 * p + 2, :].rearrange("t h d -> t (h d)"),
                                       zr[:, par, 2, 2 * p:2 * p + 2, :].rearrange("t h d -> t (h d)"), start=True, stop=True)
                    mm.then_inc(update_done, 1)
                    turn(t + 1)
                    pe.wait_ge(qd_ready, by(t))
                    pe.wait_ge(inT_ready, by(t))
                    pe.wait_ge(oc_ready, by(t - 1))
                    for p in range(NPAIR):
                        pe.matmul(o_ps[:, 2 * p:2 * p + 2, :].rearrange("t h d -> t (h d)"), qd[:, p, :], S[:, par, p, :],
                                  start=True, stop=False)
                        for r in range(2):
                            mm = pe.matmul(o_ps[:, 2 * p + r, :], inT[:, r, p, :], zr[:, par, 2, 2 * p + r, :],
                                           start=False, stop=(r == 1))
                    mm.then_inc(o_done, 1)

                pe.wait_ge(cleared, 2)
                turn(0)
                tables.row_products(pe)
                over_tiles(pe, step)
                inner(SAMPLE, NS)
                tables.sample_products(pe, 0)
                pe.wait_ge(state_landed, 32)
                pe.wait_ge(qd_ready, by(SAMPLE))
                pe.wait_ge(inT_ready, by(SAMPLE))
                pe.wait_ge(oc_ready, by(SAMPLE - 1))
                pe.wait_ge(vg_landed[0], 16 * PT // 2 + 16)
                for p in range(NPAIR):
                    for b in range(DEC_B):
                        pe.matmul(o_ps[0:NS, 2 * p:2 * p + 2, :].rearrange("t h d -> t (h d)"),
                                  qdm[:, p, b * NS:b * NS + NS], S_in[:, b, p, :], start=(b == 0), stop=False)
                    for r in range(2):
                        mm = pe.matmul(o_ps[0:NS, 2 * p + r, :], inT[0:NS, r, p, 0:NS], zr[0:NS, 0, 2, 2 * p + r, :],
                                       start=False, stop=(r == 1))
                mm.then_inc(o_done, 1)
                tables.sample_products(pe, 1)
                pe.wait_ge(kd_ready, by(SAMPLE))
                pe.wait_ge(vm_ready, 2)
                pe.wait_ge(S_ready, by(PT - 1))
                for p in range(NPAIR):
                    if p == 1:
                        tables.sample_products(pe, 2)
                    if p:
                        pe.wait_ge(sout_ready, 2 * p)
                    for r in range(2):
                        mm = pe.matmul(su_ps[HD * r:HD * r + HD].rearrange("d a (c e) -> d (a c) e", e=HD),
                                       kd[0:NS, 2 * p + r, :], vm[:, :, HD * (2 * p + r):HD * (2 * p + r + 1)],
                                       start=True, stop=True)
                    mm.then_inc(update_done, 1)


def load_pair(eng, z, q_n, k_n, qk_landed, p):
    rows = z[0:SEQ, :].rearrange("(t p) c -> p t c", p=128)
    for n, dst in enumerate((q_n, k_n)):
        eng.dma_start(dst[:, :, :], rows[:, :, bass.ds((4 + n) * WID + p * 128, 128)]).then_inc(qk_landed, 16)


def prompt_attention(nc, A, z, mix, bias, ident, q_n, k_n, qk_landed, clear, ahead):
    UNITS = 2 * PT
    at = lambda p, u: UNITS * p + u + 3
    with ExitStack() as ctx:
        sb = lambda n, s, d=F32: ctx.enter_context(nc.sbuf_tensor(n, s, d))
        ps = lambda n, s: ctx.enter_context(nc.psum_tensor(n, s, F32))
        sem = lambda n: nc.alloc_semaphore("p3_" + n)
        v_all = sb("v_all", [128, PT, WID])
        qT, kT = sb("qT", [128, SEQ]), sb("kT", [128, 2, SEQ])
        S, P_T = sb("S3", [128, 2, SEQ]), sb("P_T", [128, 2, PT, 128])
        O = sb("O", [128, PT, 128])
        least, total, share = (sb(n, [128, UNITS]) for n in ("least", "total", "share"))
        S_ps = [ps(f"S_ps{i}", [128, SEQ]) for i in range(2)]
        T_ps = [ps(f"T_ps{i}", [128, 4, 128]) for i in range(2)]
        O_ps, prep_ps = ps("O_ps", [128, 128]), ps("prep_ps", [128, 4, 128])
        v_landed, prep_done, prep_ready = sem("v_landed"), sem("prep_done"), sem("prep_ready")
        zeros_set, N_ready = sem("zeros_set"), sem("N_ready")
        S_done, E_ready, P_ready, T_done, PT_low, PT_high, share_ready, V_done, O_ready = map(
            sem, ("S_done", "E_ready", "P_ready", "T_done", "PT_low", "PT_high", "share_ready", "V_done", "O_ready"))
        O_stored = sem("O_stored")
        high = lambda p, u: PT * p + (u - PT) + 3

        with nc.Block() as block:

            @block.sync
            def _(sp):
                rows = z[0:SEQ, :].rearrange("(t p) c -> p t c", p=128)

                def load_values(p):
                    sp.dma_start(v_all[:, :, bass.ds(p * 128, 128)],
                                 rows[:, :, bass.ds(6 * WID + p * 128, 128)]).then_inc(v_landed, 16)

                def store(p):
                    sp.wait_ge(O_ready, at(p, UNITS - 1))
                    sp.dma_start(mix[0:SEQ, bass.ds(WID + p * 128, 128)].rearrange("(t p) c -> p t c", p=128),
                                 O[:, :, :]).then_inc(O_stored, 16)

                load_values(0)
                ahead(sp)
                with sp.Fori(0, NPAIR - 1) as p:
                    sp.wait_ge(v_landed, 16 * p + 16)
                    sp.wait_ge(prep_done, 4 * p + 4)
                    load_pair(sp, z, q_n, k_n, qk_landed, p + 1)
                    load_values(p + 1)
                    store(p)
                store(NPAIR - 1)
                sp.wait_ge(O_stored, 16 * NPAIR)

            @block.gpsimd
            def _(pool):
                clear(pool)

            @block.scalar
            def _(act):
                for s in (P_ready, PT_high, O_ready):
                    act.sem_inc(s, 2)
                act.sem_inc(prep_ready, 1)

                def exp(p, u):
                    n = (u // 2 + 1) * 128
                    act.wait_ge(E_ready, at(p, u))
                    act.activation(S[:, u % 2, 0:n], S[:, u % 2, 0:n], ACT.Exp, bias=least[:, u:u + 1], scale=-1.0,
                                   accum_out=total[:, u:u + 1]).then_inc(P_ready, 1)

                def evacuate(p, u):
                    nt = u // 2 + 1
                    if nt > 4:
                        act.wait_ge(T_done, at(p, u))
                        act.wait_ge(V_done, at(p, u - 2))
                        act.copy(P_T[:, u % 2, 4:nt, :], T_ps[1][:, 0:nt - 4, :]).then_inc(PT_high, 1)

                def scale(p, u):
                    act.wait_ge(V_done, at(p, u))
                    act.wait_ge(share_ready, at(p, u))
                    if u == 0:
                        act.wait_ge(O_stored, 16 * p)
                    own = slice(HD * (u % 2), HD * (u % 2) + HD)
                    act.activation(O[:, u // 2, own], O_ps[:, own], ACT.Copy, scale=share[:, u:u + 1]).then_inc(O_ready, 1)

                def pair(p):
                    for g in range(4):
                        act.wait_ge(prep_done, 4 * p + g + 1)
                        if g == 0:
                            act.wait_ge(S_done, at(p - 1, UNITS - 1))
                        src, cols = prep_ps[:].rearrange("c t p -> c (t p)"), slice(512 * (g % 2), 512 * (g % 2) + 512)
                        if g < 2:
                            act.mul(qT[:, cols], src, HD ** -0.5).then_inc(prep_ready, 1)
                        else:
                            act.copy(kT[0:HD, 0, cols], src[0:HD, :])
                            act.copy(kT[HD:128, 1, cols], src[HD:128, :]).then_inc(prep_ready, 1)
                    for u in range(UNITS + 2):
                        if u < UNITS:
                            exp(p, u)
                        if 1 <= u <= UNITS:
                            evacuate(p, u - 1)
                        if u >= 2:
                            scale(p, u - 2)

                act.wait_ge(zeros_set, 1)
                with act.Fori(0, NPAIR) as p:
                    pair(p)

            @block.vector
            def _(dve):
                dve.memset(kT[:, :, :], 0.0).then_inc(zeros_set, 1)
                for s in (N_ready, E_ready, PT_low, share_ready):
                    dve.sem_inc(s, 2)

                def scores(p, u):
                    n = (u // 2 + 1) * 128
                    dve.wait_ge(S_done, at(p, u))
                    dve.wait_ge(T_done, at(p, u - 2))
                    dve.scalar_tensor_tensor(
                        S[:, u % 2, 0:n], S_ps[u % 2][:, 0:n], -1.0,
                        bias[:, bass.ds(2 * p + u % 2, 1), SEQ - n:SEQ].rearrange("q h k -> q (h k)"),
                        ALU.mult, ALU.subtract).then_inc(N_ready, 1)
                    dve.wait_ge(N_ready, at(p, u))
                    dve.tensor_reduce(least[:, u:u + 1], S[:, u % 2, 0:n], AXX, ALU.min).then_inc(E_ready, 1)

                def evacuate(p, u):
                    nt = min(u // 2 + 1, 4)
                    dve.wait_ge(T_done, at(p, u))
                    dve.wait_ge(V_done, at(p, u - 2))
                    dve.tensor_copy(P_T[:, u % 2, 0:nt, :], T_ps[0][:, 0:nt, :]).then_inc(PT_low, 1)

                def reciprocal(p, u):
                    dve.wait_ge(P_ready, at(p, u))
                    dve.wait_ge(O_ready, at(p, u - 2))
                    dve.reciprocal(share[:, u:u + 1], total[:, u:u + 1]).then_inc(share_ready, 1)

                with dve.Fori(0, NPAIR) as p:
                    for u in range(UNITS + 1):
                        if u < UNITS:
                            scores(p, u)
                        if u >= 1:
                            evacuate(p, u - 1)
                            reciprocal(p, u - 1)

            @block.tensor
            def _(pe):
                for s in (S_done, T_done, V_done):
                    pe.sem_inc(s, 2)

                def scores(p, u):
                    n = (u // 2 + 1) * 128
                    q0 = (u // 2) * 128
                    pe.wait_ge(E_ready, at(p, u - 2))
                    for k in range(0, n, 512):
                        m = min(n, k + 512)
                        mm = pe.matmul(S_ps[u % 2][:, k:m], qT[:, q0:q0 + 128], kT[:, u % 2, k:m], start=True, stop=True)
                    mm.then_inc(S_done, 1)

                def turn(p, u):
                    pe.wait_ge(P_ready, at(p, u))
                    pe.wait_ge(PT_low, at(p, u - 1))
                    if u > PT:
                        pe.wait_ge(PT_high, high(p, u - 1))
                    for k in range(u // 2 + 1):
                        mm = pe.transpose(T_ps[k // 4][:, k % 4, :], S[:, u % 2, k * 128:k * 128 + 128], ident[:, :])
                    mm.then_inc(T_done, 1)

                def values(p, u):
                    nt = u // 2 + 1
                    pe.wait_ge(PT_low, at(p, u))
                    if u >= PT:
                        pe.wait_ge(PT_high, high(p, u))
                    pe.wait_ge(O_ready, at(p, u - 1))
                    for k in range(nt):
                        mm = pe.matmul(O_ps[:, :], P_T[:, u % 2, k, :], v_all[:, k, bass.ds(p * 128, 128)],
                                       start=(k == 0), stop=(k == nt - 1))
                    mm.then_inc(V_done, 1)

                with pe.Fori(0, NPAIR) as p:
                    pe.wait_ge(qk_landed, 32 * p + 32)
                    for g in range(4):
                        pe.wait_ge(prep_ready, 4 * p + g + 1)
                        for t in range(4):
                            mm = pe.transpose(prep_ps[:, t, :], (q_n, k_n)[g // 2][:, 4 * (g % 2) + t, :], ident[:, :])
                        mm.then_inc(prep_done, 1)
                    pe.wait_ge(prep_ready, 4 * p + 5)
                    scores(p, 0)
                    scores(p, 1)
                    pe.wait_ge(v_landed, 16 * p + 16)
                    for u in range(UNITS + 1):
                        if u + 2 < UNITS:
                            scores(p, u + 2)
                        if u < UNITS:
                            turn(p, u)
                        if u >= 1:
                            values(p, u - 1)


def load_keys(eng, A, z, K, landed, b, par):
    rows = window(A["cache_k_win"], b)
    eng.dma_start(K[:, par, 0:WIDE, :].rearrange("p j c -> p (j c)"), wide(rows, 0, WIDE)).then_inc(landed[par], 16)
    eng.dma_start(K[:, par, WIDE:WIDE + 2, :].rearrange("p j c -> p (j c)"), rest(rows)).then_inc(landed[par], 16)
    eng.dma_start(K[0:DEC_T, par, STILES - 1, :], z[bass.ds(SEQ + b * DEC_T, DEC_T), 5 * WID:6 * WID]).then_inc(landed[par], 16)


def load_values(eng, A, z, V, landed, b, g):
    rows = window(A["cache_v_win"], b)
    if g < 2:
        eng.dma_start(V[:, 4 * g:4 * g + 4, :].rearrange("p j c -> p (j c)"), wide(rows, 4 * g, 4)).then_inc(landed[g], 16)
    else:
        eng.dma_start(V[:, WIDE:WIDE + 2, :].rearrange("p j c -> p (j c)"), rest(rows)).then_inc(landed[g], 16)
        eng.dma_start(V[0:DEC_T, STILES - 1, :], z[bass.ds(SEQ + b * DEC_T, DEC_T), 6 * WID:7 * WID]).then_inc(landed[g], 16)


def window(cache, b):
    return cache[0].rearrange("b l h d -> (b l) (h d)")[bass.ds(b * L, L), :]


def wide(rows, j, n):
    return rows.rearrange("(p x) c -> p (x c)", x=16)[:, j * WID:(j + n) * WID]


def rest(rows):
    return rows[REST:L, :].rearrange("(g x) c -> g (x c)", x=16)[:, WIDE * WID:].rearrange("g (x c) -> g x c", x=4)


def sample_attention(nc, A, z, mix, bias_s, ident, K, V, K_landed, V_landed, ahead):
    RING, C, GROUPS = 4, NH * DEC_T, 3
    KEYS = STILES * 128
    PER = STILES + GROUPS
    tiles = lambda g: range(4 * g, min(4 * g + 4, STILES))
    keys = lambda g: slice(512 * g, min(512 * g + 512, KEYS))

    def entry(b, i):
        return i if known(b, 0) else PER * b - GROUPS + i

    def slot(b, par, i):
        return (i if known(b, 0) else PER * par - GROUPS + i) % RING

    def key_at(b, j):
        return j if known(b, 0) or j < 5 else j + GROUPS

    def prob_at(b, g):
        return g if known(b, DEC_B) else 5 + g

    with ExitStack() as ctx:
        sb = lambda n, s, d=F32: ctx.enter_context(nc.sbuf_tensor(n, s, d))
        ps = lambda n, s: ctx.enter_context(nc.psum_tensor(n, s, F32))
        sem = lambda n: nc.alloc_semaphore("p4_" + n)
        K_hi, K_lo = (sb(n, [128, NPAIR, STILES, 128], F32R) for n in ("K_hi", "K_lo"))
        V_hi, V_lo = (sb(n, [128, STILES, WID], F32R) for n in ("V_hi", "V_lo"))
        q_n, q_b = sb("q_n4", [NS, WID]), sb("q_b", [128, 2, NPAIR, DEC_T])
        q_s = sb("q_s", [128, 2, NPAIR, DEC_B, DEC_T])
        Q_hi, Q_lo = (sb(n, [128, 2, NPAIR * (128 + 2 * DEC_T)], F32R) for n in ("Q_hi", "Q_lo"))
        nought = sb("nought", [128, NPAIR, 2, DEC_T])
        E, P_T = sb("E4", [128, KEYS]), sb("P_T4", [128, STILES, 2, C], F32R)
        mins, least = sb("mins", [128, GROUPS]), sb("least4", [128, 1])
        total, share = sb("total4", [128, 1]), sb("share4", [128, 1])
        own, sum_t = sb("own", [128, WID]), sb("sum_t", [128, 128])
        O, out = sb("O4", [128, WID]), sb("out4", [DEC_T, WID])
        T_ps = [ps(f"T4_ps{i}", [128, 4, 128]) for i in range(RING)]
        S_ps = [ps(f"S4_ps{i}", [128, 512]) for i in range(GROUPS)]
        O_ps = ps("O_ps4", [128, WID])
        (stored, q_landed, set_up, q_turned, q_ready, qb_ready, Qhi_ready, Q_ready, turned, hi_ready, lo_ready, S_done, N_ready, min_ready,
         least_ready, P_ready, Vhi_ready, Vlo_ready, V_done, share_ready, O_ready, sum_done, out_ready) = map(
            sem, ("stored", "q_landed", "set_up", "q_turned", "q_ready", "qb_ready", "Qhi_ready", "Q_ready", "turned", "hi_ready", "lo_ready",
                  "S_done", "N_ready", "min_ready", "least_ready", "P_ready", "Vhi_ready", "Vlo_ready", "V_done",
                  "share_ready", "O_ready", "sum_done", "out_ready"))

        def over_sequences(eng, step):
            step(0, 0)
            with eng.Fori(0, DEC_B // 2 - 1) as i:
                step(2 * i + 1, 1, i)
                step(2 * i + 2, 0, i)
            step(DEC_B - 1, 1, DEC_B // 2 - 1)
            step(DEC_B, 0, DEC_B // 2 - 1)

        with nc.Block() as block:

            @block.sync
            def _(sp):
                def next_keys(b, par):
                    if not isinstance(b, int) or b >= 2:
                        sp.wait_ge(turned, entry(b, 0) - PER)
                    load_keys(sp, A, z, K, K_landed, b, par)

                def next_values(b):
                    for g in range(GROUPS):
                        sp.wait_ge(Vlo_ready, GROUPS * b + g - 2)
                        load_values(sp, A, z, V, V_landed, b, g)

                def store(b):
                    sp.wait_ge(out_ready, by(b))
                    sp.dma_start(mix[bass.ds(SEQ + b * DEC_T, DEC_T), WID:2 * WID], out[:, :]).then_inc(stored, 16)

                sp.dma_start(q_n[:, :], z[SEQ:NTOK, 4 * WID:5 * WID]).then_inc(q_landed, 16)
                sp.dma_start(own[:, :], A["c_own"]).then_inc(q_landed, 16)
                sp.dma_start(sum_t[:, :], A["c_sum_t"]).then_inc(q_landed, 16)
                next_keys(1, 1)
                next_values(1)
                next_keys(2, 0)
                with sp.Fori(1, DEC_B // 2 - 1) as i:
                    for par in range(2):
                        next_values(2 * i + par)
                        next_keys(2 * i + par + 1, 1 - par)
                        store(2 * i + par - 2)
                next_values(DEC_B - 2)
                next_keys(DEC_B - 1, 1)
                store(DEC_B - 4)
                next_values(DEC_B - 1)
                store(DEC_B - 3)
                store(DEC_B - 2)
                ahead(sp)
                store(DEC_B - 1)
                sp.wait_ge(stored, 16 * DEC_B + 16)

            @block.gpsimd
            def _(pool):
                pool.memset(Q_hi[:, :, :].bitcast(F32), 0.0).then_inc(set_up, 1)
                pool.memset(Q_lo[:, :, :].bitcast(F32), 0.0).then_inc(set_up, 1)
                pool.memset(q_s[:, :, :, :, :], 0.0).then_inc(set_up, 1)
                pool.memset(nought[:, :, :, :], 0.0).then_inc(set_up, 1)
                pool.wait_ge(set_up, 4)
                pool.wait_ge(q_ready, 2)

                def queries(b, par):
                    if not known(b, 0):
                        pool.wait_ge(Q_ready, 2 * b)
                    pool.tensor_copy(q_b[:, :, :, :], q_s[:, :, :, bass.ds(b, 1), :].rearrange("d r p b t -> d r p (b t)")
                                     ).then_inc(qb_ready, 1)
                    pool.wait_ge(qb_ready, b + 1)
                    block_of = lambda t, r: t[:, par, :].rearrange("d (p x) -> d p x", p=NPAIR)[:, :, 0:128] \
                        .rearrange("d p (c x) -> d p c x", c=2)[:, :, :, DEC_T * r:DEC_T * r + DEC_T]
                    both = lambda r: q_b[:, r].unsqueeze(2).broadcast_to([128, NPAIR, 2, DEC_T])
                    for r in range(2):
                        pool.tensor_tensor(block_of(Q_hi, r), both(r), nought[:, :, :, :], ALU.add).then_inc(Qhi_ready, 1)
                    pool.wait_ge(Qhi_ready, 2 * b + 2)
                    for r in range(2):
                        pool.tensor_tensor(block_of(Q_lo, r), both(r), block_of(Q_hi, r).bitcast(F32),
                                           ALU.subtract).then_inc(Q_ready, 1)

                def step(b, par, i=0):
                    if known(b, DEC_B):
                        return
                    if not known(b, DEC_B - 1):
                        if not known(b, 0):
                            pool.wait_ge(S_done, GROUPS * b)
                        queries(b + 1, 1 - par)
                    for g in range(GROUPS):
                        pool.wait_ge(Vhi_ready, GROUPS * b + g + 1)
                        cut = (slice(None), slice(4 * g, min(4 * g + 4, STILES)))
                        pool.tensor_tensor(V_lo[cut], V[cut], V_hi[cut].bitcast(F32), ALU.subtract).then_inc(Vlo_ready, 1)

                queries(0, 0)
                over_sequences(pool, step)

            @block.scalar
            def _(act):
                def keys_high(b, par, j):
                    i = key_at(b, j)
                    act.wait_ge(turned, entry(b, i) + 1)
                    if not known(b, 0) and j % 4 == 0:
                        act.wait_ge(S_done, GROUPS * b - 2 + j // 4)
                    act.copy(K_hi[:, :, j, :], T_ps[slot(b, par, i)][:, :, :]).then_inc(hi_ready, 1)

                def exp(b):
                    act.wait_ge(least_ready, b + 1)
                    act.wait_ge(share_ready, by(b - 1))
                    act.activation(E[:, :], E[:, :], ACT.Exp, bias=least[:, 0:1], scale=-1.0,
                                   accum_out=total[:, 0:1]).then_inc(P_ready, 1)

                def probs_high(b, par, g):
                    i, n = prob_at(b, g), len(tiles(g))
                    act.wait_ge(turned, entry(b, i) + 1)
                    act.wait_ge(V_done, GROUPS * b + g - 2)
                    act.copy(P_T[:, 4 * g:4 * g + n, 0, :], T_ps[slot(b, par, i)][:, 0:n, 0:C]).then_inc(hi_ready, 1)

                def values_high(b, g, lap):
                    act.wait_ge(V_landed[g], lap * (32 if g == 2 else 16))
                    act.wait_ge(V_done, GROUPS * b + g + 1)
                    cut = (slice(None), slice(4 * g, min(4 * g + 4, STILES)))
                    act.copy(V_hi[cut], V[cut]).then_inc(Vhi_ready, 1)

                def evacuate(b):
                    act.wait_ge(sum_done, by(b))
                    act.wait_ge(stored, 16 * b + 16)
                    act.copy(out[:, :], O_ps[0:DEC_T, :]).then_inc(out_ready, 1)

                def step(b, par, i=0):
                    begins, ends = not known(b, DEC_B), not known(b, 0)
                    if begins:
                        for j in range(5):
                            keys_high(b, par, j)
                    if ends:
                        exp(b - 1)
                        for g in range(GROUPS):
                            probs_high(b, par, g)
                    if begins:
                        for j in range(5, STILES):
                            keys_high(b, par, j)
                            if j == 7:
                                values_high(b, 0, b + 1)
                        values_high(b, 1, b + 1)
                        values_high(b, 2, b + 1)
                    if ends:
                        evacuate(b - 1)

                act.sem_inc(stored, 16)
                act.wait_ge(q_turned, 1)
                act.wait_ge(set_up, 3)
                for r in range(2):
                    d = slice(HD * r, HD * r + HD)
                    act.mul(q_s[d, r].rearrange("d p b t -> d p (b t)"),
                            O_ps[d, 0:NPAIR * NS].rearrange("d (p n) -> d p n", p=NPAIR), HD ** -0.5).then_inc(q_ready, 1)
                act.sem_inc(out_ready, 1)
                over_sequences(act, step)

            @block.vector
            def _(dve):
                dve.wait_ge(q_landed, 48)
                dve.sem_inc(share_ready, 1)
                dve.sem_inc(O_ready, 1)

                def keys_low(b, par, j):
                    i = key_at(b, j)
                    dve.wait_ge(hi_ready, entry(b, i) + 1)
                    dve.tensor_tensor(K_lo[:, :, j, :], T_ps[slot(b, par, i)][:, :, :], K_hi[:, :, j, :].bitcast(F32),
                                      ALU.subtract).then_inc(lo_ready, 1)

                def probs_low(b, par, g):
                    i, n = prob_at(b, g), len(tiles(g))
                    dve.wait_ge(hi_ready, entry(b, i) + 1)
                    cut = (slice(None), slice(4 * g, 4 * g + n))
                    dve.tensor_tensor(P_T[cut][:, :, 1, :], T_ps[slot(b, par, i)][:, 0:n, C:2 * C],
                                      P_T[cut][:, :, 0, :].bitcast(F32), ALU.subtract).then_inc(lo_ready, 1)

                def add_bias(b, g):
                    w = keys(g)
                    dve.wait_ge(S_done, GROUPS * b + g + 1)
                    if g == 0 and not known(b, 0):
                        dve.wait_ge(turned, entry(b, prob_at(b, GROUPS)))
                    dve.scalar_tensor_tensor(E[:, w], S_ps[g][:, 0:w.stop - w.start], -1.0, bias_s[:, w],
                                             ALU.mult, ALU.subtract).then_inc(N_ready, 1)
                    if g == 0 and not known(b, 0):
                        dve.wait_ge(least_ready, b)
                    dve.wait_ge(N_ready, GROUPS * b + g + 1)
                    dve.tensor_reduce(mins[:, g:g + 1], E[:, w], AXX, ALU.min).then_inc(min_ready, 1)

                def find_least(b):
                    dve.wait_ge(min_ready, GROUPS * b + GROUPS)
                    if not known(b, 0):
                        dve.wait_ge(P_ready, b)
                    dve.tensor_reduce(least[:, :], mins[:, :], AXX, ALU.min).then_inc(least_ready, 1)

                def normalise(b):
                    dve.wait_ge(P_ready, b + 1)
                    dve.wait_ge(O_ready, by(b - 1))
                    dve.reciprocal(share[:, :], total[:, :]).then_inc(share_ready, 1)
                    dve.wait_ge(share_ready, by(b))
                    dve.wait_ge(V_done, GROUPS * (b + 2))
                    dve.wait_ge(sum_done, by(b - 1))
                    dve.scalar_tensor_tensor(O[:, :], O_ps[:, :], share[:, 0:1], own[:, :], ALU.mult,
                                             ALU.mult).then_inc(O_ready, 1)

                def step(b, par, i=0):
                    begins, ends = not known(b, DEC_B), not known(b, 0)
                    if begins:
                        for j in range(5):
                            keys_low(b, par, j)
                    if ends:
                        for g in range(GROUPS):
                            probs_low(b, par, g)
                    if begins:
                        add_bias(b, 0)
                        for j in range(5, 8):
                            keys_low(b, par, j)
                        add_bias(b, 1)
                        for j in range(8, STILES):
                            keys_low(b, par, j)
                    if ends:
                        normalise(b - 1)
                    if begins:
                        add_bias(b, 2)
                        find_least(b)

                over_sequences(dve, step)

            @block.tensor
            def _(pe):
                pe.sem_inc(V_done, GROUPS)
                pe.sem_inc(sum_done, 1)

                def free(b, i):
                    if not known(b, 0) or i >= RING:
                        pe.wait_ge(lo_ready, entry(b, i) - RING + 1)

                def turn_keys(b, par, j):
                    i = key_at(b, j)
                    free(b, i)
                    for p in range(NPAIR):
                        mm = pe.transpose(T_ps[slot(b, par, i)][:, p, :], K[:, par, j, 128 * p:128 * p + 128], ident[:, :])
                    mm.then_inc(turned, 1)

                def turn_probs(b, par, g):
                    i = prob_at(b, g)
                    if g == 0:
                        pe.wait_ge(P_ready, b)
                    free(b, i)
                    for n, j in enumerate(tiles(g)):
                        mm = pe.transpose(T_ps[slot(b, par, i)][:, n, :], E[:, 128 * j:128 * j + 128], ident[:, :])
                    mm.then_inc(turned, 1)

                def scores(b, par, g):
                    w = keys(g)
                    pe.wait_ge(lo_ready, entry(b, key_at(b, tiles(g)[-1])) + 1)
                    if g == 0:
                        pe.wait_ge(Q_ready, 2 * b + 2)
                    if not known(b, 0):
                        pe.wait_ge(N_ready, GROUPS * b - 2 + g)
                    for p in range(NPAIR):
                        for m, (q, k) in enumerate(((Q_hi, K_hi), (Q_hi, K_lo), (Q_lo, K_hi))):
                            mm = pe.matmul(S_ps[g][:, 0:w.stop - w.start], q[:, par, 128 * p:128 * p + 128],
                                           k[:, p, :, :].rearrange("d j n -> d (j n)")[:, w],
                                           start=(p, m) == (0, 0), stop=(p, m) == (NPAIR - 1, 2))
                    mm.then_inc(S_done, 1)

                def values(b, g):
                    pe.wait_ge(lo_ready, entry(b, prob_at(b, g)) + 1)
                    pe.wait_ge(Vlo_ready, GROUPS * b - 2 + g)
                    if g == 0:
                        pe.wait_ge(out_ready, b)
                    for j in tiles(g):
                        for m, v in enumerate((V_hi, V_lo)):
                            mm = pe.matmul(O_ps[:, :], P_T[:, j].rearrange("k c n -> k (c n)"), v[:, j, :],
                                           start=(j, m) == (0, 0), stop=(j, m) == (STILES - 1, 1))
                    mm.then_inc(V_done, 1)

                def sum_heads(b):
                    pe.wait_ge(O_ready, by(b))
                    pe.matmul(O_ps[:, :], sum_t[:, :], O[:, :], start=True, stop=True).then_inc(sum_done, 1)

                def step(b, par, i=0):
                    begins, ends = not known(b, DEC_B), not known(b, 0)
                    if begins:
                        pe.wait_ge(K_landed[par], 48 if known(b, 0) else 48 * i + 48 * (2 - par))
                        for j in range(5):
                            turn_keys(b, par, j)
                        scores(b, par, 0)
                    if ends:
                        for g in range(GROUPS):
                            turn_probs(b, par, g)
                    if begins:
                        for j in range(5, 8):
                            turn_keys(b, par, j)
                    if ends:
                        values(b, 0)
                    if begins:
                        scores(b, par, 1)
                    if ends:
                        values(b, 1)
                    if begins:
                        for j in range(8, STILES):
                            turn_keys(b, par, j)
                    if ends:
                        values(b, 2)
                    if begins:
                        scores(b, par, 2)
                    if ends:
                        sum_heads(b - 1)

                pe.wait_ge(q_landed, 48)
                for p in range(NPAIR):
                    mm = pe.transpose(O_ps[:, NS * p:NS * p + NS], q_n[:, 128 * p:128 * p + 128], ident[0:NS, 0:NS])
                mm.then_inc(q_turned, 1)
                pe.wait_ge(q_ready, 2)
                over_sequences(pe, step)


def load_out_piece(eng, A, w_raw, w_landed, k):
    eng.dma_start(w_raw[:, k % (KT // 2), :], A["w_out"][0, k * 128:k * 128 + 128, :]).then_inc(w_landed[k % (KT // 2)], 16)


def out_projection(nc, A, mix, x_mid, h_hi, h_lo, ident, w_raw, w_landed):
    HK = KT // 2
    with ExitStack() as ctx:
        sb = lambda n, s, d=F32: ctx.enter_context(nc.sbuf_tensor(n, s, d))
        ps = lambda n, s: ctx.enter_context(nc.psum_tensor(n, s, F32))
        sem = lambda n: nc.alloc_semaphore("p5_" + n)
        w_hi, w_lo = sb("wo_hi", [128, KT, D_MODEL], F32R), sb("wo_lo", [128, KT, D_MODEL], F32R)
        m_n, x_n = sb("m_n", [128, 2, D_MODEL]), sb("x_n", [128, 2, D_MODEL])
        m_hi, m_lo = sb("m_hi", [128, 2, KT, 128], F32R), sb("m_lo", [128, 2, KT, 128], F32R)
        y, xm, xn = sb("y5", [128, D_MODEL]), sb("xm", [128, 2, D_MODEL]), sb("xn5", [128, D_MODEL])
        hg = sb("hg5", [128, 2, HK, 128])
        g_post, g_rows, gT = sb("g_post", [128, D_MODEL]), sb("g_rows5", [KT, 128]), sb("gT5", [128, KT])
        stat, mhalf = sb("stat5", [128, 6]), sb("mhalf5", [128, 1])
        m_ps = [ps(f"m5_ps{i}", [128, HK, 128]) for i in range(2)]
        x_ps = [ps(f"x5_ps{i}", [128, HK, 128]) for i in range(2)]
        y_ps = [ps(f"y5_ps{i}", [128, D_MODEL]) for i in range(2)]
        m_landed, x_landed, xm_stored = ([sem(f"{n}{i}") for i in range(2)] for n in ("m_landed", "x_landed", "xm_stored"))
        g_post_landed = sem("g_post_landed")
        g_landed, w_hi_ready, w_lo_ready, set_up, g_turned, g_ready = map(
            sem, ("g_landed", "w_hi_ready", "w_lo_ready", "set_up", "g_turned", "g_ready"))
        (m_turned, m_hi_ready, m_lo_ready, y_done, y_squared, y_mean, y_rstd, y_ready, xm_ready, xm_squared, xm_mean,
         xm_rstd, xn_ready, x_turned, hg_ready, hi_ready, lo_ready) = map(
            sem, ("m_turned", "m_hi_ready", "m_lo_ready", "y_done", "y_squared", "y_mean", "y_rstd", "y_ready", "xm_ready",
                  "xm_squared", "xm_mean", "xm_rstd", "xn_ready", "x_turned", "hg_ready", "hi_ready", "lo_ready"))
        half = lambda t, q: 2 * t + q + 3
        S = PT

        def over_tiles(eng, step):
            step(0, 0)
            step(1, 1)
            with eng.Fori(1, PT // 2) as i:
                for par in range(2):
                    step(2 * i + par, par, i)
            step(S, 0)

        with nc.Block() as block:

            @block.sync
            def _(sp):
                def load(t, par, x_rows, rows=128):
                    if not isinstance(t, int) or t >= 2:
                        sp.wait_ge(m_turned, by(t - 2))
                    sp.dma_start(m_n[0:rows, par, :], mix[bass.ds(t * 128, rows), :]).then_inc(m_landed[par], 16)
                    if not isinstance(t, int) or t >= 2:
                        sp.wait_ge(xm_ready, by(t - 2))
                    sp.dma_start(x_n[0:rows, par, :], x_rows).then_inc(x_landed[par], 16)

                def store(t, par, rows=128):
                    sp.wait_ge(xm_ready, by(t))
                    sp.dma_start(x_mid[bass.ds(t * 128, rows), :], xm[0:rows, par, :]).then_inc(xm_stored[par], 16)

                x_p = A["x_prompt"][0]
                sp.dma_start(g_rows[:, :], A["g_pre_ffn"][0].rearrange("(k p) -> k p", p=128)).then_inc(g_landed, 16)
                load(0, 0, x_p[0:128, :])
                for k in range(HK, KT):
                    sp.wait_ge(w_lo_ready, k - HK + 1)
                    load_out_piece(sp, A, w_raw, w_landed, k)
                sp.dma_start(g_post[:, :], A["g_post_mix"][0].partition_broadcast(128)).then_inc(g_post_landed, 16)
                load(1, 1, x_p[128:256, :])
                with sp.Fori(0, PT // 2 - 1) as i:
                    for par in range(2):
                        load(2 * i + 2 + par, par, x_p[bass.ds(i * 256 + 256 + 128 * par, 128), :])
                        store(2 * i + par, par)
                load(S, 0, A["x_sample"].rearrange("b t d -> (b t) d"), NS)
                store(PT - 2, 0)
                store(PT - 1, 1)
                store(S, 0, NS)
                sp.wait_ge(xm_stored[0], 80)
                sp.wait_ge(xm_stored[1], 64)

            @block.gpsimd
            def _(pool):
                pool.memset(mhalf[:, :], -0.5).then_inc(set_up, 1)
                for s in (y_rstd, xm_ready, xm_rstd):
                    pool.sem_inc(s, 1)
                pool.sem_inc(lo_ready, 2)
                pool.wait_ge(set_up, 1)

                def residual(t, par, i=0):
                    pool.wait_ge(y_mean, by(t))
                    pool.tensor_tensor(stat[:, 2:3], stat[:, 1:2], mhalf[:, :], ALU.pow).then_inc(y_rstd, 1)
                    pool.wait_ge(y_ready, by(t))
                    pool.wait_ge(x_landed[par], 16 * PT // 2 + 16 if known(t, S) else 16 * i + 16)
                    if known(t, S) or not known(i, 0):
                        pool.wait_ge(xm_stored[par], 16 * PT // 2 if known(t, S) else 16 * i)
                    pool.wait_ge(xn_ready, by(t - 1))
                    pool.tensor_tensor(xm[:, par, :], y[:, :], x_n[:, par, :], ALU.add).then_inc(xm_ready, 1)
                    pool.wait_ge(xm_mean, by(t))
                    pool.tensor_tensor(stat[:, 5:6], stat[:, 4:5], mhalf[:, :], ALU.pow).then_inc(xm_rstd, 1)

                def low(t, n=128):
                    for q in range(2):
                        pool.wait_ge(hi_ready, half(t, q))
                        cut = (slice(None), slice(HK * q, HK * q + HK), bass.ds(t * 128, n))
                        pool.tensor_tensor(h_lo[cut], hg[:, q, :, 0:n], h_hi[cut].bitcast(F32), ALU.subtract).then_inc(lo_ready, 1)

                residual(0, 0)
                residual(1, 1)
                low(0)
                with pool.Fori(1, PT // 2) as i:
                    for par in range(2):
                        residual(2 * i + par, par, i)
                        low(2 * i + par - 1)
                residual(S, 0)
                low(S - 1)
                low(S, NS)

            @block.scalar
            def _(act):
                for s in (m_hi_ready, y_squared, xm_squared):
                    act.sem_inc(s, 1)
                act.sem_inc(hi_ready, 2)

                def mix_high(t, par):
                    act.wait_ge(m_turned, by(t))
                    if not isinstance(t, int) or t >= 2:
                        act.wait_ge(y_done, by(t - 2))
                    for q in range(2):
                        x = act.copy(m_hi[:, par, HK * q:HK * q + HK, :], m_ps[q][:, :, :])
                    x.then_inc(m_hi_ready, 1)

                def square_y(t, par):
                    act.wait_ge(y_done, by(t))
                    act.wait_ge(xm_ready, by(t - 1))
                    act.activation(y[:, :], y_ps[par][:, :], ACT.Square, accum_out=stat[:, 0:1]).then_inc(y_squared, 1)

                def square_x(t, par):
                    act.wait_ge(xm_ready, by(t))
                    act.wait_ge(x_turned, half(t - 1, 1))
                    act.activation(xn[:, :], xm[:, par, :], ACT.Square, accum_out=stat[:, 3:4]).then_inc(xm_squared, 1)

                def high(t, n=128):
                    for q in range(2):
                        act.wait_ge(hg_ready, half(t, q))
                        act.copy(h_hi[:, HK * q:HK * q + HK, bass.ds(t * 128, n)], hg[:, q, :, 0:n]).then_inc(hi_ready, 1)

                def step(t, par, i=0):
                    if not known(t, S):
                        mix_high(t + 1, 1 - par)
                    square_y(t, par)
                    if not known(t, 0):
                        high(t - 1)
                    square_x(t, par)

                for k in range(KT):
                    if k == 2:
                        mix_high(0, 0)
                    act.wait_ge(w_landed[k % HK], 16 * (k // HK) + 16)
                    act.copy(w_hi[:, k, :], w_raw[:, k % HK, :]).then_inc(w_hi_ready, 1)
                over_tiles(act, step)
                high(S, NS)

            @block.vector
            def _(dve):
                for s in (m_lo_ready, y_mean, y_ready, xm_mean, xn_ready):
                    dve.sem_inc(s, 1)
                dve.sem_inc(hg_ready, 2)

                def mix_low(t, par):
                    dve.wait_ge(m_hi_ready, by(t))
                    for q in range(2):
                        cut = (slice(None), par, slice(HK * q, HK * q + HK))
                        x = dve.tensor_tensor(m_lo[cut], m_ps[q][:, :, :], m_hi[cut].bitcast(F32), ALU.subtract)
                    x.then_inc(m_lo_ready, 1)

                def scale_y(t, par):
                    dve.wait_ge(y_squared, by(t))
                    dve.tensor_scalar(stat[:, 1:2], stat[:, 0:1], 1.0 / D_MODEL, EPS, ALU.mult, ALU.add).then_inc(y_mean, 1)
                    dve.wait_ge(y_rstd, by(t))
                    dve.scalar_tensor_tensor(y[:, :], y_ps[par][:, :], stat[:, 2:3], g_post[:, :], ALU.mult, ALU.mult).then_inc(y_ready, 1)

                def scale_x(t, par):
                    dve.wait_ge(xm_squared, by(t))
                    dve.tensor_scalar(stat[:, 4:5], stat[:, 3:4], 1.0 / D_MODEL, EPS, ALU.mult, ALU.add).then_inc(xm_mean, 1)
                    dve.wait_ge(xm_rstd, by(t))
                    dve.tensor_scalar(xn[:, :], xm[:, par, :], stat[:, 5:6], None, ALU.mult).then_inc(xn_ready, 1)

                def gain(t):
                    for q in range(2):
                        dve.wait_ge(x_turned, half(t, q))
                        dve.wait_ge(lo_ready, half(t - 1, q))
                        dve.tensor_tensor(hg[:, q], x_ps[q][:, :, :], spread(gT[:, HK * q:HK * q + HK], [128, HK, 128]),
                                          ALU.mult).then_inc(hg_ready, 1)

                def step(t, par, i=0):
                    if not known(t, S):
                        mix_low(t + 1, 1 - par)
                    scale_y(t, par)
                    if not known(t, 0):
                        gain(t - 1)
                    scale_x(t, par)

                for k in range(KT):
                    if k == 2:
                        dve.wait_ge(g_turned, 1)
                        dve.tensor_copy(gT[:, :], x_ps[0][:, 0, 0:KT]).then_inc(g_ready, 1)
                        mix_low(0, 0)
                    dve.wait_ge(w_hi_ready, k + 1)
                    dve.tensor_tensor(w_lo[:, k, :], w_raw[:, k % HK, :], w_hi[:, k, :].bitcast(F32), ALU.subtract).then_inc(w_lo_ready, 1)
                dve.wait_ge(g_ready, 1)
                dve.wait_ge(g_post_landed, 16)
                over_tiles(dve, step)
                gain(S)

            @block.tensor
            def _(pe):
                for s in (m_turned, y_done):
                    pe.sem_inc(s, 1)
                pe.sem_inc(x_turned, 2)

                def turn_mix(t, par, lap):
                    pe.wait_ge(m_landed[par], lap)
                    pe.wait_ge(m_lo_ready, by(t - 1))
                    for k in range(KT):
                        mm = pe.transpose(m_ps[k // HK][:, k % HK, :], m_n[:, par, 128 * k:128 * k + 128], ident[:, :])
                    mm.then_inc(m_turned, 1)

                def project(t, par):
                    pe.wait_ge(m_lo_ready, by(t))
                    pe.wait_ge(y_ready, by(t - 2)) if (not isinstance(t, int) or t >= 2) else None
                    for c in range(0, D_MODEL, 512):
                        for k in range(KT):
                            if known(t, 0) and c == 0:
                                pe.wait_ge(w_lo_ready, k + 1)
                            for n, (x, w) in enumerate(((m_hi, w_hi), (m_hi, w_lo), (m_lo, w_hi))):
                                mm = pe.matmul(y_ps[par][:, c:c + 512], x[:, par, k, :], w[:, k, c:c + 512],
                                               start=(k, n) == (0, 0), stop=(k, n) == (KT - 1, 2))
                    mm.then_inc(y_done, 1)

                def turn_x(t):
                    pe.wait_ge(xn_ready, by(t))
                    for q in range(2):
                        pe.wait_ge(hg_ready, half(t - 1, q))
                        for k in range(HK):
                            c = (HK * q + k) * 128
                            mm = pe.transpose(x_ps[q][:, k, :], xn[:, c:c + 128], ident[:, :])
                        mm.then_inc(x_turned, 1)

                def step(t, par, i=0):
                    if not known(t, S):
                        lap = 16 if known(t, 0) else 32 if known(t, 1) else 16 * i + 16 + 16 * par
                        turn_mix(t + 1, 1 - par, lap)
                    project(t, par)
                    if not known(t, 0):
                        turn_x(t - 1)

                pe.wait_ge(g_landed, 16)
                pe.transpose(x_ps[0][:, 0, 0:KT], g_rows[:, :], ident[0:KT, 0:KT]).then_inc(g_turned, 1)
                pe.wait_ge(g_ready, 1)
                turn_mix(0, 0, 16)
                over_tiles(pe, step)
                turn_x(S)


def ffn(nc, A, z, x_mid, h_hi, h_lo, kept):
    HK, SUB, GROUP_D = KT // 2, 2, 2 * TT
    GROUPS = D_FF // (128 * SUB)
    CHUNKS = ((0, 364), (364, 362), (726, 362))
    UNITS = SUB * len(CHUNKS)
    DOWN_AFTER = (0, 3, 4, 4, 4, 3)
    SHARE = (L - DEC_T - EARLY_ROWS) // ((GROUPS - 1) * UNITS)
    gu_v = A["w_gu"][0].rearrange("(q k p) n -> q p k n", q=2, p=128)
    rows = lambda t: slice(128 - tile_rows(t), 128)
    whole = lambda t: 4 + GROUP_D * (GROUPS - 1) + 2 * t + 2
    with ExitStack() as ctx:
        sb = lambda n, s, d=F32: ctx.enter_context(nc.sbuf_tensor(n, s, d))
        ps = lambda n, s: ctx.enter_context(nc.psum_tensor(n, s, F32))
        sem = lambda n: nc.alloc_semaphore("p6_" + n)
        raw = sb("raw6", [128, 2, D_MODEL])
        gu_hi, gu_lo = (sb(n, [128, SUB, KT, 2, 128], F32R) for n in ("gu_hi", "gu_lo"))
        wd_hi, wd_lo = (sb(n, [128, SUB, D_MODEL], F32R) for n in ("wd_hi", "wd_lo"))
        acc = sb("acc", [128, TT, D_MODEL])
        x_own, g_post = sb("x_own", [128, D_MODEL]), sb("g_post6", [128, D_MODEL])
        squares, x_m = raw[:, 0, :], (x_own[:, :], raw[:, 1, :])
        stat, mhalf = sb("stat6", [128, 3, TT]), sb("mhalf6", [128, 1])
        s_t, f_t = sb("s_t", [128, 364]), sb("f_t", [128, 364])
        f_hi, f_lo = (sb(n, [128, 2, SUB, NTOK], F32R) for n in ("f_hi", "f_lo"))
        gate_ps = [ps(f"gate_ps{i}", [128, 512]) for i in range(2)]
        up_ps = [ps(f"up_ps{i}", [128, 512]) for i in range(2)]
        d_ps = [ps(f"d_ps{i}", [128, 512]) for i in range(4)]
        landed = [sem(f"landed{i}") for i in range(2)]
        x_landed, y_stored = [sem(f"x_landed{i}") for i in range(2)], sem("y_stored")
        g_landed, half_set, squared, mean_ready, rstd_ready, scaled, y_ready = map(
            sem, ("g_landed", "half_set", "squared", "mean_ready", "rstd_ready", "scaled", "y_ready"))
        (hi_ready, lo_ready, unit_done, silu_ready, f_ready, f_hi_ready, f_lo_ready, down_done, added,
         zeroed) = map(sem, ("hi_ready", "lo_ready", "unit_done", "silu_ready", "f_ready", "f_hi_ready", "f_lo_ready",
                           "down_done", "added", "zeroed"))
        piece = lambda g, e, p: 6 * g + 2 * e + p
        raw_gu = lambda p: raw[:, p, :].rearrange("q (k h n) -> q k h n", k=HK, h=2)

        def over_steps(eng, step):
            step(0, 0)
            with eng.Fori(0, (GROUPS - 3) // 2) as i:
                step(2 * i + 1, 1)
                step(2 * i + 2, 0)
            step(GROUPS - 2, 1)
            step(GROUPS - 1, 0)
            step(GROUPS, 1)

        with nc.Block() as block:

            @block.sync
            def _(sp):
                def load_gu(g, e, tile):
                    for p in range(2):
                        if not known(g, 0) or e > 0:
                            sp.wait_ge(lo_ready, piece(g, e, p) - 1)
                        for h in range(2):
                            sp.dma_start(raw_gu(p)[:, :, h, :],
                                         gu_v[p][:, :, bass.ds(tile * 128 + h * D_FF, 128)]).then_inc(landed[p], 16)

                def load_down(g, e, group):
                    for p in range(2):
                        sp.wait_ge(lo_ready, piece(g, e, p) - 1)
                        sp.dma_start(raw[:, p, :], A["w_down"][0, bass.ds((group * 2 + p) * 128, 128), :]).then_inc(landed[p], 16)

                def step(g, par):
                    if known(g, GROUPS):
                        load_down(GROUPS - 1, 2, GROUPS - 1)
                        return
                    if not known(g, 0):
                        load_down(g, 0, g - 1)
                    load_gu(g, 1, 2 * g + 1)
                    if not known(g, GROUPS - 1):
                        load_gu(g, 2, 2 * g + 2)

                def load_x(t):
                    sp.dma_start(x_m[t % 2][rows(t), :],
                                 x_mid[t * 128:t * 128 + tile_rows(t), :]).then_inc(x_landed[t % 2], 16)

                load_gu(0, 0, 0)
                sp.dma_start(g_post[:, :], A["g_post_ffn"][0].partition_broadcast(128)).then_inc(g_landed, 16)
                load_x(0)
                over_steps(sp, step)
                sp.wait_ge(lo_ready, piece(GROUPS - 1, 2, 2))
                load_x(1)
                for t in range(TT):
                    sp.wait_ge(y_ready, t + 1)
                    if t + 2 < TT:
                        load_x(t + 2)
                    out = (A["y_prompt"][0, t * 128:t * 128 + 128, :] if t < PT
                           else A["y_sample"].rearrange("b t d -> (b t) d"))
                    sp.dma_start(out, acc[rows(t), t, :]).then_inc(y_stored, 16)
                sp.wait_ge(y_stored, 16 * TT)

            @block.gpsimd
            def _(pool):
                def step(g, par):
                    if known(g, GROUPS):
                        return
                    for u in range(UNITS):
                        if not known(g, 0):
                            copy_windows(pool, A, kept, EARLY_ROWS + ((g - 1) * UNITS + u) * SHARE, SHARE)
                        c, n = CHUNKS[u % 3]
                        cut = (slice(None), par, u // 3, slice(c, c + n))
                        pool.wait_ge(f_hi_ready, UNITS * g + u + 1)
                        pool.tensor_tensor(f_lo[cut], f_t[:, 0:n], f_hi[cut].bitcast(F32), ALU.subtract).then_inc(f_lo_ready, 1)

                pool.memset(acc[:, :, :], 0.0).then_inc(zeroed, 1)
                pool.memset(mhalf[:, :], -0.5).then_inc(half_set, 1)
                for n, (p_out, s_out) in enumerate((("k_prompt", "ks_sample"), ("v_prompt", "vs_sample"))):
                    cols = slice((5 + n) * WID, (6 + n) * WID)
                    pool.dma_start(A[p_out][0, 0].rearrange("s h d -> s (h d)"), z[0:SEQ, cols]).then_inc(kept, 16)
                    pool.dma_start(A[s_out][0, :, L - DEC_T:L].rearrange("b t h d -> b t (h d)"),
                                   z[SEQ:NTOK, cols].rearrange("(b t) c -> b t c", b=DEC_B)).then_inc(kept, 16)
                over_steps(pool, step)
                pool.wait_ge(half_set, 1)

                def root(t):
                    pool.wait_ge(mean_ready, t + 1)
                    if t == PT:
                        pool.wait_ge(y_ready, t - 1)
                    pool.tensor_tensor(stat[rows(t), 2, t:t + 1], stat[rows(t), 1, t:t + 1], mhalf[rows(t), :],
                                       ALU.pow).then_inc(rstd_ready, 1)

                root(0)
                for t in range(TT):
                    if t + 1 < TT:
                        root(t + 1)
                    pool.wait_ge(rstd_ready, min(t + 2, TT))
                    if t == PT:
                        pool.wait_ge(y_ready, t)
                    pool.wait_ge(scaled, t + 1)
                    pool.wait_ge(x_landed[t % 2], 16 * (t // 2) + 16)
                    pool.tensor_tensor(acc[rows(t), t, :], acc[rows(t), t, :], x_m[t % 2][rows(t), :],
                                       ALU.add).then_inc(y_ready, 1)
                pool.wait_ge(kept, 16 * (4 + 2 * EARLY_COPIES + 2 * (GROUPS - 1) * UNITS))

            @block.scalar
            def _(act):
                def split(dst, src, out, lap):
                    for p in dst:
                        act.wait_ge(landed[p], lap)
                        act.copy(out(p), src(p)).then_inc(hi_ready, 1)

                gu = lambda s: lambda p: gu_hi[:, s, HK * p:HK * p + HK]
                raw_wd = lambda p: raw[:, p, :]
                wd = lambda p: wd_hi[:, p, :]

                def unit(g, par, u):
                    c, n = CHUNKS[u % 3]
                    act.wait_ge(unit_done, UNITS * g + u + 1)
                    if not (known(g, 0) and u == 0):
                        act.wait_ge(f_ready, UNITS * g + u)
                    act.activation(s_t[:, 0:n], gate_ps[u % 2][:, 0:n], ACT.Silu).then_inc(silu_ready, 1)
                    act.wait_ge(f_ready, UNITS * g + u + 1)
                    act.copy(f_hi[:, par, u // 3, c:c + n], f_t[:, 0:n]).then_inc(f_hi_ready, 1)

                def step(g, par):
                    if known(g, GROUPS):
                        act.wait_ge(down_done, GROUP_D * g)
                        split((0, 1), raw_wd, wd, 80 * g)
                        for t in range(TT):
                            act.wait_ge(added, whole(t))
                            if t:
                                act.wait_ge(squared, t)
                            else:
                                act.wait_ge(lo_ready, piece(GROUPS - 1, 2, 2))
                            act.activation(squares[rows(t), :], acc[rows(t), t, :], ACT.Square,
                                           accum_out=stat[rows(t), 0, t:t + 1]).then_inc(squared, 1)
                        return
                    if not known(g, 0):
                        act.wait_ge(down_done, GROUP_D * g)
                        split((0, 1), raw_wd, wd, 80 * g + 32)
                    unit(g, par, 0)
                    if not known(g, 0):
                        act.wait_ge(unit_done, UNITS * g)
                    split((0, 1), raw_gu, gu(1), 80 * g + 64)
                    unit(g, par, 1)
                    unit(g, par, 2)
                    for u in (3, 4):
                        if not known(g, GROUPS - 1):
                            act.wait_ge(unit_done, UNITS * g + 3)
                            split((u - 3,), raw_gu, gu(0), 80 * g + 96)
                        unit(g, par, u)
                    unit(g, par, 5)

                split((0, 1), raw_gu, gu(0), 32)
                over_steps(act, step)

            @block.vector
            def _(dve):
                dve.sem_inc(added, 4)

                def split(n, dst, src, hi, lo):
                    for p in dst:
                        dve.wait_ge(hi_ready, n + p + 1)
                        dve.tensor_tensor(lo(p), src(p), hi(p).bitcast(F32), ALU.subtract).then_inc(lo_ready, 1)

                raw_wd = lambda p: raw[:, p, :]
                wd = lambda t: lambda p: t[:, p, :]
                gu = lambda t, s: lambda p: t[:, s, HK * p:HK * p + HK]

                def unit(g, u):
                    c, n = CHUNKS[u % 3]
                    dve.wait_ge(silu_ready, UNITS * g + u + 1)
                    if not (known(g, 0) and u == 0):
                        dve.wait_ge(f_lo_ready, UNITS * g + u)
                    dve.tensor_tensor(f_t[:, 0:n], s_t[:, 0:n], up_ps[u % 2][:, 0:n], ALU.mult).then_inc(f_ready, 1)

                def add(g, par, first, count):
                    for j in range(first, first + count):
                        lo = 64 if j // 2 == PT else 0
                        cut = (slice(lo, 128), j // 2, slice(j % 2 * 512, j % 2 * 512 + 512))
                        dve.wait_ge(down_done, GROUP_D * g + j + 1)
                        dve.tensor_tensor(acc[cut], acc[cut], d_ps[(2 * (1 - par) + j) % 4][lo:128, :], ALU.add).then_inc(added, 1)

                def mean(t):
                    dve.wait_ge(squared, t + 1)
                    dve.tensor_scalar(stat[rows(t), 1, t:t + 1], stat[rows(t), 0, t:t + 1], 1.0 / D_MODEL, EPS,
                                      ALU.mult, ALU.add).then_inc(mean_ready, 1)

                def scale(t):
                    dve.wait_ge(rstd_ready, t + 1)
                    dve.scalar_tensor_tensor(acc[rows(t), t, :], acc[rows(t), t, :], stat[rows(t), 2, t:t + 1],
                                             g_post[rows(t), :], ALU.mult, ALU.mult).then_inc(scaled, 1)

                def step(g, par):
                    if known(g, GROUPS):
                        split(piece(GROUPS - 1, 2, 0), (0, 1), raw_wd, wd(wd_hi), wd(wd_lo))
                        dve.wait_ge(g_landed, 16)
                        for t in range(TT + 2):
                            if t < TT:
                                add(g, par, 2 * t, 2)
                            if 1 <= t <= TT:
                                mean(t - 1)
                            if t >= 2:
                                scale(t - 2)
                        return
                    if not known(g, 0):
                        split(piece(g, 0, 0), (0, 1), raw_wd, wd(wd_hi), wd(wd_lo))
                    unit(g, 0)
                    split(piece(g, 1, 0), (0, 1), raw_gu, gu(gu_hi, 1), gu(gu_lo, 1))
                    first = 0
                    for u in range(1, UNITS):
                        if u in (3, 4) and not known(g, GROUPS - 1):
                            split(piece(g, 2, 0), (u - 3,), raw_gu, gu(gu_hi, 0), gu(gu_lo, 0))
                        unit(g, u)
                        if not known(g, 0):
                            add(g, par, first, DOWN_AFTER[u])
                            first += DOWN_AFTER[u]

                split(0, (0, 1), raw_gu, gu(gu_hi, 0), gu(gu_lo, 0))
                dve.wait_ge(zeroed, 1)
                over_steps(dve, step)

            @block.tensor
            def _(pe):
                pe.sem_inc(down_done, GROUP_D)

                def unit(g, u):
                    s, (c, n) = u // 3, CHUNKS[u % 3]
                    if not known(g, 0) or u >= 2:
                        pe.wait_ge(f_ready, UNITS * g + u - 1)
                    for h, bank in enumerate((gate_ps, up_ps)):
                        for k in range(KT):
                            for m, (w, x) in enumerate(((gu_hi, h_hi), (gu_hi, h_lo), (gu_lo, h_hi))):
                                mm = pe.matmul(bank[u % 2][:, 0:n], w[:, s, k, h, :], x[:, k, c:c + n],
                                               start=(k, m) == (0, 0), stop=(k, m) == (KT - 1, 2))
                    mm.then_inc(unit_done, 1)

                def down(g, par, first, count):
                    for j in range(first, first + count):
                        end, col = min(j // 2 * 128 + 128, NTOK), j % 2 * 512
                        pe.wait_ge(added, GROUP_D * (g - 1) + j + 1)
                        for s in range(SUB):
                            for m, (x, w) in enumerate(((f_hi, wd_hi), (f_hi, wd_lo), (f_lo, wd_hi))):
                                mm = pe.matmul(d_ps[(2 * (1 - par) + j) % 4][:, :], x[:, 1 - par, s, end - 128:end],
                                               w[:, s, col:col + 512], start=(s, m) == (0, 0), stop=(s, m) == (SUB - 1, 2))
                        mm.then_inc(down_done, 1)

                def step(g, par):
                    if known(g, GROUPS):
                        pe.wait_ge(lo_ready, piece(GROUPS - 1, 2, 2))
                        pe.wait_ge(f_lo_ready, UNITS * g)
                        down(g, par, 0, GROUP_D)
                        return
                    first = 0
                    for u in range(UNITS):
                        if u == 0:
                            pe.wait_ge(lo_ready, 2 if known(g, 0) else piece(g, 0, 0))
                        if u == 3:
                            pe.wait_ge(lo_ready, piece(g, 2, 0))
                        unit(g, u)
                        if not known(g, 0) and DOWN_AFTER[u]:
                            if first == 0:
                                pe.wait_ge(lo_ready, piece(g, 1, 0))
                                pe.wait_ge(f_lo_ready, UNITS * g)
                            down(g, par, first, DOWN_AFTER[u])
                            first += DOWN_AFTER[u]

                over_steps(pe, step)



OUTPUTS = {
    "y_prompt": (1, SEQ, D_MODEL), "y_sample": (DEC_B, DEC_T, D_MODEL),
    "state_p": (1, 1, NH, HD, HD), "k_prompt": (1, 1, SEQ, NH, HD), "v_prompt": (1, 1, SEQ, NH, HD),
    "state_s": (1, DEC_B, NH, HD, HD), "ks_sample": (1, DEC_B, L, NH, HD), "vs_sample": (1, DEC_B, L, NH, HD),
}


def hymba_layer(nc, A):
    scratch = lambda n, s: nc.dram_tensor(n, s, F32, kind="Internal").ap()
    z, mix = scratch("z_scratch", [NTOK, ZC]), scratch("mix_scratch", [NTOK, D_MODEL])
    x_mid, tab = scratch("x_mid_scratch", [NTOK, D_MODEL]), scratch("tab_scratch", [NH, 128, TABW])
    kept = nc.alloc_semaphore("kept")
    with nc.sbuf_tensor("ident", [128, 128], F32) as ident:
        with nc.cleanup_on_exit():
            with nc.sbuf_tensor("h_hi", [128, KT, NTOK], F32R) as h_hi, \
                 nc.sbuf_tensor("h_lo", [128, KT, NTOK], F32R) as h_lo:
                in_projection(nc, A, z, h_hi, h_lo, ident, kept)
        sems = lambda name, n: [nc.alloc_semaphore(f"{name}{i}") for i in range(n)]
        qk_landed, padded = nc.alloc_semaphore("qk_landed"), nc.alloc_semaphore("padded")
        K_landed, V_landed, w_landed = sems("K_landed", 2), sems("V_landed", 3), sems("w_landed", KT // 2)
        with_2_3, with_2_4, with_3_4, with_4_5 = ExitStack(), ExitStack(), ExitStack(), ExitStack()
        hold = lambda life, side, name, shape, dtype=F32: life.enter_context(nc.sbuf_tensor(name, shape, dtype, side=side))

        bias_s = hold(with_2_4, "right", "bias_s", [128, STILES * 128])
        bias_p = hold(with_2_3, "left", "bias_p", [128, NH, SEQ])
        q_n, k_n = (hold(with_2_3, "left", n, [128, PT, 128]) for n in ("q_n", "k_n"))
        retention(nc, A, z, mix, ident, A["state_p"][0, 0], A["state_s"][0], tab, bias_p, bias_s,
                  lambda sp: load_pair(sp, z, q_n, k_n, qk_landed, 0))

        K, V = hold(with_3_4, "right", "K", [128, 2, STILES, WID]), hold(with_3_4, "right", "V", [128, STILES, WID])

        def clear_padding(pool):
            for pad in (K[:, 0, STILES - 1, :], K[:, 1, STILES - 1, :], V[:, STILES - 1, :]):
                pool.memset(pad, 0.0).then_inc(padded, 1)

        def load_first_window(sp):
            sp.wait_ge(padded, 3)
            load_keys(sp, A, z, K, K_landed, 0, 0)
            for g in range(3):
                load_values(sp, A, z, V, V_landed, 0, g)

        prompt_attention(nc, A, z, mix, bias_p, ident, q_n, k_n, qk_landed, clear_padding, load_first_window)
        with_2_3.close()

        w_raw = hold(with_4_5, "left", "wo_raw", [128, KT // 2, D_MODEL])
        load_w_out = lambda sp: [load_out_piece(sp, A, w_raw, w_landed, k) for k in range(KT // 2)]
        sample_attention(nc, A, z, mix, bias_s, ident, K, V, K_landed, V_landed, load_w_out)
        with_3_4.close()
        with_2_4.close()

        with nc.sbuf_tensor("h2_hi", [128, KT, NTOK], F32R, side="right") as h_hi, \
             nc.sbuf_tensor("h2_lo", [128, KT, NTOK], F32R, side="right") as h_lo:
            out_projection(nc, A, mix, x_mid, h_hi, h_lo, ident, w_raw, w_landed)
            with_4_5.close()
            ffn(nc, A, z, x_mid, h_hi, h_lo, kept)


def kernel(**inputs):
    import concourse.bacc as bacc
    from concourse.bass_utils import run_bass_kernel_spmd

    nc = bacc.Bacc("TRN2", target_bir_lowering=False, num_devices=1)
    arrays = {n: np.ascontiguousarray(a) for n, a in inputs.items()}
    arrays.update(shape_constants())
    A = {n: nc.dram_tensor(n, a.shape, mybir.dt.from_np(a.dtype), kind="ExternalInput").ap() for n, a in arrays.items()}
    for n, shape in OUTPUTS.items():
        A[n] = nc.dram_tensor(n, shape, F32, kind="ExternalOutput").ap()
    hymba_layer(nc, A)
    got = run_bass_kernel_spmd(nc, [arrays], core_ids=[0])
    return tuple(got.results[0][n] for n in OUTPUTS)
```
